# Optimizing a Trainium2 kernel written in Bass

```python
import jax, jax.numpy as jnp
from jax import lax
import numpy as np

D_MODEL = 1024
BATCH = 1
SEQ = 512
DEPTH = 2

HEAD_DIM = 64
NSA_HEADS = 8
NSA_KV_GROUPS = 2
NSA_HPG = NSA_HEADS // NSA_KV_GROUPS
NSA_WIDTH = NSA_HEADS * HEAD_DIM
KV_WIDTH = NSA_KV_GROUPS * HEAD_DIM
CMP_BLOCK = 32
CMP_STRIDE = 16
CMP_HIDDEN = 128
SEL_BLOCK = 64
SEL_TOPK = 16
WINDOW = 512
Q_BLOCK = 128
GM_GROUPS = 8
GM_CHUNK = 128
GM_WIDTH = GM_GROUPS * HEAD_DIM
N_BRANCH = 2
D_FF = 2816
ROPE_THETA = 10000.0
EPS = 1e-6
NEG = -1e30
FORCE = 1e4
IN_SIZES = [NSA_WIDTH, 6 * KV_WIDTH, 3 * NSA_HEADS, 2 * GM_WIDTH, D_MODEL, D_MODEL]
IN_WIDTH = sum(IN_SIZES)
IN_SPLITS = np.cumsum(IN_SIZES)[:-1].tolist()


def _rmsnorm(x, g):
    x32 = x.astype(jnp.float32)
    y = x32 * lax.rsqrt(jnp.mean(x32 * x32, axis=-1, keepdims=True) + EPS)
    return y.astype(x.dtype) * g

def _layernorm(x, g, b):
    x32 = x.astype(jnp.float32)
    mu = jnp.mean(x32, axis=-1, keepdims=True)
    var = jnp.mean(jnp.square(x32 - mu), axis=-1, keepdims=True)
    return ((x32 - mu) * lax.rsqrt(var + EPS)).astype(x.dtype) * g + b

def _rope_tables(pos):
    inv = 1.0 / (ROPE_THETA ** (jnp.arange(0, HEAD_DIM, 2, dtype=jnp.float32) / HEAD_DIM))
    ang = pos.astype(jnp.float32)[:, None] * inv[None, :]
    return jnp.cos(ang), jnp.sin(ang)

def _rope(x, cos, sin):
    x32 = x.astype(jnp.float32)
    x1, x2 = jnp.split(x32, 2, axis=-1)
    c = cos[None, :, None, :]
    s = sin[None, :, None, :]
    return jnp.concatenate([x1 * c - x2 * s, x2 * c + x1 * s], axis=-1).astype(x.dtype)

def _modulate(xn, shift, scale):
    return xn * (1.0 + scale) + shift

def _swiglu(x, w_in, w_out):
    a, b = jnp.split(x @ w_in, 2, axis=-1)
    return (jax.nn.silu(a) * b) @ w_out

def _nsa(q, k_cmp, v_cmp, k_sel, v_sel, k_win, v_win, gates, pe, w1, w2):
    B, S = q.shape[0], q.shape[1]
    G, HG = NSA_KV_GROUPS, NSA_HPG
    scale = HEAD_DIM ** -0.5
    pos = jnp.arange(S, dtype=jnp.int32)
    cos, sin = _rope_tables(pos)
    qr = _rope(q, cos, sin).reshape(B, S, G, HG, HEAD_DIM)

    n_cmp = (S - CMP_BLOCK) // CMP_STRIDE + 1
    starts = jnp.arange(n_cmp, dtype=jnp.int32) * CMP_STRIDE
    win_idx = starts[:, None] + jnp.arange(CMP_BLOCK, dtype=jnp.int32)[None, :]

    def compress(t, j):
        blk = t[:, win_idx] + pe[j][None, None, :, None, :]
        h = jax.nn.silu(jnp.einsum('bnlgd,ldf->bngf', blk, w1[j]))
        return h @ w2[j]

    kc = compress(k_cmp, 0)
    vc = compress(v_cmp, 1)
    cend = starts + CMP_BLOCK - 1
    ccos, csin = _rope_tables(cend)
    kc = _rope(kc, ccos, csin)
    s_c = jnp.einsum('bsghd,bngd->bsghn', qr, kc).astype(jnp.float32) * scale
    m_c = (cend[None, :] <= pos[:, None])[None, :, None, None, :]
    p_c = jax.nn.softmax(jnp.where(m_c, s_c, NEG), axis=-1) * m_c
    o_cmp = jnp.einsum('bsghn,bngd->bsghd', p_c.astype(vc.dtype), vc)

    n_sel = S // SEL_BLOCK
    top = min(SEL_TOPK, n_sel)
    sel_start = jnp.arange(n_sel, dtype=jnp.int32) * SEL_BLOCK
    overlap = jnp.clip(
        jnp.minimum(starts[:, None] + CMP_BLOCK, sel_start[None, :] + SEL_BLOCK)
        - jnp.maximum(starts[:, None], sel_start[None, :]), 0, None
    ).astype(jnp.float32) / CMP_BLOCK
    imp = jnp.einsum('bsgn,nj->bsgj', jnp.sum(p_c, axis=3), overlap)
    cur = pos // SEL_BLOCK
    blk = jnp.arange(n_sel, dtype=jnp.int32)
    forced = (blk[None, :] == 0) | (blk[None, :] == cur[:, None]) | (blk[None, :] == cur[:, None] - 1)
    valid = blk[None, :] <= cur[:, None]
    imp = jnp.where(forced[None, :, None, :], FORCE,
                    jnp.where(valid[None, :, None, :], imp, -FORCE))
    _, sel_idx = lax.top_k(imp, top)
    sel_idx = sel_idx.transpose(0, 2, 1, 3)

    ks = _rope(k_sel, cos, sin).reshape(B, n_sel, SEL_BLOCK, G, HEAD_DIM).transpose(0, 3, 1, 2, 4)
    vs = v_sel.reshape(B, n_sel, SEL_BLOCK, G, HEAD_DIM).transpose(0, 3, 1, 2, 4)
    pad = ((0, 0), (WINDOW, 0), (0, 0), (0, 0))
    kw = jnp.pad(_rope(k_win, cos, sin), pad)
    vw = jnp.pad(v_win, pad)
    bi = jnp.arange(B)[:, None, None, None]
    gi = jnp.arange(G)[None, :, None, None]
    jj = jnp.arange(SEL_BLOCK, dtype=jnp.int32)
    wj = jnp.arange(Q_BLOCK + WINDOW, dtype=jnp.int32)

    def block(qb):
        q0 = qb * Q_BLOCK
        qq = lax.dynamic_slice_in_dim(qr, q0, Q_BLOCK, axis=1)
        tq = q0 + jnp.arange(Q_BLOCK, dtype=jnp.int32)
        idx = lax.dynamic_slice_in_dim(sel_idx, q0, Q_BLOCK, axis=2)
        kg = ks[bi, gi, idx]
        vg = vs[bi, gi, idx]
        s = jnp.einsum('bqghd,bgqnjd->bgqhnj', qq, kg).astype(jnp.float32) * scale
        kpos = idx[..., None] * SEL_BLOCK + jj
        m = (kpos <= tq[None, None, :, None, None])[:, :, :, None]
        s = jnp.where(m, s, NEG).reshape(B, G, Q_BLOCK, HG, top * SEL_BLOCK)
        p = jax.nn.softmax(s, axis=-1).reshape(B, G, Q_BLOCK, HG, top, SEL_BLOCK)
        o_s = jnp.einsum('bgqhnj,bgqnjd->bqghd', p.astype(vg.dtype), vg)
        kk = lax.dynamic_slice_in_dim(kw, q0, Q_BLOCK + WINDOW, axis=1)
        vv = lax.dynamic_slice_in_dim(vw, q0, Q_BLOCK + WINDOW, axis=1)
        kp = q0 - WINDOW + wj
        d = tq[:, None] - kp[None, :]
        mw = ((d >= 0) & (d < WINDOW) & (kp[None, :] >= 0))[None, :, None, None, :]
        sw = jnp.einsum('bqghd,bkgd->bqghk', qq, kk).astype(jnp.float32) * scale
        pw = jax.nn.softmax(jnp.where(mw, sw, NEG), axis=-1)
        o_w = jnp.einsum('bqghk,bkgd->bqghd', pw.astype(vv.dtype), vv)
        return o_s, o_w

    o_sel, o_win = lax.map(block, jnp.arange(S // Q_BLOCK, dtype=jnp.int32))
    o_sel = o_sel.transpose(1, 0, 2, 3, 4, 5).reshape(B, S, G, HG, HEAD_DIM)
    o_win = o_win.transpose(1, 0, 2, 3, 4, 5).reshape(B, S, G, HG, HEAD_DIM)
    g = gates.reshape(B, S, G, HG, 3)
    o = g[..., 0:1] * o_cmp + g[..., 1:2] * o_sel + g[..., 2:3] * o_win
    return o.reshape(B, S, NSA_WIDTH)

def _gmlp(uv, ln_g, ln_b, ws, bs):
    B, S = uv.shape[0], uv.shape[1]
    u, v = jnp.split(jax.nn.gelu(uv), 2, axis=-1)
    v = _layernorm(v, ln_g, ln_b)
    v = v.reshape(B, S // GM_CHUNK, GM_CHUNK, GM_GROUPS, HEAD_DIM)
    w = ws * jnp.tril(jnp.ones((GM_CHUNK, GM_CHUNK), ws.dtype))
    sv = jnp.einsum('gts,bnsgc->bntgc', w, v) + bs.T[None, None, :, :, None]
    return u * sv.reshape(B, S, GM_WIDTH)

def first_inputs(seed: int = 0) -> dict:
    key = jax.random.key(seed)
    k = jax.random.split(key, 24)
    L, D = DEPTH, D_MODEL

    def nrm(kk, shape, scale):
        return jax.random.normal(kk, shape, jnp.float32) * scale

    return {
        "x": nrm(k[0], (BATCH, SEQ, D), 1.0),
        "c": nrm(k[1], (BATCH, D), 1.0),
        "ada_w": nrm(k[2], (L, D, 9 * D), 0.5 * D ** -0.5),
        "ada_b": nrm(k[3], (L, 9 * D), 0.1),
        "norm_g": 1.0 + nrm(k[4], (L, 3, D), 0.1),
        "ffn_w_in": nrm(k[5], (L, 2, D, 2 * D_FF), D ** -0.5),
        "ffn_w_out": nrm(k[6], (L, 2, D_FF, D), D_FF ** -0.5),
        "mix_w_in": nrm(k[7], (L, D, IN_WIDTH), D ** -0.5),
        "cmp_pe": nrm(k[8], (L, 2, CMP_BLOCK, HEAD_DIM), 0.1),
        "cmp_w1": nrm(k[9], (L, 2, CMP_BLOCK, HEAD_DIM, CMP_HIDDEN), (CMP_BLOCK * HEAD_DIM) ** -0.5),
        "cmp_w2": nrm(k[10], (L, 2, CMP_HIDDEN, HEAD_DIM), CMP_HIDDEN ** -0.5),
        "gm_ln_g": 1.0 + nrm(k[11], (L, GM_WIDTH), 0.1),
        "gm_ln_b": nrm(k[12], (L, GM_WIDTH), 0.1),
        "gm_ws": nrm(k[13], (L, GM_GROUPS, GM_CHUNK, GM_CHUNK), GM_CHUNK ** -0.5),
        "gm_bs": 1.0 + nrm(k[14], (L, GM_GROUPS, GM_CHUNK), 0.1),
        "proj_a": nrm(k[15], (L, NSA_WIDTH, D), NSA_WIDTH ** -0.5),
        "proj_b": nrm(k[16], (L, GM_WIDTH, D), GM_WIDTH ** -0.5),
        "w_out": nrm(k[17], (L, D, D), D ** -0.5),
        "final_g": 1.0 + nrm(k[18], (D,), 0.1),
    }

def first_block(x, c, ada_w, ada_b, norm_g, ffn_w_in, ffn_w_out, mix_w_in, cmp_pe, cmp_w1,
              cmp_w2, gm_ln_g, gm_ln_b, gm_ws, gm_bs, proj_a, proj_b, w_out, final_g):
    B, S, D = x.shape
    h = x
    for l in range(DEPTH):
        mod = (jax.nn.silu(c) @ ada_w[l] + ada_b[l]).reshape(B, 3, 3, 1, D)

        n = _modulate(_rmsnorm(h, norm_g[l, 0]), mod[:, 0, 0], mod[:, 0, 1])
        h = h + 0.5 * mod[:, 0, 2] * _swiglu(n, ffn_w_in[l, 0], ffn_w_out[l, 0])

        n = _modulate(_rmsnorm(h, norm_g[l, 1]), mod[:, 1, 0], mod[:, 1, 1])
        z = n @ mix_w_in[l]
        zq, zkv, zg, zuv, zga, zgb = jnp.split(z, IN_SPLITS, axis=-1)
        q = zq.reshape(B, S, NSA_HEADS, HEAD_DIM)
        kv = zkv.reshape(B, S, 6, NSA_KV_GROUPS, HEAD_DIM)
        nsa_gates = jax.nn.sigmoid(zg).reshape(B, S, NSA_HEADS, 3)
        y_a = _nsa(q, kv[:, :, 0], kv[:, :, 1], kv[:, :, 2], kv[:, :, 3], kv[:, :, 4], kv[:, :, 5],
                   nsa_gates, cmp_pe[l], cmp_w1[l], cmp_w2[l])
        y_b = _gmlp(zuv, gm_ln_g[l], gm_ln_b[l], gm_ws[l], gm_bs[l])
        merged = jax.nn.sigmoid(zga) * (y_a @ proj_a[l]) + jax.nn.sigmoid(zgb) * (y_b @ proj_b[l])
        h = h + mod[:, 1, 2] * (merged @ w_out[l])

        n = _modulate(_rmsnorm(h, norm_g[l, 2]), mod[:, 2, 0], mod[:, 2, 1])
        h = h + 0.5 * mod[:, 2, 2] * _swiglu(n, ffn_w_in[l, 1], ffn_w_out[l, 1])
    return _rmsnorm(h, final_g)


GRID_W = 64
CTX_LEN = 256
N_MIXERS = 2
N_POOL_GROUPS = 4
POOL_WINDOWS = (2, 4, 8, 16)
POOL_GROUP_DIM = D_MODEL // N_POOL_GROUPS
HEAD_DIM_2 = 128
N_Q_HEADS = D_MODEL // HEAD_DIM_2
N_KV_HEADS = 2
Q_PER_KV = N_Q_HEADS // N_KV_HEADS
QKV_DIM = (N_Q_HEADS + 2 * N_KV_HEADS) * HEAD_DIM_2
D_FF_2 = 4 * D_MODEL
N_MOD = 6
N_POOL_LAYERS = (DEPTH + 1) // 2
N_ATTN_LAYERS = DEPTH // 2


def rms_norm(x, g):
    xf = x.astype(jnp.float32)
    y = xf * lax.rsqrt(jnp.mean(xf * xf, axis=-1, keepdims=True) + EPS)
    return (y * g.astype(jnp.float32)).astype(x.dtype)

def ada_mods(cond, w, b):
    m = (jax.nn.silu(cond) @ w + b)[..., None, :]
    return jnp.split(m, N_MOD, axis=-1)

def modulate(h, shift, scale):
    return h * (1.0 + scale) + shift

def pool_mixer(h, w_pool, pool_scale):
    B, L, D = h.shape
    t = jnp.arange(L)
    hf = h.astype(jnp.float32)
    cs = jnp.concatenate([jnp.zeros((B, 1, D), jnp.float32), jnp.cumsum(hf, axis=1)], axis=1)
    outs = []
    for g, w in enumerate(POOL_WINDOWS):
        sl = slice(g * POOL_GROUP_DIM, (g + 1) * POOL_GROUP_DIM)
        lo = jnp.clip(t - w // 2, 0, L)
        hi = jnp.clip(t + w - w // 2, 0, L)
        csg = cs[..., sl]
        cnt = (hi - lo).astype(jnp.float32)[:, None]
        mean = (jnp.take(csg, hi, axis=1) - jnp.take(csg, lo, axis=1)) / cnt
        diff = (mean - hf[..., sl]).astype(h.dtype)
        outs.append(diff @ w_pool[g])
    return jnp.concatenate(outs, axis=-1) * pool_scale

def axial_rope_tables(L):
    rows = L // GRID_W
    row = jnp.broadcast_to(jnp.arange(rows)[:, None], (rows, GRID_W)).reshape(L).astype(jnp.float32)
    col = jnp.broadcast_to(jnp.arange(GRID_W)[None, :], (rows, GRID_W)).reshape(L).astype(jnp.float32)
    half = HEAD_DIM_2 // 2
    inv_freq = jnp.power(jnp.float32(ROPE_THETA), -jnp.arange(0, half, 2, dtype=jnp.float32) / half)
    ang_r = row[:, None] * inv_freq
    ang_c = col[:, None] * inv_freq
    return (jnp.cos(ang_r)[:, None, :], jnp.sin(ang_r)[:, None, :],
            jnp.cos(ang_c)[:, None, :], jnp.sin(ang_c)[:, None, :])

def _rotate(x, cos, sin):
    x1, x2 = jnp.split(x, 2, axis=-1)
    return jnp.concatenate([x1 * cos - x2 * sin, x2 * cos + x1 * sin], axis=-1)

def apply_axial_rope(x, tables):
    cr, sr, cc, sc = tables
    xf = x.astype(jnp.float32)
    half = HEAD_DIM_2 // 2
    out = jnp.concatenate([_rotate(xf[..., :half], cr, sr), _rotate(xf[..., half:], cc, sc)], axis=-1)
    return out.astype(x.dtype)

def qkv_project(h, w_qkv, g_q, g_k):
    B, L, _ = h.shape
    qkv = h @ w_qkv
    q = qkv[..., :N_Q_HEADS * HEAD_DIM_2].reshape(B, L, N_Q_HEADS, HEAD_DIM_2)
    k = qkv[..., N_Q_HEADS * HEAD_DIM_2:(N_Q_HEADS + N_KV_HEADS) * HEAD_DIM_2].reshape(B, L, N_KV_HEADS, HEAD_DIM_2)
    v = qkv[..., (N_Q_HEADS + N_KV_HEADS) * HEAD_DIM_2:].reshape(B, L, N_KV_HEADS, HEAD_DIM_2)
    return rms_norm(q, g_q), rms_norm(k, g_k), v

def attend(q, k, v):
    s = jnp.einsum('bqhgd,bkhd->bhgqk', q, k).astype(jnp.float32) * (HEAD_DIM_2 ** -0.5)
    p = jax.nn.softmax(s, axis=-1).astype(v.dtype)
    return jnp.einsum('bhgqk,bkhd->bqhgd', p, v)

def attention_mixer(h_lat, h_ctx, w_qkv, g_q, g_k, w_o, need_ctx_out):
    B, L, D = h_lat.shape
    C = h_ctx.shape[1]
    tables = axial_rope_tables(L)
    q_l, k_l, v_l = qkv_project(h_lat, w_qkv, g_q, g_k)
    q_l = apply_axial_rope(q_l, tables)
    k_l = apply_axial_rope(k_l, tables)
    q_c, k_c, v_c = qkv_project(h_ctx, w_qkv, g_q, g_k)
    k_all = jnp.concatenate([k_c, k_l], axis=1)
    v_all = jnp.concatenate([v_c, v_l], axis=1)
    nb = L // Q_BLOCK
    qb = q_l.reshape(B, nb, Q_BLOCK, N_KV_HEADS, Q_PER_KV, HEAD_DIM_2).transpose(1, 0, 2, 3, 4, 5)
    o_blocks = lax.map(lambda qblk: attend(qblk, k_all, v_all), qb)
    o_lat = o_blocks.transpose(1, 0, 2, 3, 4, 5).reshape(B, L, D) @ w_o
    o_ctx = None
    if need_ctx_out:
        qc = q_c.reshape(B, C, N_KV_HEADS, Q_PER_KV, HEAD_DIM_2)
        o_ctx = attend(qc, k_c, v_c).reshape(B, C, D) @ w_o
    return o_lat, o_ctx

def sq_relu_mlp(h, w_in, w_out):
    return jnp.square(jax.nn.relu(h @ w_in)) @ w_out

def second_inputs(seed: int = 0) -> dict:
    key = jax.random.key(seed)
    ks = jax.random.split(key, 20)
    f32 = jnp.float32
    nrm = lambda k, shape: jax.random.normal(k, shape, f32)
    gain = lambda k, shape: 1.0 + 0.05 * nrm(k, shape)
    return {
        'x': nrm(ks[0], (BATCH, SEQ, D_MODEL)),
        'c': nrm(ks[1], (BATCH, D_MODEL)),
        'ctx': nrm(ks[2], (BATCH, CTX_LEN, D_MODEL)),
        'c_ctx': nrm(ks[3], (D_MODEL,)),
        'w_ada': nrm(ks[4], (DEPTH, D_MODEL, N_MOD * D_MODEL)) * (0.5 * D_MODEL ** -0.5),
        'b_ada': 0.01 * nrm(ks[5], (DEPTH, N_MOD * D_MODEL)),
        'g_mix_pre': gain(ks[6], (DEPTH, D_MODEL)),
        'g_mix_post': gain(ks[7], (DEPTH, D_MODEL)),
        'g_mlp_pre': gain(ks[8], (DEPTH, D_MODEL)),
        'g_mlp_post': gain(ks[9], (DEPTH, D_MODEL)),
        'w_pool': nrm(ks[10], (N_POOL_LAYERS, N_POOL_GROUPS, POOL_GROUP_DIM, POOL_GROUP_DIM)) * POOL_GROUP_DIM ** -0.5,
        'pool_scale': 1.0 + 0.1 * nrm(ks[11], (N_POOL_LAYERS, D_MODEL)),
        'w_qkv': nrm(ks[12], (N_ATTN_LAYERS, D_MODEL, QKV_DIM)) * D_MODEL ** -0.5,
        'g_q': gain(ks[13], (N_ATTN_LAYERS, HEAD_DIM_2)),
        'g_k': gain(ks[14], (N_ATTN_LAYERS, HEAD_DIM_2)),
        'w_o': nrm(ks[15], (N_ATTN_LAYERS, D_MODEL, D_MODEL)) * D_MODEL ** -0.5,
        'w_mlp_in': nrm(ks[16], (DEPTH, D_MODEL, D_FF_2)) * D_MODEL ** -0.5,
        'w_mlp_out': nrm(ks[17], (DEPTH, D_FF_2, D_MODEL)) * D_FF_2 ** -0.5,
    }

def second_block(x, c, ctx, c_ctx, w_ada, b_ada, g_mix_pre, g_mix_post, g_mlp_pre, g_mlp_post,
              w_pool, pool_scale, w_qkv, g_q, g_k, w_o, w_mlp_in, w_mlp_out):
    for i in range(DEPTH):
        last = i == DEPTH - 1
        j = i // N_MIXERS
        sh1, sc1, gt1, sh2, sc2, gt2 = ada_mods(c, w_ada[i], b_ada[i])
        csh1, csc1, cgt1, csh2, csc2, cgt2 = ada_mods(c_ctx, w_ada[i], b_ada[i])
        h_lat = modulate(rms_norm(x, g_mix_pre[i]), sh1, sc1)
        h_ctx = modulate(rms_norm(ctx, g_mix_pre[i]), csh1, csc1)
        if i % N_MIXERS == 0:
            y_lat = pool_mixer(h_lat, w_pool[j], pool_scale[j])
            y_ctx = None if last else pool_mixer(h_ctx, w_pool[j], pool_scale[j])
        else:
            y_lat, y_ctx = attention_mixer(h_lat, h_ctx, w_qkv[j], g_q[j], g_k[j], w_o[j], not last)
        x = x + gt1 * rms_norm(y_lat, g_mix_post[i])
        m_lat = sq_relu_mlp(modulate(rms_norm(x, g_mlp_pre[i]), sh2, sc2), w_mlp_in[i], w_mlp_out[i])
        x = x + gt2 * rms_norm(m_lat, g_mlp_post[i])
        if not last:
            ctx = ctx + cgt1 * rms_norm(y_ctx, g_mix_post[i])
            m_ctx = sq_relu_mlp(modulate(rms_norm(ctx, g_mlp_pre[i]), csh2, csc2), w_mlp_in[i], w_mlp_out[i])
            ctx = ctx + cgt2 * rms_norm(m_ctx, g_mlp_post[i])
    return x


def setup_inputs(seed=0):
    out = dict(first_inputs(seed))
    for name, value in second_inputs(seed + 1).items():
        if name != "x":
            out[name + "_2"] = value
    return out


def reference(
    x, c, ada_w, ada_b, norm_g, ffn_w_in, ffn_w_out, mix_w_in, cmp_pe, cmp_w1, cmp_w2, gm_ln_g,
    gm_ln_b, gm_ws, gm_bs, proj_a, proj_b, w_out, final_g, c_2, ctx_2, c_ctx_2, w_ada_2,
    b_ada_2, g_mix_pre_2, g_mix_post_2, g_mlp_pre_2, g_mlp_post_2, w_pool_2, pool_scale_2,
    w_qkv_2, g_q_2, g_k_2, w_o_2, w_mlp_in_2, w_mlp_out_2,
):
    x = first_block(
        x, c, ada_w, ada_b, norm_g, ffn_w_in, ffn_w_out, mix_w_in, cmp_pe, cmp_w1, cmp_w2,
        gm_ln_g, gm_ln_b, gm_ws, gm_bs, proj_a, proj_b, w_out, final_g,
    )
    return second_block(
        x, c_2, ctx_2, c_ctx_2, w_ada_2, b_ada_2, g_mix_pre_2, g_mix_post_2, g_mlp_pre_2,
        g_mlp_post_2, w_pool_2, pool_scale_2, w_qkv_2, g_q_2, g_k_2, w_o_2, w_mlp_in_2,
        w_mlp_out_2,
    )


_drawn_inputs = setup_inputs


def setup_inputs(seed=0):
    import zlib

    import numpy as np

    out = dict(_drawn_inputs(seed))
    spreads = {}
    factors = {'cmp_pe': 7.724,
     'gm_ln_g': 4.613,
     'gm_ln_b': 4.607,
     'gm_bs': 3.21,
     'b_ada_2': 2.676,
     'g_mix_pre_2': 3.464,
     'g_mix_post_2': 2.702,
     'g_mlp_post_2': 2.881,
     'g_q_2': 8.0,
     'g_k_2': 8.0}
    for name, (base, spread) in spreads.items():
        noise = np.random.default_rng([zlib.crc32(name.encode()), seed]).standard_normal(out[name].shape)
        drawn = base * np.exp(spread * noise) if base else spread * noise
        out[name] = __import__('jax').numpy.asarray(drawn.astype(out[name].dtype))
    for name, factor in factors.items():
        out[name] = (out[name] * factor).astype(out[name].dtype)
    return out
```

```python
from contextlib import ExitStack

import numpy as np
import concourse.bass as bass
from concourse import mybir

F32 = mybir.dt.float32
F32R = mybir.dt.float32r
BF16 = mybir.dt.bfloat16
ALU = mybir.AluOpType
ACT = mybir.ActivationFunctionType
AX = mybir.AxisListType.X

D = 1024
KT = 8
S = 512
C = 256
NF = 22
NF2 = 32
EPS = 1e-6
ENGINES = ("pe", "act", "dve", "pool", "sp")


def ffn_chunks(nf):
    out, at = [], 0
    while at < nf:
        out.append((at, min(4, nf - at)))
        at += 4
    return out


def plan():
    out = []

    def cols(a, idx, r0, nk, c0, n, w):
        for c in range(c0, c0 + n, w):
            out.append((a, idx, r0, nk, c, min(w, c0 + n - c)))

    def ffn1(l, j):
        cs = ffn_chunks(NF)
        for i, (f0, nf) in enumerate(cs):
            for p in range(0, nf, 2):
                out.append(("ffn_w_in", (l, j), 0, KT, (f0 + p) * 128, 256))
                out.append(("ffn_w_in", (l, j), 0, KT, (NF + f0 + p) * 128, 256))
            for g0, ng in ([cs[i - 1]] if i else []) + ([(f0, nf)] if i == len(cs) - 1 else []):
                cols("ffn_w_out", (l, j), g0 * 128, ng, 0, D, 2048 // ng)

    def ffn2(l):
        cs = ffn_chunks(NF2)
        for i, (f0, nf) in enumerate(cs):
            cols("w_mlp_in_2", (l,), 0, KT, f0 * 128, nf * 128, 256)
            for g0, ng in ([cs[i - 1]] if i else []) + ([(f0, nf)] if i == len(cs) - 1 else []):
                cols("w_mlp_out_2", (l,), g0 * 128, ng, 0, D, 2048 // ng)

    for l in range(2):
        ffn1(l, 0)
        cols("mix_w_in", (l,), 0, KT, 512, 768, 256)
        cols("mix_w_in", (l,), 0, KT, 0, 512, 256)
        out.append(("mix_w_in", (l,), 0, KT, 1280, 24))
        out.append(("cmp_w1", (l, 0), 0, 16, 0, 128))
        out.append(("cmp_w1", (l, 1), 0, 16, 0, 128))
        cols("mix_w_in", (l,), 0, KT, 1304, 1024, 256)
        for m in range(4):
            out.append(("mix_w_in", (l,), 0, KT, 2328 + 256 * m, 256))
            out.append(("proj_a", (l,), 0, 4, 256 * m, 256))
            out.append(("mix_w_in", (l,), 0, KT, 3352 + 256 * m, 256))
            out.append(("proj_b", (l,), 0, 4, 256 * m, 256))
        cols("w_out", (l,), 0, KT, 0, D, 256)
        ffn1(l, 1)
    out.append(("w_pool_2", (0,), 0, 8, 0, 256))
    ffn2(0)
    out.append(("w_pool_2", (0,), 0, 8, 0, 256))
    ffn2(0)
    cols("w_qkv_2", (0,), 0, KT, 1024, 512, 256)
    cols("w_qkv_2", (0,), 0, KT, 0, 1536, 256)
    cols("w_o_2", (0,), 0, KT, 0, D, 256)
    ffn2(1)
    return out


def ada_plan():
    out = [(1, l, m, True, False) for l in range(2) for m in range(9)]
    out += [(2, 0, m, True, True) for m in range(6)]
    out += [(2, 1, m, True, m < 2) for m in range(6)]
    return out


VEC = {}


def vec_layout():
    at, out = 0, {}
    for name, n in (("norm_g", 48), ("ada_b", 144), ("final_g", 8), ("b_ada_2", 96), ("g_mix_pre_2", 16),
                    ("g_mix_post_2", 16), ("g_mlp_pre_2", 16), ("g_mlp_post_2", 16), ("pool_scale_2", 8),
                    ("g_q_2", 1), ("g_k_2", 1), ("c", 8), ("c_2", 8), ("c_ctx_2", 8)):
        out[name] = at
        at += n
    return out, at


class Program:

    def __init__(self, nc, ctx):
        self.nc, self.ctx = nc, ctx
        self.queue = {e: [] for e in ENGINES}
        self.count = {e: 0 for e in ENGINES}
        self.sem = {e: ctx.enter_context(nc.semaphore("s_" + e)) for e in ENGINES}
        self.seen = {e: {} for e in ENGINES}
        self.dma_sems = {}
        self.n = 0

    def wait(self, e, *tokens):
        for t in tokens:
            if t is None:
                continue
            if isinstance(t, list):
                self.wait(e, *t)
                continue
            key, sem, val = t
            if self.seen[e].get(key, 0) < val:
                self.seen[e][key] = val
                self.queue[e].append(lambda g, sem=sem, val=val: g.wait_ge(sem, val))

    def op(self, e, fn, *tokens):
        self.wait(e, *tokens)
        self.count[e] += 1
        self.queue[e].append(lambda g, fn=fn, s=self.sem[e]: fn(g).then_inc(s, 1))
        return (e, self.sem[e], self.count[e])

    def quiet(self, e, fn, *tokens):
        self.wait(e, *tokens)
        self.queue[e].append(fn)

    def last(self, e):
        return (e, self.sem[e], self.count[e]) if self.count[e] else None

    def dma(self, e, name, out, in_, *tokens):
        self.wait(e, *tokens)
        if name not in self.dma_sems:
            self.dma_sems[name] = [self.ctx.enter_context(self.nc.semaphore("d_" + name)), 0]
        d = self.dma_sems[name]
        d[1] += 16
        self.queue[e].append(lambda g, s=d[0]: g.dma_start(out, in_).then_inc(s, 16))
        return ("d_" + name, d[0], d[1])

    def everyone(self):
        return [self.last(e) for e in ("pe", "act", "dve", "pool")]

    def barrier(self):
        now = self.everyone()
        for e in ENGINES:
            self.wait(e, now)

    def emit(self, block):
        def run(e):
            def body(g):
                for f in self.queue[e]:
                    f(g)
            return body
        block.tensor(run("pe"))
        block.scalar(run("act"))
        block.vector(run("dve"))
        block.gpsimd(run("pool"))
        block.sync(run("sp"))


def build(nc, A, out):
    ctx = ExitStack()
    P = Program(nc, ctx)
    slots = plan()
    adas = ada_plan()
    VEC, NV = vec_layout()
    names = [0]

    def sb(scope, name, shape, dt=F32):
        names[0] += 1
        return scope.enter_context(nc.sbuf_tensor(f"{name}_{names[0]}", shape, dt))

    with ctx:
        h = sb(ctx, "h", [128, KT, S])
        nH = sb(ctx, "nH", [128, KT, S], F32R)
        nL = sb(ctx, "nL", [128, KT, S], F32R)
        NR, NW, NA = 3, 3, 2
        raw = [sb(ctx, f"raw{i}", [128, 2048]) for i in range(NR)]
        WH = [sb(ctx, f"WH{i}", [128, 2048], F32R) for i in range(NW)]
        WL = [sb(ctx, f"WL{i}", [128, 2048], F32R) for i in range(NW)]
        araw = [sb(ctx, f"araw{i}", [128, 1024]) for i in range(NA)]
        aacc = [sb(ctx, f"aacc{i}", [128, 1024]) for i in range(2)]
        vec = sb(ctx, "vec", [128, NV])
        cs = sb(ctx, "cs", [128, 24])
        mods = sb(ctx, "mods", [128, 38 * 8])
        der = sb(ctx, "der", [128, 2, 32])
        ident = sb(ctx, "ident", [128, 128])
        ones = sb(ctx, "ones", [128, 128])
        epsc = sb(ctx, "epsc", [128, 1])
        tiny = sb(ctx, "tiny", [128, 64])
        banks = [ctx.enter_context(nc.psum_tensor(f"ps{i}", [128, 512], F32)) for i in range(8)]

        class Banks(dict):

            def __init__(self):
                super().__init__({b: None for b in range(8)})
                self.order = list(range(6))

            def __setitem__(self, b, token):
                super().__setitem__(b, token)
                if b < 6:
                    if b in self.order:
                        self.order.remove(b)
                    self.order.append(b)

        bank_free = Banks()

        def take():
            b = bank_free.order.pop(0)
            return b, bank_free[b]

        def mm(out_, lhsT, rhs, start, stop, *tokens, inc=False, **kw):
            f = lambda g: g.matmul(out_, lhsT, rhs, start=start, stop=stop, **kw)
            if inc:
                return P.op("pe", f, *tokens)
            P.quiet("pe", f, *tokens)

        def tr(out_, in_, idn, *tokens, inc=False):
            f = lambda g: g.transpose(out_, in_, idn)
            if inc:
                return P.op("pe", f, *tokens)
            P.quiet("pe", f, *tokens)

        def act(out_, in_, func, *tokens, **kw):
            return P.op("act", lambda g: g.activation(out_, in_, func, **kw), *tokens)

        def tt(out_, a, b, op, *tokens, e="dve"):
            return P.op(e, lambda g: g.tensor_tensor(out_, a, b, op), *tokens)

        def ts(out_, a, s1, s2, op0, op1, *tokens, e="dve"):
            if s2 is None:
                return P.op(e, lambda g: g.tensor_scalar(out_, a, s1, None, op0), *tokens)
            return P.op(e, lambda g: g.tensor_scalar(out_, a, s1, s2, op0, op1), *tokens)

        def stt(out_, a, s, b, op0, op1, *tokens):
            return P.op("dve", lambda g: g.scalar_tensor_tensor(out=out_, in0=a, scalar=s, in1=b, op0=op0, op1=op1),
                        *tokens)

        def cp(e, out_, in_, *tokens):
            if e == "act":
                return act(out_, in_, ACT.Copy, *tokens)
            return P.op(e, lambda g: g.tensor_copy(out_, in_), *tokens)

        t_vec = P.dma("sp", "vec", vec[:, :], A["vec"])
        t_id = P.dma("sp", "ident", ident[:, :], A["ident"])
        t_h = P.dma("sp", "h", h[:, :, :], A["xT"])
        t_ones = P.op("dve", lambda g: g.memset(ones[:, :], 1.0))
        t_eps = P.op("dve", lambda g: g.memset(epsc[:, :], EPS))
        t_cs = act(cs[:, :], vec[:, VEC["c"]:VEC["c"] + 24], ACT.Silu, t_vec)
        for e in ("pe", "act", "dve", "pool"):
            P.wait(e, t_vec, t_id, t_ones, t_eps, t_cs)

        def V(name, i=0, n=8):
            return vec[:, VEC[name] + i:VEC[name] + i + n]

        offs, at = [], 0
        for s in slots:
            offs.append(at)
            at += 128 * s[3] * s[5]
        W = A["wst"]
        st = dict(loaded=0, split=0, used=0)
        t_raw = [None] * len(slots)
        t_hi = [None] * len(slots)
        t_lo = [None] * len(slots)
        t_use = [None] * len(slots)

        def load(k):
            n = slots[k][3] * slots[k][5]
            src = W[offs[k]:offs[k] + 128 * n].rearrange("(p n) -> p n", p=128)
            free = [t_hi[k - NR], t_lo[k - NR]] if k >= NR else None
            t_raw[k] = P.dma("sp", f"raw{k % NR}", raw[k % NR][:, 0:n], src, free)

        def split(k):
            n = slots[k][3] * slots[k][5]
            free = t_use[k - NW] if k >= NW else None
            r, a, b = raw[k % NR], WH[k % NW], WL[k % NW]
            t_hi[k] = act(a[:, 0:n], r[:, 0:n], ACT.Copy, t_raw[k], free)
            t_lo[k] = tt(b[:, 0:n], r[:, 0:n], a[:, 0:n].bitcast(F32), ALU.subtract, t_raw[k], free, t_hi[k])

        def advance():
            done_ = next((i for i in range(st["used"] + 1) if i == st["used"] or t_use[i] is None))
            while st["split"] < min(done_ + NW, len(slots)):
                while st["loaded"] < min(st["split"] + NR, len(slots)):
                    if st["loaded"] >= NR and t_lo[st["loaded"] - NR] is None:
                        break
                    load(st["loaded"])
                    st["loaded"] += 1
                split(st["split"])
                st["split"] += 1
            while st["loaded"] < min(st["split"] + NR, len(slots)):
                load(st["loaded"])
                st["loaded"] += 1

        def slot(want):
            k = st["used"]
            assert slots[k][0] == want, (slots[k], want)
            advance()
            st["used"] += 1
            ada_step()
            _, _, _, nk, _, nc_ = slots[k]
            hi = WH[k % NW][:, 0:nk * nc_].rearrange("p (k c) -> p k c", k=nk)
            lo = WL[k % NW][:, 0:nk * nc_].rearrange("p (k c) -> p k c", k=nk)
            return k, hi, lo, [t_hi[k], t_lo[k]]

        def done(k, tok):
            t_use[k] = tok

        mod_col, c_ = {}, 0
        for b_, l_, m_, a1, a2 in adas:
            mod_col[(b_, l_, m_, 0)] = c_
            c_ += 8
            if a2:
                mod_col[(b_, l_, m_, 1)] = c_
                c_ += 8
        assert c_ <= 38 * 8
        ad = dict(step=0, loaded=0, pend=[])
        t_araw, t_aread, t_acc = {}, {}, [None, None]
        t_red = [None, None]
        acc_i = [0]
        t_mod = {}
        cur = {}

        def ada_load(j):
            t_araw[j] = P.dma("sp", f"araw{j % NA}", araw[j % NA][:, :], A["ast"][j], t_aread.get(j - NA))

        def ada_flush():
            for b, psb, t_pe, m, bias in ad["pend"]:
                t = tt(mods[:, m:m + 8], banks[b][:, 0:8], bias, ALU.add, t_pe)
                bank_free[b] = t
                t_mod[m] = t
            ad["pend"] = []

        def ada_step():
            j = ad["step"]
            if j >= 8 * len(adas):
                ada_flush()
                return
            while ad["loaded"] < min(8 * len(adas), j + NA):
                ada_load(ad["loaded"])
                ad["loaded"] += 1
            b_, l_, m_, a1, a2 = adas[j // 8]
            kt = j % 8
            if kt == 1:
                ada_flush()
            w = araw[j % NA]
            kinds = [0, 1] if a2 else [0]
            for q in kinds:
                if kt == 0:
                    cur[q] = acc_i[0]
                    acc_i[0] = (acc_i[0] + 1) % 2
                a = cur[q]
                col = (0 if b_ == 1 else 8 + 8 * q) + kt
                if kt == 0:
                    t = ts(aacc[a][:, :], w[:, :], cs[:, col:col + 1], None, ALU.mult, None, t_araw[j], t_red[a])
                else:
                    t = stt(aacc[a][:, :], w[:, :], cs[:, col:col + 1], aacc[a][:, :], ALU.mult, ALU.add,
                            t_araw[j], t_acc[a])
                t_acc[a] = t
            t_aread[j] = t
            ad["step"] += 1
            if kt == 7:
                for q in kinds:
                    a = cur[q]
                    b, free = take()
                    for f in range(8):
                        t_pe = mm(banks[b][:, f:f + 1], aacc[a][:, f * 128:f * 128 + 128], ones[:, 0:1], True, True,
                                  free, t_acc[a], inc=(f == 7))
                    t_red[a] = t_pe
                    bias = V("ada_b", l_ * 72 + m_ * 8) if b_ == 1 else V("b_ada_2", l_ * 48 + m_ * 8)
                    ad["pend"].append((b, None, t_pe, mod_col[(b_, l_, m_, q)], bias))

        def mod(b_, l_, m_, q=0):
            m = mod_col[(b_, l_, m_, q)]
            while m not in t_mod:
                if any(p[3] == m for p in ad["pend"]):
                    ada_flush()
                else:
                    ada_step()
            return mods[:, m:m + 8], t_mod[m]

        der_i = [0]
        der_read = [None, None]

        def scaled_gain(g, b_, l_, m_, q=0):
            sh, t1 = mod(b_, l_, m_, q)
            sc, t2 = mod(b_, l_, m_ + 1, q)
            i = der_i[0]
            der_i[0] = 1 - i
            G = der[:, i, 0:8]
            t = stt(G, sc, 1.0, g, ALU.add, ALU.mult, t1, t2, P.last("act"), P.last("dve"), P.last("pool"))
            return G, sh, [t, t1]

        def rstd(scope, tiles, toks, N, dim, pre="n"):
            sq = [sb(scope, f"sq{i}", [128, N]) for i in range(2)]
            ssum = sb(scope, "ssum", [128, N])
            dg = sb(scope, "dg", [128, N])
            t_add = [None] * len(tiles)
            for i, (x, tk) in enumerate(zip(tiles, toks)):
                o = ssum if len(tiles) == 1 else sq[i % 2]
                t = act(o[:, :], x, ACT.Square, tk, t_add[i - 2] if i >= 2 else None)
                if i == 0:
                    t_first = t
                    t_add[0] = t
                elif i == 1:
                    t_add[0] = t_add[1] = tt(ssum[:, :], sq[0][:, :], sq[1][:, :], ALU.add, t_first, t)
                else:
                    t_add[i] = tt(ssum[:, :], ssum[:, :], sq[i % 2][:, :], ALU.add, t, t_add[i - 1])
            t_sum = t_add[-1]
            nt = N // 128
            b, free = take()
            for j in range(nt):
                t = mm(banks[b][:, j:j + 1], ssum[:, j * 128:j * 128 + 128], ones[:, 0:1], True, True,
                       free, t_sum, inc=(j == nt - 1))
            s = sb(scope, "rs", [128, 8])
            t = act(s[:, 0:nt], banks[b][:, 0:nt], ACT.Sqrt, t, bias=epsc[:, 0:1], scale=1.0 / dim)
            bank_free[b] = t
            t = P.op("dve", lambda g: g.reciprocal(s[:, 4:4 + nt], s[:, 0:nt]), t)
            for j in range(nt):
                td = ts(dg[:, j * 128:j * 128 + 128], ident[:, :], s[:, 4 + j:5 + j], None, ALU.mult, None, t)
            b, free = take()
            t = mm(banks[b][:, 0:N], ones[:, :], dg[:, :], True, True, free, td, inc=True)
            return b, t

        def halves(dH, dL, y, tok, free=None):
            t1 = act(dH, y, ACT.Copy, tok, free)
            t2 = tt(dL, y, dH.bitcast(F32), ALU.subtract, tok, t1, free)
            return [t1, t2]

        def normed(tiles, toks, N, G, Sh, t_gs, keep=None):
            outs = []
            with ExitStack() as sc:
                P.barrier()
                b, t_r = rstd(sc, tiles, toks, N, D)
                t_ = [sb(sc, f"t{i}", [128, N]) for i in range(2)]
                y_ = [sb(sc, f"y{i}", [128, N]) for i in range(2)]
                ty = [None] * len(tiles)
                tl = [None] * len(tiles)
                th = [None] * len(tiles)
                for i, x in enumerate(tiles):
                    t, y = t_[i % 2], y_[i % 2]
                    fr = [ty[i - 2], th[i - 2]] if i >= 2 else None
                    t1 = tt(t[:, :], x, banks[b][:, 0:N], ALU.mult, t_r, toks[i], fr)
                    if i == len(tiles) - 1:
                        bank_free[b] = t1
                    sh = Sh[:, i:i + 1] if Sh is not None else None
                    if keep is not None:
                        if sh is None:
                            ty[i] = th[i] = ts(keep(i), t[:, :], G[:, i:i + 1], None, ALU.mult, None, t1, t_gs)
                        else:
                            ty[i] = th[i] = act(keep(i), t[:, :], ACT.Identity, t1, t_gs, scale=G[:, i:i + 1], bias=sh)
                        outs.append(ty[i])
                        continue
                    th[i] = act(nH[:, i, 0:N], t[:, :], ACT.Identity, t1, t_gs, scale=G[:, i:i + 1], bias=sh)
                    ty[i] = ts(y[:, :], t[:, :], G[:, i:i + 1], sh, ALU.mult, ALU.add, t1, t_gs,
                               tl[i - 2] if i >= 2 else None, e="pool")
                    tl[i] = tt(nL[:, i, 0:N], y[:, :], nH[:, i, 0:N].bitcast(F32), ALU.subtract, ty[i], th[i])
                    outs.append([th[i], tl[i]])
            return outs

        def groups(k, hi, lo, tw, xH, xL, tx, N, each=None):
            nk = hi.shape[1]
            res = []
            for c in range(hi.shape[2] // 128):
                b, free = take()
                cc = slice(c * 128, c * 128 + 128)
                for i in range(nk):
                    for n, (w, x) in enumerate(((hi, xH), (hi, xL), (lo, xH))):
                        t = mm(banks[b][:, 0:N], w[:, i, cc], x(i), i == 0 and n == 0, i == nk - 1 and n == 2,
                               free, tw, tx[i], inc=(i == nk - 1 and n == 2))
                res.append((b, t))
                if c == hi.shape[2] // 128 - 1:
                    done(k, t)
                if each:
                    each(c, b, t)
            return res

        def wide(sl, xH, xL, tx, N):
            cols, res = [], []
            for (k, hi, lo, tw) in sl:
                for c in range(hi.shape[2] // 128):
                    b, free = take()
                    cols.append((b, free, k, hi, lo, tw, slice(c * 128, c * 128 + 128)))
            nk = sl[0][1].shape[1]
            toks = {}
            for i in range(nk):
                for b, free, k, hi, lo, tw, cc in cols:
                    for n, (w, x) in enumerate(((hi, xH), (hi, xL), (lo, xH))):
                        t = mm(banks[b][:, 0:N], w[:, i, cc], x(i), i == 0 and n == 0, i == nk - 1 and n == 2,
                               free, tw, tx[i], inc=(i == nk - 1 and n == 2), skip_group_check=True)
                    toks[b] = t
            for b, free, k, *_ in cols:
                res.append((b, toks[b]))
                done(k, toks[b])
            return res

        nHk = lambda N: (lambda i: nH[:, i, 0:N])
        nLk = lambda N: (lambda i: nL[:, i, 0:N])

        def ffn(nf, w_in, w_out, tx, N, gated, sink):
            with ExitStack() as sc:
                P.barrier()
                hH = sb(sc, "hH", [128, 2, 4, N], F32R)
                hL = sb(sc, "hL", [128, 2, 4, N], F32R)
                a_ = [sb(sc, f"a{i}", [128, N]) for i in range(2)]
                y_ = [sb(sc, f"hy{i}", [128, N]) for i in range(2)]
                chunks = ffn_chunks(nf)
                t_hid = {}
                t_out = {}
                rd = [None, None]
                ra = [None, None]
                n_ = [0]

                def hidden(ci):
                    f0, cn = chunks[ci]
                    for p in range(0, cn, 2):
                        sl = [slot(w_in)]
                        if gated:
                            sl.append(slot(w_in))
                        if ci == 0 and p == 0:
                            res = wide(sl, nHk(N), nLk(N), tx, N)
                        else:
                            res = []
                            for q in sl:
                                res += groups(*q, nHk(N), nLk(N), tx, N)
                        for i in range(2):
                            f = p + i
                            b, t = res[i]
                            u = n_[0] % 2
                            n_[0] += 1
                            a, y = a_[u], y_[u]
                            free_h = t_out.get(ci - 2)
                            if gated:
                                ta = act(a[:, :], banks[b][:, 0:N], ACT.Silu, t, ra[u])
                                bank_free[b] = ta
                                b2, t2 = res[2 + i]
                                ty = tt(y[:, :], a[:, :], banks[b2][:, 0:N], ALU.mult, ta, t2, rd[u])
                                bank_free[b2] = ty
                            else:
                                ta = act(a[:, :], banks[b][:, 0:N], ACT.Relu, t, ra[u])
                                bank_free[b] = ta
                                ty = tt(y[:, :], a[:, :], a[:, :], ALU.mult, ta, rd[u])
                            ra[u] = ty
                            r = halves(hH[:, ci % 2, f, :], hL[:, ci % 2, f, :], y[:, :], ty, free_h)
                            rd[u] = r
                            t_hid[(ci, f)] = r

                def outp(ci):
                    f0, cn = chunks[ci]
                    tx_ = [t_hid[(ci, f)] for f in range(cn)]
                    o = 0
                    while o < 8:
                        q = slot(w_out)

                        def each(c, b, t):
                            bank_free[b] = sink(ci == 0, o + c, b, t)

                        res = groups(*q, lambda i: hH[:, ci % 2, i, :], lambda i: hL[:, ci % 2, i, :], tx_, N, each)
                        o += len(res)
                    t_out[ci] = res[-1][1]

                for ci in range(len(chunks)):
                    hidden(ci)
                    if ci:
                        outp(ci - 1)
                outp(len(chunks) - 1)

        th = [t_h] * 8
        htiles = [h[:, i, :] for i in range(8)]

        def add_to_h(gate, t_g):
            def sink(first, o, b, t):
                th[o] = stt(h[:, o, :], banks[b][:, :], gate[:, o:o + 1], h[:, o, :], ALU.mult, ALU.add, t, t_g, th[o])
                return th[o]
            return sink

        def ffn_block1(l, j):
            G, Sh, tg = scaled_gain(V("norm_g", (l * 3 + 2 * j) * 8), 1, l, 6 * j)
            tx = normed(htiles, th, S, G, Sh, tg)
            g, t_g = mod(1, l, 6 * j + 2)
            gh = der[:, j, 16:24]
            t_g = ts(gh, g, 0.5, None, ALU.mult, None, t_g, P.last("dve"))
            ffn(NF, "ffn_w_in", "ffn_w_out", tx, S, True, add_to_h(gh, t_g))

        def rope(b, t, N, cosT, sinT, dst, tmp, rot, t_tab, frees):
            for q in range(4):
                d0, s0 = 32 * q, 32 * (q ^ 1)
                tr_ = act(rot[d0:d0 + 32, 0:N], banks[b][s0:s0 + 32, 0:N], ACT.Copy, t, frees)
            t1 = tt(tmp[:, 0:N], banks[b][:, 0:N], cosT, ALU.mult, t, t_tab, frees, tr_)
            bank_free[b] = t1
            t2 = tt(rot[:, 0:N], rot[:, 0:N], sinT, ALU.mult, tr_, t_tab)
            return tt(dst, tmp[:, 0:N], rot[:, 0:N], ALU.add, t1, t2)

        def mixer(l):
            G, Sh, tg = scaled_gain(V("norm_g", (l * 3 + 1) * 8), 1, l, 3)
            tx = normed(htiles, th, S, G, Sh, tg)
            mg, t_mg = mod(1, l, 5)
            ph = ExitStack()
            P.barrier()
            yaH = sb(ph, "yaH", [128, 4, S], F32R)
            yaL = sb(ph, "yaL", [128, 4, S], F32R)
            t_ya = attention1(l, tx, yaH, yaL)
            P.barrier()
            ybH = sb(ph, "ybH", [128, 4, S], F32R)
            ybL = sb(ph, "ybL", [128, 4, S], F32R)
            t_yb = gmlp(l, tx, ybH, ybL)
            with ExitStack() as sc:
                P.barrier()
                mH = sb(sc, "mH", [128, 8, S], F32R)
                mL = sb(sc, "mL", [128, 8, S], F32R)
                sg = [sb(sc, "sg", [128, S])] * 2
                t_m = [None] * 8
                mt = [sb(sc, f"mt{i}", [128, S]) for i in range(2)]
                sg_free = [None]
                mt_free = [None, None]
                for m in range(4):
                    prod = {}
                    for which, (nm, xH, xL, ty) in enumerate((("proj_a", yaH, yaL, t_ya), ("proj_b", ybH, ybL, t_yb))):
                        q = slot("mix_w_in")
                        zs = groups(*q, nHk(S), nLk(S), tx, S)
                        ps_ = groups(*slot(nm), lambda i, x=xH: x[:, i, :], lambda i, x=xL: x[:, i, :], ty, S)
                        for i in range(2):
                            f = 2 * m + i
                            b, t = zs[i]
                            g = sg[i]
                            ta = act(g[:, :], banks[b][:, :], ACT.Sigmoid, t, sg_free[0])
                            bank_free[b] = ta
                            b2, t2 = ps_[i]
                            if which == 0:
                                tp = tt(mt[i][:, :], g[:, :], banks[b2][:, :], ALU.mult, ta, t2, mt_free[i])
                                bank_free[b2] = tp
                                sg_free[0] = tp
                                prod[i] = tp
                            else:
                                tp = tt(g[:, :], g[:, :], banks[b2][:, :], ALU.mult, ta, t2)
                                bank_free[b2] = tp
                                tp = tt(mt[i][:, :], mt[i][:, :], g[:, :], ALU.add, tp, prod[i])
                                sg_free[0] = tp
                                t_m[f] = halves(mH[:, f, :], mL[:, f, :], mt[i][:, :], tp)
                                mt_free[i] = t_m[f]
                sink = add_to_h(mg, t_mg)
                for o in range(0, 8, 2):
                    q = slot("w_out")
                    for i, (b, t) in enumerate(groups(*q, lambda i: mH[:, i, :], lambda i: mL[:, i, :], t_m, S)):
                        bank_free[b] = sink(False, o + i, b, t)
            ph.close()

        def attention1(l, tx, yaH, yaL):
            ph = ExitStack()
            q = sb(ph, "q", [128, 4, S])
            ko = [sb(ph, f"ko{i}", [128, S]) for i in range(2)]
            ks = [sb(ph, f"ks{i}", [128, S]) for i in range(2)]
            Vt = [sb(ph, f"Vt{i}", [128, 4, 128]) for i in range(2)]
            kc = sb(ph, "kc", [128, 2, 32])
            vc = sb(ph, "vc", [32, 128])
            gate = sb(ph, "gate", [128, 4, 24])
            negm = sb(ph, "negm", [128, 128], BF16)
            idb = sb(ph, "idb", [128, 128], BF16)
            cneg = sb(ph, "cneg", [128, 128], BF16)
            rowok = sb(ph, "rowok", [128, 4])
            t_negm = P.dma("sp", "negm", negm[:, :], A["negm"])
            t_idb = P.dma("sp", "idb", idb[:, :], A["idb"])
            t_cneg = P.dma("sp", "cneg", cneg[:, :], A["cneg"])
            t_row = P.dma("sp", "rowok", rowok[:, :], A["rowok"])

            with ExitStack() as sc:
                tab = sb(sc, "tab", [128, 4, S])
                ctab = sb(sc, "ctab", [128, 2, 32])
                tmp = sb(sc, "tmp", [128, S])
                rot = sb(sc, "rot", [128, S])
                cm = [sb(sc, f"cm{i}", [128, S]) for i in range(2)]
                R = sb(sc, "R", [128, 16, 62])
                RH = sb(sc, "RH", [128, 16, 62], F32R)
                RL = sb(sc, "RL", [128, 16, 62], F32R)
                pe_ = sb(sc, "pe", [128, 2, 16])
                w2 = sb(sc, "w2", [128, 192])
                hc = sb(sc, "hc", [128, 2, 62])
                t_tab = P.dma("sp", "tab", tab[:, :, :], A["rope1"])
                t_ctab = P.dma("sp", "ctab", ctab[:, :, :], A["crope"])
                t_pe = P.dma("sp", "pe", pe_[:, :, :], A["pe"][l])
                t_w2 = P.dma("sp", "w2", w2[:, :], A["w2"][l])
                t_vt = [None, None]
                t_k = [None, None]
                t_ks = [None, None]
                t_cm = [None, None]
                t_rope = None
                t_v = None
                for i in range(3):
                    res = groups(*slot("mix_w_in"), nHk(S), nLk(S), tx, S)
                    b, t = res[0]
                    b2, t2 = res[1]
                    if i == 0:
                        for j, (bb, t_) in enumerate(res):
                            t_cm[j] = cp("act", cm[j][:, :], banks[bb][:, :], t_)
                            bank_free[bb] = t_cm[j]
                        continue
                    t_rope = rope(b, t, S, tab[:, 2, :], tab[:, 3, :], ko[i - 1][:, :], tmp, rot, t_tab, t_rope)
                    t_k[i - 1] = t_rope
                    for hf in range(2):
                        t_ks[i - 1] = cp("pool", ks[i - 1][64 * hf:64 * hf + 64, :],
                                         ko[i - 1][64 - 64 * hf:128 - 64 * hf, :], t_rope)
                    vx = R[:, 0:9, :].rearrange("p a b -> p (a b)")[:, 0:S]
                    tv = cp("act", vx, banks[b2][:, :], t2, t_v)
                    bank_free[b2] = tv
                    bt, free = take()
                    for j in range(4):
                        t_v = tr(banks[bt][:, j * 128:j * 128 + 128], vx[:, j * 128:j * 128 + 128], ident[:, :],
                                 free, tv, inc=(j == 3))
                    t_vt[i - 1] = cp("act", Vt[i - 1][:, :, :], banks[bt][:, :].rearrange("p (a b) -> p a b", a=4), t_v)
                    bank_free[bt] = t_vt[i - 1]
                t_q = [None] * 4
                for i in range(2):
                    for j, (b, t) in enumerate(groups(*slot("mix_w_in"), nHk(S), nLk(S), tx, S)):
                        t_rope = rope(b, t, S, tab[:, 0, :], tab[:, 1, :], q[:, 2 * i + j, :], tmp, rot, t_tab, t_rope)
                        t_q[2 * i + j] = t_rope
                k, hi, lo, tw = slot("mix_w_in")
                b, free = take()
                for j in range(4):
                    tok_ = slice(j * 128, j * 128 + 128)
                    for i in range(8):
                        for n, (x, w) in enumerate(((nH, hi), (nL, hi), (nH, lo))):
                            t = mm(banks[b][:, j * 32:j * 32 + 24], x[:, i, tok_], w[:, i, 0:24],
                                   i == 0 and n == 0, i == 7 and n == 2, free, tw, tx[i],
                                   inc=(j == 3 and i == 7 and n == 2))
                done(k, t)
                t_gate = act(gate[:, :, :], banks[b][:, 0:128].rearrange("p (a b) -> p a b", a=4)[:, :, 0:24],
                             ACT.Sigmoid, t)
                bank_free[b] = t_gate
                t_R = t_v
                for j in range(2):
                    for hf in range(2):
                        for g in range(2):
                            src = cm[j][64 * g:64 * g + 64, :].rearrange("p (n l) -> p l n", l=16)[:, :, hf:hf + 31]
                            dst = R[64 * hf:64 * hf + 64, :, 31 * g:31 * g + 31]
                            tc_ = cp("dve", dst, src, t_cm[j], t_R)
                    pb = pe_[:, j, :].unsqueeze(2).broadcast_to([128, 16, 62])
                    tc_ = tt(R[:, :, :], R[:, :, :], pb, ALU.add, tc_, t_pe)
                    r = halves(RH[:, :, :], RL[:, :, :], R[:, :, :], tc_, t_R)
                    k, hi, lo, tw = slot("cmp_w1")
                    b, free = take()
                    for i in range(16):
                        for n, (w, x) in enumerate(((hi, RH), (hi, RL), (lo, RH))):
                            t = mm(banks[b][:, 0:62], w[:, i, :], x[:, i, :], i == 0 and n == 0, i == 15 and n == 2,
                                   free, tw, r, inc=(i == 15 and n == 2))
                    done(k, t)
                    t_R = [t] + r
                    t = act(hc[:, j, :], banks[b][:, 0:62], ACT.Silu, t)
                    bank_free[b] = t
                    if j == 0:
                        b, free = take()
                        t = mm(banks[b][:, 0:62], w2[:, 0:128], hc[:, 0, :], True, True, free, t, t_w2, inc=True)
                        for qd in range(4):
                            d0, s0 = 32 * qd, 32 * (qd ^ 1)
                            tr_ = act(rot[d0:d0 + 32, 0:62], banks[b][s0:s0 + 32, 0:62], ACT.Copy, t, t_rope)
                        v3 = lambda x: x.rearrange("p (g n) -> p g n", g=2)
                        cb = ctab[:, 0, 0:31].unsqueeze(1).broadcast_to([128, 2, 31])
                        sb_ = ctab[:, 1, 0:31].unsqueeze(1).broadcast_to([128, 2, 31])
                        t1 = tt(v3(tmp[:, 0:62]), v3(banks[b][:, 0:62]), cb, ALU.mult, t, t_ctab, t_rope, tr_)
                        bank_free[b] = t1
                        t2 = tt(v3(rot[:, 0:62]), v3(rot[:, 0:62]), sb_, ALU.mult, tr_, t_ctab)
                        tz = P.op("dve", lambda g: g.memset(kc[:, :, :], 0.0))
                        t_kc = tt(kc[:, :, 0:31], v3(tmp[:, 0:62]), v3(rot[:, 0:62]), ALU.add, t1, t2, tz)
                    else:
                        b, free = take()
                        for g in range(2):
                            t = mm(banks[b][0:31, 64 * g:64 * g + 64], hc[:, 1, 31 * g:31 * g + 31], w2[:, 128:192],
                                   True, True, free, t, t_w2, inc=(g == 1)) or t
                        tz = P.op("dve", lambda g: g.memset(vc[:, :], 0.0))
                        t_vc = cp("dve", vc[0:31, :], banks[b][0:31, 0:128], t, tz)
                        bank_free[b] = t_vc

            P.barrier()
            Pb = [sb(ph, f"P{i}", [128, S]) for i in range(4)]
            PT = [sb(ph, f"PT{i}", [128, S]) for i in range(2)]
            Pc = [sb(ph, f"Pc{i}", [128, 4, 32]) for i in range(2)]
            PcT = [sb(ph, f"PcT{i}", [32, S]) for i in range(2)]
            st_ = sb(ph, "st", [128, 8, 4])
            stc = sb(ph, "stc", [128, 2, 16])
            yo = sb(ph, "yo", [128, 2, S])
            units = []
            for hh in range(8):
                units.append((hh, 0, 0))
                for qt in range(4):
                    units += [(hh, 1, qt), (hh, 2, qt)]
            U = len(units)
            sP, sPT = [None] * U, [None] * U
            p_free, pt_free = {}, {}
            pc_free, pct_free = {}, {}
            o_free = {6: bank_free[6], 7: bank_free[7]}
            t_ya = [None] * 4
            yo_free = [None, None]
            wait_c = [t_negm, t_idb, t_cneg, t_row, t_gate, t_kc, t_vc, t_vt[0], t_vt[1], t_k, t_ks, t_q]
            ntok = {"i": 0, "c": 0, "j": 0, "cj": 0}

            def score(u):
                hh, br, qt = units[u]
                hf, g = hh % 2, hh // 4
                ps_ = slice(64 * hf, 64 * hf + 64)
                b, free = take()
                if br == 0:
                    for x in range(4):
                        mm(banks[b][:, 32 * x:32 * x + 32], q[ps_, hh // 2, 128 * x:128 * x + 128], kc[ps_, g, :],
                           x == 0, False, free, wait_c, skip_group_check=True)
                    t = mm(banks[b][:, 0:128], idb[:, :], cneg[:, :], False, True, skip_group_check=True, inc=True)
                    i = ntok["c"] % 2
                    ntok["c"] += 1
                    bk = banks[b][:, 0:128].rearrange("p (a b) -> p a b", a=4)
                    mx, sm, rr = stc[:, i, 0:4], stc[:, i, 4:8], stc[:, i, 8:12]
                    bc = lambda x: x.unsqueeze(2).broadcast_to([128, 4, 32])
                    t = P.op("dve", lambda e: e.tensor_reduce(mx, bk, AX, ALU.max), t, pc_free.get(i))
                    t = tt(Pc[i][:, :, :], bk, bc(mx), ALU.subtract, t)
                    bank_free[b] = t
                    t = act(Pc[i][:, :, :], Pc[i][:, :, :], ACT.Exp, t)
                    t = P.op("dve", lambda e: e.tensor_reduce(sm, Pc[i][:, :, :], AX, ALU.add), t)
                    t = P.op("dve", lambda e: e.reciprocal(rr, sm), t)
                    t = tt(rr, rr, gate[:, :, 3 * hh], ALU.mult, t)
                    t = tt(rr, rr, rowok[:, :], ALU.mult, t, t_row)
                    t = tt(Pc[i][:, :, :], Pc[i][:, :, :], bc(rr), ALU.mult, t)
                    sP[u] = (t, i)
                    return
                nk = 128 * (qt + 1)
                K = (ko if hf == g else ks)[br - 1]
                mm(banks[b][:, 0:nk], q[ps_, hh // 2, 128 * qt:128 * qt + 128], K[ps_, 0:nk], True, False,
                   free, wait_c, skip_group_check=True)
                t = mm(banks[b][:, nk - 128:nk], idb[:, :], negm[:, :], False, True, skip_group_check=True, inc=True)
                i = ntok["i"] % 4
                ntok["i"] += 1
                mx, sm, rr = st_[:, i, 0:1], st_[:, i, 1:2], st_[:, i, 2:3]
                t = P.op("dve", lambda e: e.tensor_reduce(mx, banks[b][:, 0:nk], AX, ALU.max, negate=True),
                         t, p_free.get(i))
                t = act(Pb[i][:, 0:nk], banks[b][:, 0:nk], ACT.Exp, t, bias=mx, accum_out=sm)
                bank_free[b] = t
                t = P.op("dve", lambda e: e.reciprocal(rr, sm), t)
                t = tt(rr, rr, gate[:, qt, 3 * hh + br:3 * hh + br + 1], ALU.mult, t)
                t = ts(Pb[i][:, 0:nk], Pb[i][:, 0:nk], rr, None, ALU.mult, None, t, e="pool")
                sP[u] = (t, i)

            def turn(u):
                hh, br, qt = units[u]
                t, i = sP[u]
                b, free = take()
                if br == 0:
                    for x in range(4):
                        tp = tr(banks[b][0:32, 128 * x:128 * x + 128], Pc[i][:, x, :], ident[:, :], free, t,
                                inc=(x == 3))
                    pc_free[i] = tp
                    j = ntok["cj"] % 2
                    ntok["cj"] += 1
                    t = cp("dve", PcT[j][:, :], banks[b][0:32, :], tp, pct_free.get(j))
                    bank_free[b] = t
                    sPT[u] = (t, j)
                    return
                for x in range(qt + 1):
                    tp = tr(banks[b][:, 128 * x:128 * x + 128], Pb[i][:, 128 * x:128 * x + 128], ident[:, :], free, t,
                            inc=(x == qt))
                p_free[i] = tp
                j = ntok["j"] % 2
                ntok["j"] += 1
                nk = 128 * (qt + 1)
                t = cp("act" if u % 2 else "dve", PT[j][:, 0:nk], banks[b][:, 0:nk], tp, pt_free.get(j))
                bank_free[b] = t
                sPT[u] = (t, j)

            def value(u):
                hh, br, qt = units[u]
                hf, g, ft = hh % 2, hh // 4, hh // 2
                ob = 6 + ft % 2
                ps_ = slice(64 * hf, 64 * hf + 64)
                t, j = sPT[u]
                last = br == 2 and qt == 3
                if br == 0:
                    pct_free[j] = mm(banks[ob][ps_, :], vc[:, 64 * g:64 * g + 64], PcT[j][:, :], True, False,
                                     t, o_free[ob], skip_group_check=True, inc=True)
                    return
                for x in range(qt + 1):
                    tp = mm(banks[ob][ps_, 128 * qt:128 * qt + 128], Vt[br - 1][:, x, 64 * g:64 * g + 64],
                            PT[j][:, 128 * x:128 * x + 128], False, last and x == qt, t, skip_group_check=True,
                            inc=(x == qt))
                pt_free[j] = tp
                if last and hf == 1:
                    i = ft % 2
                    t = cp("act", yo[:, i, :], banks[ob][:, :], tp, yo_free[i])
                    o_free[ob] = t
                    t_ya[ft] = halves(yaH[:, ft, :], yaL[:, ft, :], yo[:, i, :], t)
                    yo_free[i] = t_ya[ft]

            for u in range(U + 3):
                if u < U:
                    score(u)
                if 2 <= u < U + 2:
                    turn(u - 2)
                if u >= 3:
                    value(u - 3)
            bank_free[6], bank_free[7] = o_free[6], o_free[7]
            ph.close()
            return t_ya

        def gmlp(l, tx, ybH, ybL):
            with ExitStack() as sc:
                uu = sb(sc, "uu", [128, 4, S])
                vf = sb(sc, "vf", [128, 4, S])
                vn = sb(sc, "vn", [128, 4, S])
                wT = sb(sc, "wT", [128, 8, 128])
                msk = sb(sc, "msk", [128, 128])
                bsb = sb(sc, "bsb", [128, 4, 128])
                lnp = sb(sc, "lnp", [128, 2, S])
                stt_ = sb(sc, "bst", [128, 4, 16])
                t_w = P.dma("sp", "wT", wT[:, :, :], A["wsT"][l])
                t_ms = P.dma("sp", "msk", msk[:, :], A["msk"])
                t_bs = P.dma("sp", "bsb", bsb[:, :, :], A["bsb"][l])
                t_ln = P.dma("sp", "lnp", lnp[:, :, :], A["lnp"][l])
                t_w = tt(wT[:, :, :], wT[:, :, :], msk[:, :].unsqueeze(1).broadcast_to([128, 8, 128]), ALU.mult,
                         t_w, t_ms, e="pool")
                t_u = [None] * 4
                t_v = [None] * 4
                for m in range(4):
                    for i, (b, t) in enumerate(groups(*slot("mix_w_in"), nHk(S), nLk(S), tx, S)):
                        f = 2 * m + i
                        d = uu[:, f, :] if f < 4 else vf[:, f - 4, :]
                        t = act(d, banks[b][:, :], ACT.Gelu_apprx_tanh, t)
                        bank_free[b] = t
                        if f < 4:
                            t_u[f] = t
                        else:
                            t_v[f - 4] = t
                t_n = [None] * 4
                for tt_ in range(4):
                    b, free = take()
                    for f in range(4):
                        t = tr(banks[b][:, f * 128:f * 128 + 128], vf[:, f, tt_ * 128:tt_ * 128 + 128], ident[:, :],
                               free, t_v[f], inc=(f == 3))
                    s = stt_[:, tt_, :]
                    t0 = t
                    t = P.op("dve", lambda g, s=s, b=b: g.bn_stats(s[:, 0:6], banks[b][:, :]), t)
                    t = P.op("dve", lambda g, s=s: g.bn_aggr(s[:, 6:8], s[:, 0:6]), t)
                    t = act(s[:, 8:9], s[:, 7:8], ACT.Sqrt, t, bias=epsc[:, 0:1])
                    t = P.op("dve", lambda g, s=s: g.reciprocal(s[:, 9:10], s[:, 8:9]), t)
                    t = ts(vn[:, tt_, :], banks[b][:, :], s[:, 6:7], s[:, 9:10], ALU.subtract, ALU.mult, t)
                    bank_free[b] = t
                    t = tt(vn[:, tt_, :], vn[:, tt_, :], lnp[:, 0, :], ALU.mult, t, t_ln)
                    t_n[tt_] = tt(vn[:, tt_, :], vn[:, tt_, :], lnp[:, 1, :], ALU.add, t, t_ln)
                t_y = [None] * 4
                for f in range(4):
                    b, free = take()
                    for hf in range(2):
                        for tt_ in range(4):
                            g = 2 * f + hf
                            t = mm(banks[b][64 * hf:64 * hf + 64, tt_ * 128:tt_ * 128 + 128],
                                   vn[:, tt_, 64 * g:64 * g + 64], wT[:, g, :], tt_ == 0, tt_ == 3, free, t_w, t_n[tt_],
                                   skip_group_check=True, inc=(hf == 1 and tt_ == 3))
                    v = vf[:, f, :].rearrange("p (a b) -> p a b", a=4)
                    t = tt(v, banks[b][:, :].rearrange("p (a b) -> p a b", a=4),
                           bsb[:, f, :].unsqueeze(1).broadcast_to([128, 4, 128]), ALU.add, t, t_bs)
                    bank_free[b] = t
                    t = tt(vf[:, f, :], vf[:, f, :], uu[:, f, :], ALU.mult, t, t_u[f])
                    t_y[f] = halves(ybH[:, f, :], ybL[:, f, :], vf[:, f, :], t)
                return t_y

        for l in range(2):
            ffn_block1(l, 0)
            mixer(l)
            ffn_block1(l, 1)
        fin = normed(htiles, th, S, V("final_g"), None, None, keep=lambda i: h[:, i, :])
        th[:] = fin

        b2 = ExitStack()
        P.barrier()
        xc = sb(b2, "xc", [128, KT, C])
        t_xc = P.dma("sp", "xc", xc[:, :, :], A["ctxT"], P.everyone())
        tc = [t_xc] * 8
        ctiles = [xc[:, i, :] for i in range(8)]

        def post(tiles, x, tx_, N, g, gt, t_gt):
            i = der_i[0]
            der_i[0] = 1 - i
            Gp = der[:, i, 8:16]
            t_gp = tt(Gp, g, gt, ALU.mult, t_gt, P.last("dve"), P.last("act"), P.last("pool"))
            ts_ = [t for _, t in tiles]
            with ExitStack() as sc:
                P.barrier()
                b, t_r = rstd(sc, [a for a, _ in tiles], ts_, N, D)
                t_ = [sb(sc, f"pt{i}", [128, N]) for i in range(2)]
                rd = [None, None]
                for i, (m, tm) in enumerate(tiles):
                    t1 = tt(t_[i % 2][:, :], m, banks[b][:, 0:N], ALU.mult, t_r, tm, rd[i % 2])
                    if i == 7:
                        bank_free[b] = t1
                    tx_[i] = stt(x[i], t_[i % 2][:, :], Gp[:, i:i + 1], x[i], ALU.mult, ALU.add, t1, t_gp, tx_[i])
                    rd[i % 2] = tx_[i]

        def mlp2(l, x, tx_, N, q):
            G, Sh, tg = scaled_gain(V("g_mlp_pre_2", l * 8), 2, l, 3, q)
            tx = normed(x, tx_, N, G, Sh, tg)
            gt, t_gt = mod(2, l, 5, q)
            with ExitStack() as sc:
                P.barrier()
                ma = sb(sc, "ma", [128, KT, N])
                tm = [None] * 8

                def sink(first, o, b, t):
                    if first:
                        tm[o] = cp("dve", ma[:, o, :], banks[b][:, 0:N], t)
                    else:
                        tm[o] = tt(ma[:, o, :], ma[:, o, :], banks[b][:, 0:N], ALU.add, t, tm[o])
                    return tm[o]

                ffn(NF2, "w_mlp_in_2", "w_mlp_out_2", tx, N, False, sink)
                post([(ma[:, o, :], tm[o]) for o in range(8)], x, tx_, N, V("g_mlp_post_2", l * 8), gt, t_gt)

        def pool_block(x, tx_, N, q, cnt):
            G, Sh, tg = scaled_gain(V("g_mix_pre_2"), 2, 0, 0, q)
            with ExitStack() as sc:
                P.barrier()
                hp = sb(sc, "hp", [128, KT, N + 16])
                t_z = P.op("dve", lambda g: g.memset(hp[:, :, 0:8], 0.0))
                t_z = P.op("dve", lambda g: g.memset(hp[:, :, N + 8:N + 16], 0.0))
                tn = normed(x, tx_, N, G, Sh, tg, keep=lambda i: hp[:, i, 8:N + 8])
                gt, t_gt = mod(2, 0, 2, q)
                P.barrier()
                cn = sb(sc, "cn", [128, 4, N])
                ym = sb(sc, "ym", [128, KT, N])
                t_cn = P.dma("sp", "cn", cn[:, :, :], cnt, P.everyone())
                s_ = [sb(sc, f"s{i}", [128, N + 16]) for i in range(2)]
                tx = [None] * 8
                prev = None
                for f in range(8):
                    g = f // 2
                    src, t, lo, hi = hp[:, f, :], [tn[f], t_z], 0, N + 16
                    for lev in range(g + 1):
                        a = 1 if lev == 0 else 2 ** (lev - 1)
                        b_ = 0 if lev == 0 else 2 ** (lev - 1)
                        lo, hi = lo + a, hi - b_
                        d = s_[lev % 2]
                        t = tt(d[:, lo:hi], src[:, lo - a:hi - a], src[:, lo + b_:hi + b_], ALU.add, t, prev)
                        src = d
                    o = s_[(g + 1) % 2]
                    t = tt(o[:, 8:N + 8], src[:, 8:N + 8], cn[:, g, :], ALU.mult, t, t_cn)
                    t = tt(ym[:, f, :], o[:, 8:N + 8], hp[:, f, 8:N + 8], ALU.subtract, t)
                    prev = t
                    tx[f] = halves(nH[:, f, 0:N], nL[:, f, 0:N], ym[:, f, :], t)
                k, hi, lo, tw = slot("w_pool_2")
                tm = [None] * 8
                for g in range(4):
                    res = groups(k, hi[:, 2 * g:2 * g + 2, :], lo[:, 2 * g:2 * g + 2, :], tw,
                                 lambda i: nH[:, 2 * g + i, 0:N], lambda i: nL[:, 2 * g + i, 0:N], tx[2 * g:2 * g + 2], N)
                    for i, (b, t) in enumerate(res):
                        f = 2 * g + i
                        tm[f] = act(ym[:, f, :], banks[b][:, 0:N], ACT.Copy, t, tx[f],
                                    scale=vec[:, VEC["pool_scale_2"] + f:VEC["pool_scale_2"] + f + 1])
                        bank_free[b] = tm[f]
                post([(ym[:, f, :], tm[f]) for f in range(8)], x, tx_, N, V("g_mix_post_2"), gt, t_gt)

        pool_block(htiles, th, S, 0, A["cnt"])
        mlp2(0, htiles, th, S, 0)
        pool_block(ctiles, tc, C, 1, A["cntc"])
        mlp2(0, ctiles, tc, C, 1)

        T = S + C
        G, Sh, tg = scaled_gain(V("g_mix_pre_2", 8), 2, 1, 0, 1)
        with ExitStack() as ph:
            P.barrier()
            KTt = sb(ph, "KTt", [128, 2, T])
            Vtk = sb(ph, "Vtk", [128, 6, 256])
            ps2 = ExitStack()
            tx = normed(ctiles, tc, C, G, Sh, tg)
            Q = sb(ph, "Q", [128, 8, S])
            tab = sb(ps2, "tab2", [128, 2, S])
            tmp = sb(ps2, "tmp2", [128, S])
            rot = sb(ps2, "rot2", [128, S])
            vT = sb(ps2, "vT", [128, S])
            qx = sb(ps2, "qx", [128, S])
            ssq = sb(ps2, "ssq", [128, S])
            sdg = sb(ps2, "sdg", [128, S])
            srs = sb(ps2, "srs", [128, 8])
            t_tab = P.dma("sp", "tab2", tab[:, :, :], A["rope2"], P.everyone())
            P.barrier()
            fr = {"vT": None, "x": None}

            def head_norm(b, t, N, dst, gain, roped):
                nt = N // 128
                t0 = act(qx[:, 0:N], banks[b][:, 0:N], ACT.Copy, t, fr["x"], scale=gain)
                t1 = act(ssq[:, 0:N], banks[b][:, 0:N], ACT.Square, t, fr["x"])
                bank_free[b] = [t0, t1]
                b1, free = take()
                for j in range(nt):
                    t = mm(banks[b1][:, j:j + 1], ssq[:, j * 128:j * 128 + 128], ones[:, 0:1], True, True, free, t1,
                           inc=(j == nt - 1))
                t = act(srs[:, 0:nt], banks[b1][:, 0:nt], ACT.Sqrt, t, bias=epsc[:, 0:1], scale=1.0 / 128)
                bank_free[b1] = t
                t = P.op("dve", lambda g: g.reciprocal(srs[:, 4:4 + nt], srs[:, 0:nt]), t)
                for j in range(nt):
                    td = ts(sdg[:, j * 128:j * 128 + 128], ident[:, :], srs[:, 4 + j:5 + j], None, ALU.mult, None, t)
                b2_, free = take()
                t = mm(banks[b2_][:, 0:N], ones[:, :], sdg[:, 0:N], True, True, free, td, inc=True)
                if not roped:
                    t = tt(dst, qx[:, 0:N], banks[b2_][:, 0:N], ALU.mult, t, t0)
                    bank_free[b2_] = t
                    fr["x"] = t
                    return t
                t = tt(qx[:, 0:N], qx[:, 0:N], banks[b2_][:, 0:N], ALU.mult, t, t0)
                bank_free[b2_] = t
                for q in range(4):
                    d0, s0 = 32 * q, 32 * (q ^ 1)
                    tr_ = cp("act", rot[d0:d0 + 32, 0:N], qx[s0:s0 + 32, 0:N], t)
                t1 = tt(tmp[:, 0:N], qx[:, 0:N], tab[:, 0, 0:N], ALU.mult, t, t_tab)
                t2 = tt(rot[:, 0:N], rot[:, 0:N], tab[:, 1, 0:N], ALU.mult, tr_, t_tab)
                t = tt(dst, tmp[:, 0:N], rot[:, 0:N], ALU.add, t1, t2)
                fr["x"] = t
                return t

            t_K, t_V = [], []

            def values(b, t, N, hd, base):
                tv = cp("act", vT[:, 0:N], banks[b][:, 0:N], t, fr["vT"])
                bank_free[b] = tv
                bt, free = take()
                for j in range(N // 128):
                    t = tr(banks[bt][:, j * 128:j * 128 + 128], vT[:, j * 128:j * 128 + 128], ident[:, :], free, tv,
                           inc=(j == N // 128 - 1))
                fr["vT"] = t
                t = cp("dve", Vtk[:, base:base + N // 128, hd * 128:hd * 128 + 128],
                       banks[bt][:, 0:N].rearrange("p (a b) -> p a b", b=128), t)
                bank_free[bt] = t
                t_V.append(t)

            gq, gk = V("g_q_2", 0, 1), V("g_k_2", 0, 1)
            for i, (b, t) in enumerate(groups(*slot("w_qkv_2"), nHk(C), nLk(C), tx, C)):
                t_K.append(head_norm(b, t, C, KTt[:, i, 0:C], gk, False))
            for i, (b, t) in enumerate(groups(*slot("w_qkv_2"), nHk(C), nLk(C), tx, C)):
                values(b, t, C, i, 0)
            G, Sh, tg = scaled_gain(V("g_mix_pre_2", 8), 2, 1, 0, 0)
            tx = normed(htiles, th, S, G, Sh, tg)
            t_Q = [None] * 8
            for m in range(4):
                for i, (b, t) in enumerate(groups(*slot("w_qkv_2"), nHk(S), nLk(S), tx, S)):
                    t_Q[2 * m + i] = head_norm(b, t, S, Q[:, 2 * m + i, :], gq, True)
            for i, (b, t) in enumerate(groups(*slot("w_qkv_2"), nHk(S), nLk(S), tx, S)):
                t_K.append(head_norm(b, t, S, KTt[:, i, C:T], gk, True))
            for i, (b, t) in enumerate(groups(*slot("w_qkv_2"), nHk(S), nLk(S), tx, S)):
                values(b, t, S, i, 2)
            ps2.close()
            P.barrier()
            Pb = [sb(ph, f"Pb{i}", [128, T]) for i in range(3)]
            PT = sb(ph, "PTb", [128, 2, T])
            yo = sb(ph, "yo2", [128, 2, S])
            st2 = sb(ph, "st2", [128, 4, 8])
            SC = 128 ** -0.5
            units = [(hh, qt) for hh in range(8) for qt in range(4)]
            sP, sT = {}, {}
            p_free, pt_free = {}, {}
            o_free = {6: bank_free[6], 7: bank_free[7]}
            t_o = [None] * 8
            yo_free = [None, None]

            def score2(u):
                hh, qt = units[u]
                kv = hh // 4
                i = u % 3
                m1, m2, mm_, s1, s2, rr = (st2[:, i, x:x + 1] for x in range(6))
                bk, tk = [], []
                for part, (c0, n) in enumerate(((0, 384), (384, 384))):
                    b, free = take()
                    t = mm(banks[b][:, 0:n], Q[:, hh, 128 * qt:128 * qt + 128], KTt[:, kv, c0:c0 + n], True, True,
                           free, t_K, t_Q[hh], inc=True)
                    bk.append(b)
                    tk.append(P.op("dve", lambda g, o=(m1, m2)[part], b=b, n=n: g.tensor_reduce(
                        o, banks[b][:, 0:n], AX, ALU.max), t, p_free.get(i)))
                t = tt(mm_, m1, m2, ALU.max, tk)
                t = ts(mm_, mm_, -SC, None, ALU.mult, None, t)
                ta = act(Pb[i][:, 0:384], banks[bk[0]][:, 0:384], ACT.Exp, t, bias=mm_, scale=SC, accum_out=s1)
                bank_free[bk[0]] = ta
                tb = act(Pb[i][:, 384:768], banks[bk[1]][:, 0:384], ACT.Exp, t, bias=mm_, scale=SC, accum_out=s2)
                bank_free[bk[1]] = tb
                t = tt(rr, s1, s2, ALU.add, ta, tb)
                t = P.op("dve", lambda g: g.reciprocal(rr, rr), t)
                t = ts(Pb[i][:, :], Pb[i][:, :], rr, None, ALU.mult, None, t, e="pool")
                sP[u] = t

            def turn2(u):
                i, j = u % 3, u % 2
                t = []
                for part in range(2):
                    b, free = take()
                    for x in range(3):
                        c = 3 * part + x
                        tp = tr(banks[b][:, 128 * x:128 * x + 128], Pb[i][:, 128 * c:128 * c + 128], ident[:, :],
                                free, sP[u], inc=(x == 2))
                    e = "act" if part else "dve"
                    tq = cp(e, PT[:, j, 384 * part:384 * part + 384], banks[b][:, 0:384], tp, pt_free.get(j))
                    bank_free[b] = tq
                    t.append(tq)
                p_free[i] = tp
                sT[u] = t

            def value2(u):
                hh, qt = units[u]
                kv, j, ob = hh // 4, u % 2, 6 + hh % 2
                for x in range(6):
                    tp = mm(banks[ob][:, 128 * qt:128 * qt + 128], Vtk[:, x, 128 * kv:128 * kv + 128],
                            PT[:, j, 128 * x:128 * x + 128], qt == 0 and x == 0, qt == 3 and x == 5, sT[u], t_V,
                            o_free[ob] if qt == 0 else None, skip_group_check=True, inc=(x == 5))
                pt_free[j] = tp
                if qt == 3:
                    i = hh % 2
                    t = cp("act", yo[:, i, :], banks[ob][:, :], tp, yo_free[i])
                    o_free[ob] = t
                    t_o[hh] = halves(nH[:, hh, :], nL[:, hh, :], yo[:, i, :], t)
                    yo_free[i] = t_o[hh]

            U = len(units)
            for u in range(U + 2):
                if u < U:
                    score2(u)
                if 1 <= u < U + 1:
                    turn2(u - 1)
                if u >= 2:
                    value2(u - 2)
            bank_free[6], bank_free[7] = o_free[6], o_free[7]
        gt, t_gt = mod(2, 1, 2)
        with ExitStack() as sc:
            P.barrier()
            ym = sb(sc, "ym1", [128, KT, S])
            tm = [None] * 8
            for m in range(4):
                for i, (b, t) in enumerate(groups(*slot("w_o_2"), nHk(S), nLk(S), t_o, S)):
                    tm[2 * m + i] = cp("act", ym[:, 2 * m + i, :], banks[b][:, :], t)
                    bank_free[b] = tm[2 * m + i]
            post([(ym[:, f, :], tm[f]) for f in range(8)], htiles, th, S, V("g_mix_post_2", 8), gt, t_gt)
        mlp2(1, htiles, th, S, 0)
        b2.close()
        t_end = [P.dma("sp", f"out{i}", out[:, i, :], h[:, i, :], th[i]) for i in range(8)]
        P.wait("sp", t_end)
        assert st["used"] == len(slots), (st, len(slots))

        block = ctx.enter_context(nc.Block())
        P.emit(block)


def tables():
    f = np.float32
    c = {}
    c["ident"] = np.eye(128, dtype=f)
    inv = (1.0 / (f(10000.0) ** (np.arange(0, 64, 2, dtype=f) / f(64)))).astype(f)
    p = np.arange(128)
    sign = np.where((p % 64) < 32, -1.0, 1.0).astype(f)[:, None]

    def rope(pos):
        ang = (pos.astype(f)[None, :] * inv[p % 32][:, None]).astype(f)
        return np.cos(ang).astype(f), (np.sin(ang).astype(f) * sign).astype(f)

    co, si = rope(np.arange(S))
    c["rope1"] = np.stack([co * f(0.125), si * f(0.125), co, si], 1).reshape(128, 4, S).astype(f)
    ce = np.arange(31) * 16 + 31
    cc, cs_ = rope(np.concatenate([ce, ce[-1:]]))
    c["crope"] = np.stack([cc, cs_], 1).astype(f)
    inv2 = np.power(f(10000.0), -np.arange(0, 64, 2, dtype=f) / f(64)).astype(f)
    t = np.arange(S)
    pos = np.where(p[:, None] < 64, (t // 64)[None, :], (t % 64)[None, :]).astype(f)
    ang = (pos * inv2[p % 32][:, None]).astype(f)
    c["rope2"] = np.stack([np.cos(ang).astype(f), np.sin(ang).astype(f) * sign], 1).astype(f)
    q, k = np.arange(128)[:, None], np.arange(128)[None, :]
    c["negm"] = np.where(k <= q, 0.0, -1e30).astype(f)
    c["msk"] = (k >= q).astype(f)
    n = np.arange(32)
    cn = np.full((128, 4, 32), -1e30, f)
    for qt in range(4):
        ok = (n[None, :] < 31) & (16 * n[None, :] + 31 <= np.arange(128)[:, None] + 128 * qt)
        cn[:, qt][ok] = 0.0
    c["cneg"] = cn.reshape(128, 128)
    row = np.ones((128, 4), f)
    row[:31, 0] = 0.0
    c["rowok"] = row
    for name, L in (("cnt", S), ("cntc", C)):
        t = np.arange(L)
        o = np.zeros((4, L), f)
        for g, w in enumerate((2, 4, 8, 16)):
            o[g] = f(1.0) / (np.clip(t + w - w // 2, 0, L) - np.clip(t - w // 2, 0, L)).astype(f)
        c[name] = np.ascontiguousarray(np.broadcast_to(o[None], (128, 4, L)))
    return c


_IN = {"ident": (128, 128), "rope1": (128, 4, S), "crope": (128, 2, 32), "rope2": (128, 2, S), "msk": (128, 128),
       "rowok": (128, 4), "cnt": (128, 4, S), "cntc": (128, 4, C)}


def kernel(**inputs):
    import ml_dtypes as _ml
    import concourse.bacc as _bacc
    from concourse import mybir as _mybir
    from concourse.bass_utils import run_bass_kernel_spmd as _run

    I = {k: np.asarray(v) for k, v in inputs.items()}
    arrays = {}
    cst = tables()
    for n in _IN:
        arrays[n] = cst[n]
    for n in ("negm", "cneg"):
        arrays[n] = cst[n].astype(_ml.bfloat16)
    arrays["idb"] = np.eye(128).astype(_ml.bfloat16)

    def fm(a):
        r, n = a.shape
        return np.ascontiguousarray(a.T.reshape(n // 128, 128, r).transpose(1, 0, 2))

    arrays["xT"] = fm(I["x"][0])
    arrays["ctxT"] = fm(I["ctx_2"][0])
    parts = []
    for a, idx, r0, nk, c0, n in plan():
        w = I[a][idx]
        if a == "cmp_w1":
            b = w.reshape(2, 16, 64, 128).transpose(0, 2, 1, 3)
        elif a == "w_pool_2":
            b = w.reshape(8, 128, 256).transpose(1, 0, 2)
        else:
            b = w[r0:r0 + nk * 128, c0:c0 + n].reshape(nk, 128, n).transpose(1, 0, 2)
        parts.append(b.reshape(-1))
    arrays["wst"] = np.concatenate(parts)
    parts = []
    for b_, l, m, _, _ in ada_plan():
        w = I["ada_w" if b_ == 1 else "w_ada_2"][l][:, m * 1024:(m + 1) * 1024]
        parts.append(w.reshape(8, 128, 1024))
    arrays["ast"] = np.concatenate(parts)
    lay, nv = vec_layout()
    arrays["vec"] = np.ascontiguousarray(np.concatenate([I[n].reshape(-1) for n in lay]).reshape(nv, 128).T)
    arrays["pe"] = np.ascontiguousarray(I["cmp_pe"].reshape(2, 2, 2, 16, 64).transpose(0, 2, 4, 1, 3).reshape(2, 128, 2, 16))
    w2 = I["cmp_w2"]
    arrays["w2"] = np.ascontiguousarray(np.concatenate([w2[:, 0], w2[:, 0], w2[:, 1]], axis=2))
    arrays["wsT"] = np.ascontiguousarray(I["gm_ws"].transpose(0, 3, 1, 2))
    bs = I["gm_bs"].reshape(2, 4, 2, 1, 128)
    arrays["bsb"] = np.ascontiguousarray(np.broadcast_to(bs, (2, 4, 2, 64, 128)).reshape(2, 4, 128, 128).transpose(0, 2, 1, 3))
    ln = np.stack([I["gm_ln_g"], I["gm_ln_b"]], 1)[:, None]
    arrays["lnp"] = np.ascontiguousarray(np.broadcast_to(ln, (2, 128, 2, 512)))

    nc = _bacc.Bacc("TRN2", target_bir_lowering=False, num_devices=1, dynamic_dma_scratch_size=1024)
    A = {}
    for n, a in arrays.items():
        A[n] = nc.dram_tensor(f"in_{n}", a.shape, _mybir.dt.from_np(a.dtype), kind="ExternalInput").ap()
    out = nc.dram_tensor("out_0", (128, 8, S), F32, kind="ExternalOutput").ap()
    build(nc, A, out)
    r = _run(nc, [{f"in_{n}": a for n, a in arrays.items()}], core_ids=[0])
    got = r.results[0]["out_0"]
    return np.ascontiguousarray(got.transpose(2, 1, 0).reshape(1, S, D))
```

```python
from contextlib import ExitStack

import numpy as np
import concourse.bass as bass
from concourse import mybir

F32 = mybir.dt.float32
F32R = mybir.dt.float32r
BF16 = mybir.dt.bfloat16
ALU = mybir.AluOpType
ACT = mybir.ActivationFunctionType
AX = mybir.AxisListType.X

D = 1024
KT = 8
S = 512
C = 256
NF = 22
NF2 = 32
EPS = 1e-6
ENGINES = ("pe", "act", "dve", "pool", "sp")


def ffn_chunks(nf):
    out, at = [], 0
    while at < nf:
        out.append((at, min(4, nf - at)))
        at += 4
    return out


def plan():
    out = []

    def cols(a, idx, r0, nk, c0, n, w):
        for c in range(c0, c0 + n, w):
            out.append((a, idx, r0, nk, c, min(w, c0 + n - c)))

    def ffn1(l, j):
        cs = ffn_chunks(NF)
        for i, (f0, nf) in enumerate(cs):
            for p in range(0, nf, 2):
                out.append(("ffn_w_in", (l, j), 0, KT, (f0 + p) * 128, 256))
                out.append(("ffn_w_in", (l, j), 0, KT, (NF + f0 + p) * 128, 256))
            for g0, ng in ([cs[i - 1]] if i else []) + ([(f0, nf)] if i == len(cs) - 1 else []):
                cols("ffn_w_out", (l, j), g0 * 128, ng, 0, D, 2048 // ng)

    def ffn2(l):
        cs = ffn_chunks(NF2)
        for i, (f0, nf) in enumerate(cs):
            cols("w_mlp_in_2", (l,), 0, KT, f0 * 128, nf * 128, 256)
            for g0, ng in ([cs[i - 1]] if i else []) + ([(f0, nf)] if i == len(cs) - 1 else []):
                cols("w_mlp_out_2", (l,), g0 * 128, ng, 0, D, 2048 // ng)

    for l in range(2):
        ffn1(l, 0)
        cols("mix_w_in", (l,), 0, KT, 512, 512, 256)
        out.append(("cmp_w1", (l, 0), 0, 16, 0, 128))
        cols("mix_w_in", (l,), 0, KT, 1024, 256, 256)
        out.append(("cmp_w1", (l, 1), 0, 16, 0, 128))
        cols("mix_w_in", (l,), 0, KT, 0, 512, 256)
        out.append(("mix_w_in", (l,), 0, KT, 1280, 24))
        cols("mix_w_in", (l,), 0, KT, 1304, 1024, 256)
        for m in range(4):
            out.append(("mix_w_in", (l,), 0, KT, 2328 + 256 * m, 256))
            out.append(("proj_a", (l,), 0, 4, 256 * m, 256))
            out.append(("mix_w_in", (l,), 0, KT, 3352 + 256 * m, 256))
            out.append(("proj_b", (l,), 0, 4, 256 * m, 256))
        cols("w_out", (l,), 0, KT, 0, D, 256)
        ffn1(l, 1)
    out.append(("w_pool_2", (0,), 0, 8, 0, 256))
    ffn2(0)
    out.append(("w_pool_2", (0,), 0, 8, 0, 256))
    ffn2(0)
    cols("w_qkv_2", (0,), 0, KT, 1024, 512, 256)
    cols("w_qkv_2", (0,), 0, KT, 1024, 256, 256)
    cols("w_qkv_2", (0,), 0, KT, 0, 1024, 256)
    cols("w_qkv_2", (0,), 0, KT, 1280, 256, 256)
    cols("w_o_2", (0,), 0, KT, 0, D, 256)
    ffn2(1)
    return out


def ada_plan():
    out = [(1, l, m, True, False) for l in range(2) for m in range(9)]
    out += [(2, 0, m, True, True) for m in range(6)]
    out += [(2, 1, m, True, m < 2) for m in range(6)]
    return out


VEC = {}


def vec_layout():
    at, out = 0, {}
    for name, n in (("norm_g", 48), ("ada_b", 144), ("final_g", 8), ("b_ada_2", 96), ("g_mix_pre_2", 16),
                    ("g_mix_post_2", 16), ("g_mlp_pre_2", 16), ("g_mlp_post_2", 16), ("pool_scale_2", 8),
                    ("g_q_2", 1), ("g_k_2", 1), ("c", 8), ("c_2", 8), ("c_ctx_2", 8)):
        out[name] = at
        at += n
    return out, at


class Program:

    def __init__(self, nc, ctx):
        self.nc, self.ctx = nc, ctx
        self.queue = {e: [] for e in ENGINES}
        self.count = {e: 0 for e in ENGINES}
        self.sem = {e: ctx.enter_context(nc.semaphore("s_" + e)) for e in ENGINES}
        self.seen = {e: {} for e in ENGINES}
        self.dma_sems = {}
        self.n = 0

    def wait(self, e, *tokens):
        for t in tokens:
            if t is None:
                continue
            if isinstance(t, list):
                self.wait(e, *t)
                continue
            key, sem, val = t
            if self.seen[e].get(key, 0) < val:
                self.seen[e][key] = val
                self.queue[e].append(lambda g, sem=sem, val=val: g.wait_ge(sem, val))

    def op(self, e, fn, *tokens):
        self.wait(e, *tokens)
        self.count[e] += 1
        self.queue[e].append(lambda g, fn=fn, s=self.sem[e]: fn(g).then_inc(s, 1))
        return (e, self.sem[e], self.count[e])

    def quiet(self, e, fn, *tokens):
        self.wait(e, *tokens)
        self.queue[e].append(fn)

    def last(self, e):
        return (e, self.sem[e], self.count[e]) if self.count[e] else None

    def dma(self, e, name, out, in_, *tokens):
        self.wait(e, *tokens)
        if name not in self.dma_sems:
            self.dma_sems[name] = [self.ctx.enter_context(self.nc.semaphore("d_" + name)), 0]
        d = self.dma_sems[name]
        d[1] += 16
        self.queue[e].append(lambda g, s=d[0]: g.dma_start(out, in_).then_inc(s, 16))
        return ("d_" + name, d[0], d[1])

    def everyone(self):
        return [self.last(e) for e in ("pe", "act", "dve", "pool")]

    def barrier(self):
        now = self.everyone()
        for e in ("act", "dve", "pool", "sp"):
            self.wait(e, now)

    def emit(self, block):
        def run(e):
            def body(g):
                for f in self.queue[e]:
                    f(g)
            return body
        block.tensor(run("pe"))
        block.scalar(run("act"))
        block.vector(run("dve"))
        block.gpsimd(run("pool"))
        block.sync(run("sp"))


def build(nc, A, out):
    ctx = ExitStack()
    P = Program(nc, ctx)
    slots = plan()
    adas = ada_plan()
    VEC, NV = vec_layout()
    names = [0]

    def sb(scope, name, shape, dt=F32):
        names[0] += 1
        return scope.enter_context(nc.sbuf_tensor(f"{name}_{names[0]}", shape, dt))

    with ctx:
        h = sb(ctx, "h", [128, KT, S])
        nH = sb(ctx, "nH", [128, KT, S], F32R)
        nL = sb(ctx, "nL", [128, KT, S], F32R)
        NR, NW, NA = 2, 4, 2
        raw = [sb(ctx, f"raw{i}", [128, 2048]) for i in range(NR)]
        WH = [sb(ctx, f"WH{i}", [128, 2048], F32R) for i in range(NW)]
        WL = [sb(ctx, f"WL{i}", [128, 2048], F32R) for i in range(NW)]
        araw = [sb(ctx, f"araw{i}", [128, 1024]) for i in range(NA)]
        aacc = [sb(ctx, f"aacc{i}", [128, 1024]) for i in range(2)]
        vec = sb(ctx, "vec", [128, NV])
        cs = sb(ctx, "cs", [128, 24])
        mods = sb(ctx, "mods", [128, 38 * 8])
        der = sb(ctx, "der", [128, 2, 32])
        ident = sb(ctx, "ident", [128, 128])
        ones = sb(ctx, "ones", [128, 128])
        epsc = sb(ctx, "epsc", [128, 1])
        scr = [sb(ctx, f"scr{i}", [128, S]) for i in range(4)]
        dummy = sb(ctx, "dummy", [128, 1])
        negm = sb(ctx, "negm", [128, 128], BF16)
        idb = sb(ctx, "idb", [128, 128], BF16)
        cneg = sb(ctx, "cneg", [128, 128], BF16)
        rowok = sb(ctx, "rowok", [128, 4])
        ctab = sb(ctx, "ctab", [128, 2, 32])
        msk = sb(ctx, "msk", [128, 128])
        banks = [ctx.enter_context(nc.psum_tensor(f"ps{i}", [128, 512], F32)) for i in range(8)]

        class Banks(dict):

            def __init__(self):
                super().__init__({b: None for b in range(8)})
                self.order = list(range(6))

            def __setitem__(self, b, token):
                super().__setitem__(b, token)
                if b < 6:
                    if b in self.order:
                        self.order.remove(b)
                    self.order.append(b)

        bank_free = Banks()

        def take():
            b = bank_free.order.pop(0)
            return b, bank_free[b]

        def mm(out_, lhsT, rhs, start, stop, *tokens, inc=False, **kw):
            f = lambda g: g.matmul(out_, lhsT, rhs, start=start, stop=stop, **kw)
            if inc:
                return P.op("pe", f, *tokens)
            P.quiet("pe", f, *tokens)

        def tr(out_, in_, idn, *tokens, inc=False):
            f = lambda g: g.transpose(out_, in_, idn)
            if inc:
                return P.op("pe", f, *tokens)
            P.quiet("pe", f, *tokens)

        def act(out_, in_, func, *tokens, **kw):
            return P.op("act", lambda g: g.activation(out_, in_, func, **kw), *tokens)

        def tt(out_, a, b, op, *tokens, e="dve"):
            return P.op(e, lambda g: g.tensor_tensor(out_, a, b, op), *tokens)

        def ts(out_, a, s1, s2, op0, op1, *tokens, e="dve"):
            if s2 is None:
                return P.op(e, lambda g: g.tensor_scalar(out_, a, s1, None, op0), *tokens)
            return P.op(e, lambda g: g.tensor_scalar(out_, a, s1, s2, op0, op1), *tokens)

        def stt(out_, a, s, b, op0, op1, *tokens):
            return P.op("dve", lambda g: g.scalar_tensor_tensor(out=out_, in0=a, scalar=s, in1=b, op0=op0, op1=op1),
                        *tokens)

        def cp(e, out_, in_, *tokens):
            if e == "act":
                return act(out_, in_, ACT.Copy, *tokens)
            return P.op(e, lambda g: g.tensor_copy(out_, in_), *tokens)

        t_vec = P.dma("sp", "vec", vec[:, :], A["vec"])
        t_id = P.dma("sp", "ident", ident[:, :], A["ident"])
        t_h = P.dma("sp", "h", h[:, :, :], A["xT"])
        t_ones = P.op("dve", lambda g: g.memset(ones[:, :], 1.0))
        t_eps = P.op("dve", lambda g: g.memset(epsc[:, :], EPS))
        t_cs = act(cs[:, :], vec[:, VEC["c"]:VEC["c"] + 24], ACT.Silu, t_vec)
        for e in ("pe", "act", "dve", "pool"):
            P.wait(e, t_vec, t_id, t_ones, t_eps, t_cs)
        t_const = [P.dma("sp", nm, tl, A[nm]) for nm, tl in (
            ("negm", negm[:, :]), ("idb", idb[:, :]), ("cneg", cneg[:, :]), ("rowok", rowok[:, :]),
            ("crope", ctab[:, :, :]), ("msk", msk[:, :]))]

        def V(name, i=0, n=8):
            return vec[:, VEC[name] + i:VEC[name] + i + n]

        offs, at = [], 0
        for s in slots:
            offs.append(at)
            at += 128 * s[3] * s[5]
        W = A["wst"]
        st = dict(loaded=0, split=0, used=0)
        t_raw = [None] * len(slots)
        t_hi = [None] * len(slots)
        t_lo = [None] * len(slots)
        t_use = [None] * len(slots)

        def load(k):
            n = slots[k][3] * slots[k][5]
            src = W[offs[k]:offs[k] + 128 * n].rearrange("(p n) -> p n", p=128)
            free = [t_hi[k - NR], t_lo[k - NR]] if k >= NR else None
            t_raw[k] = P.dma("sp", f"raw{k % NR}", raw[k % NR][:, 0:n], src, free)

        def split(k):
            n = slots[k][3] * slots[k][5]
            free = t_use[k - NW] if k >= NW else None
            r, a, b = raw[k % NR], WH[k % NW], WL[k % NW]
            t_hi[k] = act(a[:, 0:n], r[:, 0:n], ACT.Copy, t_raw[k], free)
            t_lo[k] = tt(b[:, 0:n], r[:, 0:n], a[:, 0:n].bitcast(F32), ALU.subtract, t_raw[k], free, t_hi[k])

        def advance():
            done_ = next((i for i in range(st["used"] + 1) if i == st["used"] or t_use[i] is None))
            while st["split"] < min(done_ + NW, len(slots)):
                while st["loaded"] < min(st["split"] + NR, len(slots)):
                    if st["loaded"] >= NR and t_lo[st["loaded"] - NR] is None:
                        break
                    load(st["loaded"])
                    st["loaded"] += 1
                split(st["split"])
                st["split"] += 1
            while st["loaded"] < min(st["split"] + NR, len(slots)):
                load(st["loaded"])
                st["loaded"] += 1

        def slot(want):
            k = st["used"]
            assert slots[k][0] == want, (slots[k], want)
            advance()
            st["used"] += 1
            ada_step()
            _, _, _, nk, _, nc_ = slots[k]
            hi = WH[k % NW][:, 0:nk * nc_].rearrange("p (k c) -> p k c", k=nk)
            lo = WL[k % NW][:, 0:nk * nc_].rearrange("p (k c) -> p k c", k=nk)
            return k, hi, lo, [t_hi[k], t_lo[k]]

        def done(k, tok):
            t_use[k] = tok

        mod_col, c_ = {}, 0
        for b_, l_, m_, a1, a2 in adas:
            mod_col[(b_, l_, m_, 0)] = c_
            c_ += 8
            if a2:
                mod_col[(b_, l_, m_, 1)] = c_
                c_ += 8
        assert c_ <= 38 * 8
        ad = dict(step=0, loaded=0, red=[], pend=[])
        t_araw, t_aread, t_acc = {}, {}, [None, None]
        t_red = [None, None]
        acc_i = [0]
        t_mod = {}
        cur = {}

        def ada_load(j):
            t_araw[j] = P.dma("sp", f"araw{j % NA}", araw[j % NA][:, :], A["ast"][j], t_aread.get(j - NA))

        def ada_flush():
            for b, psb, t_pe, m, bias in ad["pend"]:
                t = tt(mods[:, m:m + 8], banks[b][:, 0:8], bias, ALU.add, t_pe)
                bank_free[b] = t
                t_mod[m] = t
            ad["pend"] = []

        def ada_step():
            j = ad["step"]
            if j >= 8 * len(adas):
                if not ad["red"]:
                    ada_flush()
                ada_reduce()
                return
            while ad["loaded"] < min(8 * len(adas), j + NA):
                ada_load(ad["loaded"])
                ad["loaded"] += 1
            b_, l_, m_, a1, a2 = adas[j // 8]
            kt = j % 8
            if kt == (0 if len(ad["red"]) > 1 or a2 else 1):
                ada_reduce()
            if kt == 3:
                ada_flush()
            w = araw[j % NA]
            kinds = [0, 1] if a2 else [0]
            for q in kinds:
                if kt == 0:
                    cur[q] = acc_i[0]
                    acc_i[0] = (acc_i[0] + 1) % 2
                a = cur[q]
                col = (0 if b_ == 1 else 8 + 8 * q) + kt
                if kt == 0:
                    t = ts(aacc[a][:, :], w[:, :], cs[:, col:col + 1], None, ALU.mult, None, t_araw[j], t_red[a])
                else:
                    t = stt(aacc[a][:, :], w[:, :], cs[:, col:col + 1], aacc[a][:, :], ALU.mult, ALU.add,
                            t_araw[j], t_acc[a])
                t_acc[a] = t
            t_aread[j] = t
            ad["step"] += 1
            if kt == 7:
                ad["red"] = [(cur[q], b_, l_, m_, q) for q in kinds]

        def ada_reduce():
            for a, b_, l_, m_, q in ad["red"]:
                b, free = take()
                for f in range(8):
                    t_pe = mm(banks[b][:, f:f + 1], aacc[a][:, f * 128:f * 128 + 128], ones[:, 0:1], True, True,
                              free, t_acc[a], inc=(f == 7))
                t_red[a] = t_pe
                bias = V("ada_b", l_ * 72 + m_ * 8) if b_ == 1 else V("b_ada_2", l_ * 48 + m_ * 8)
                ad["pend"].append((b, None, t_pe, mod_col[(b_, l_, m_, q)], bias))
            ad["red"] = []

        def mod(b_, l_, m_, q=0):
            m = mod_col[(b_, l_, m_, q)]
            while m not in t_mod:
                if any(mod_col[r[1:]] == m for r in ad["red"]):
                    ada_reduce()
                elif any(p[3] == m for p in ad["pend"]):
                    ada_flush()
                else:
                    ada_step()
            return mods[:, m:m + 8], t_mod[m]

        der_i = [0]
        der_read = [None, None]

        def scaled_gain(g, b_, l_, m_, q=0):
            sh, t1 = mod(b_, l_, m_, q)
            sc, t2 = mod(b_, l_, m_ + 1, q)
            i = der_i[0]
            der_i[0] = 1 - i
            G = der[:, i, 0:8]
            t = stt(G, sc, 1.0, g, ALU.add, ALU.mult, t1, t2, P.last("act"), P.last("dve"), P.last("pool"))
            return G, sh, [t, t1]

        rs = sb(ctx, "rs", [128, 8])

        def rstd(tiles, toks, N, dim):
            sq, ssum, dg = [scr[0][:, 0:N], scr[1][:, 0:N]], scr[2][:, 0:N], scr[3][:, 0:N]
            act(dummy[:, :], epsc[:, :], ACT.Sqrt, P.last("act"))
            before = P.last("dve")
            t_add = [None] * len(tiles)
            for i, (x, tk) in enumerate(zip(tiles, toks)):
                t = act(sq[i % 2], x, ACT.Square, tk, t_add[i - 2] if i >= 2 else None)
                if i == 0:
                    t_first = t
                    t_add[0] = t
                elif i == 1:
                    t_add[0] = t_add[1] = tt(ssum, sq[0], sq[1], ALU.add, t_first, t, before)
                else:
                    t_add[i] = tt(ssum, ssum, sq[i % 2], ALU.add, t, t_add[i - 1])
            t_sum = t_add[-1]
            nt = N // 128
            b, free = take()
            for j in range(nt):
                t = mm(banks[b][:, j:j + 1], ssum[:, j * 128:j * 128 + 128], ones[:, 0:1], True, True,
                       free, t_sum, inc=(j == nt - 1))
            s = rs
            t = act(s[:, 0:nt], banks[b][:, 0:nt], ACT.Sqrt, t, bias=epsc[:, 0:1], scale=1.0 / dim)
            bank_free[b] = t
            t = P.op("dve", lambda g: g.reciprocal(s[:, 4:4 + nt], s[:, 0:nt]), t)
            for j in range(nt):
                td = ts(dg[:, j * 128:j * 128 + 128], ident[:, :], s[:, 4 + j:5 + j], None, ALU.mult, None, t)
            b, free = take()
            t = mm(banks[b][:, 0:N], ones[:, :], dg[:, :], True, True, free, td, inc=True)
            return b, t

        def halves(dH, dL, y, tok, free=None):
            t1 = act(dH, y, ACT.Copy, tok, free)
            t2 = tt(dL, y, dH.bitcast(F32), ALU.subtract, tok, t1, free)
            return [t1, t2]

        def normed(tiles, toks, N, G, Sh, t_gs, keep=None):
            outs = []
            if True:
                b, t_r = rstd(tiles, toks, N, D)
                t_ = [scr[i][:, 0:N] for i in range(2)]
                y_ = [scr[2 + i][:, 0:N] for i in range(2)]
                ty = [None] * len(tiles)
                tl = [None] * len(tiles)
                th = [None] * len(tiles)
                for i, x in enumerate(tiles):
                    t, y = t_[i % 2], y_[i % 2]
                    fr = [ty[i - 2], th[i - 2]] if i >= 2 else None
                    t1 = tt(t[:, :], x, banks[b][:, 0:N], ALU.mult, t_r, toks[i], fr)
                    if i == len(tiles) - 1:
                        bank_free[b] = t1
                    sh = Sh[:, i:i + 1] if Sh is not None else None
                    if keep is not None:
                        if sh is None:
                            ty[i] = th[i] = ts(keep(i), t[:, :], G[:, i:i + 1], None, ALU.mult, None, t1, t_gs)
                        else:
                            ty[i] = th[i] = act(keep(i), t[:, :], ACT.Identity, t1, t_gs, scale=G[:, i:i + 1], bias=sh)
                        outs.append(ty[i])
                        continue
                    th[i] = act(nH[:, i, 0:N], t[:, :], ACT.Identity, t1, t_gs, scale=G[:, i:i + 1], bias=sh)
                    ty[i] = ts(y[:, :], t[:, :], G[:, i:i + 1], sh, ALU.mult, ALU.add, t1, t_gs,
                               tl[i - 2] if i >= 2 else None, e="pool")
                    tl[i] = tt(nL[:, i, 0:N], y[:, :], nH[:, i, 0:N].bitcast(F32), ALU.subtract, ty[i], th[i])
                    outs.append([th[i], tl[i]])
            return outs

        def groups(k, hi, lo, tw, xH, xL, tx, N, each=None):
            nk = hi.shape[1]
            res = []
            for c in range(hi.shape[2] // 128):
                b, free = take()
                cc = slice(c * 128, c * 128 + 128)
                for i in range(nk):
                    for n, (w, x) in enumerate(((hi, xH), (hi, xL), (lo, xH))):
                        t = mm(banks[b][:, 0:N], w[:, i, cc], x(i), i == 0 and n == 0, i == nk - 1 and n == 2,
                               free, tw, tx[i], inc=(i == nk - 1 and n == 2))
                res.append((b, t))
                if c == hi.shape[2] // 128 - 1:
                    done(k, t)
                if each:
                    each(c, b, t)
            return res

        def wide(sl, xH, xL, tx, N):
            cols, res = [], []
            for (k, hi, lo, tw) in sl:
                for c in range(hi.shape[2] // 128):
                    b, free = take()
                    cols.append((b, free, k, hi, lo, tw, slice(c * 128, c * 128 + 128)))
            nk = sl[0][1].shape[1]
            toks = {}
            for i in range(nk):
                for b, free, k, hi, lo, tw, cc in cols:
                    for n, (w, x) in enumerate(((hi, xH), (hi, xL), (lo, xH))):
                        t = mm(banks[b][:, 0:N], w[:, i, cc], x(i), i == 0 and n == 0, i == nk - 1 and n == 2,
                               free, tw, tx[i], inc=(i == nk - 1 and n == 2), skip_group_check=True)
                    toks[b] = t
            for b, free, k, *_ in cols:
                res.append((b, toks[b]))
                done(k, toks[b])
            return res

        nHk = lambda N: (lambda i: nH[:, i, 0:N])
        nLk = lambda N: (lambda i: nL[:, i, 0:N])

        def ffn(nf, w_in, w_out, tx, N, gated, sink):
            with ExitStack() as sc:
                hH = sb(sc, "hH", [128, 2, 4, N], F32R)
                hL = sb(sc, "hL", [128, 2, 4, N], F32R)
                a_ = [scr[i][:, 0:N] for i in range(2)]
                y_ = [scr[2 + i][:, 0:N] for i in range(2)]
                chunks = ffn_chunks(nf)
                t_hid = {}
                t_out = {}
                rd = [None, None]
                ra = [None, None]
                n_ = [0]

                def hidden(ci):
                    f0, cn = chunks[ci]
                    free_h = t_out.get(ci - 2)
                    for p in range(0, cn, 2):
                        ta, us = {}, {}

                        def first(i, b, t):
                            u = us[i] = n_[0] % 2
                            n_[0] += 1
                            ta[i] = act(a_[u][:, :], banks[b][:, 0:N], ACT.Silu if gated else ACT.Relu, t, ra[u])
                            bank_free[b] = ta[i]
                            if not gated:
                                finish(i, tt(y_[u][:, :], a_[u][:, :], a_[u][:, :], ALU.mult, ta[i], rd[u]))

                        def second(i, b, t):
                            u = us[i]
                            ty = tt(y_[u][:, :], a_[u][:, :], banks[b][:, 0:N], ALU.mult, ta[i], t, rd[u])
                            bank_free[b] = ty
                            finish(i, ty)

                        def finish(i, ty):
                            u = us[i]
                            ra[u] = ty
                            rd[u] = halves(hH[:, ci % 2, p + i, :], hL[:, ci % 2, p + i, :], y_[u][:, :], ty, free_h)
                            t_hid[(ci, p + i)] = rd[u]

                        if ci == 0 and p == 0:
                            res = wide([slot(w_in) for _ in range(2 if gated else 1)], nHk(N), nLk(N), tx, N)
                            for i in range(2):
                                first(i, *res[i])
                            for i in range(2 if gated else 0):
                                second(i, *res[2 + i])
                        else:
                            groups(*slot(w_in), nHk(N), nLk(N), tx, N, first)
                            if gated:
                                groups(*slot(w_in), nHk(N), nLk(N), tx, N, second)

                def outp(ci):
                    f0, cn = chunks[ci]
                    tx_ = [t_hid[(ci, f)] for f in range(cn)]
                    o = 0
                    while o < 8:
                        q = slot(w_out)

                        def each(c, b, t):
                            bank_free[b] = sink(ci == 0, o + c, b, t)

                        res = groups(*q, lambda i: hH[:, ci % 2, i, :], lambda i: hL[:, ci % 2, i, :], tx_, N, each)
                        o += len(res)
                    t_out[ci] = res[-1][1]

                for ci in range(len(chunks)):
                    hidden(ci)
                    if ci:
                        outp(ci - 1)
                outp(len(chunks) - 1)

        th = [t_h] * 8
        htiles = [h[:, i, :] for i in range(8)]

        def add_to_h(gate_of):
            got = []

            def sink(first, o, b, t):
                if not got:
                    got.extend(gate_of())
                gate, t_g = got
                th[o] = stt(h[:, o, :], banks[b][:, :], gate[:, o:o + 1], h[:, o, :], ALU.mult, ALU.add, t, t_g, th[o])
                return th[o]
            return sink

        def ffn_block1(l, j):
            G, Sh, tg = scaled_gain(V("norm_g", (l * 3 + 2 * j) * 8), 1, l, 6 * j)
            tx = normed(htiles, th, S, G, Sh, tg)

            def half_gate():
                g, t_g = mod(1, l, 6 * j + 2)
                gh = der[:, j, 16:24]
                return gh, ts(gh, g, 0.5, None, ALU.mult, None, t_g, P.last("dve"))

            ffn(NF, "ffn_w_in", "ffn_w_out", tx, S, True, add_to_h(half_gate))

        def rope(b, t, N, cosT, sinT, dst, tmp, rot, t_tab, frees):
            for q in range(4):
                d0, s0 = 32 * q, 32 * (q ^ 1)
                tr_ = act(rot[d0:d0 + 32, 0:N], banks[b][s0:s0 + 32, 0:N], ACT.Copy, t, frees)
            t1 = tt(tmp[:, 0:N], banks[b][:, 0:N], cosT, ALU.mult, t, t_tab, frees, tr_)
            bank_free[b] = t1
            t2 = tt(rot[:, 0:N], rot[:, 0:N], sinT, ALU.mult, tr_, t_tab)
            return tt(dst, tmp[:, 0:N], rot[:, 0:N], ALU.add, t1, t2)

        def mixer(l):
            G, Sh, tg = scaled_gain(V("norm_g", (l * 3 + 1) * 8), 1, l, 3)
            fence = P.everyone()
            tx = normed(htiles, th, S, G, Sh, tg)
            ph = ExitStack()
            yaH = sb(ph, "yaH", [128, 4, S], F32R)
            yaL = sb(ph, "yaL", [128, 4, S], F32R)
            t_ya = attention1(l, tx, yaH, yaL, fence)
            P.barrier()
            ybH = sb(ph, "ybH", [128, 4, S], F32R)
            ybL = sb(ph, "ybL", [128, 4, S], F32R)
            t_yb = gmlp(l, tx, ybH, ybL)
            with ExitStack() as sc:
                P.barrier()
                mH = sb(sc, "mH", [128, 8, S], F32R)
                mL = sb(sc, "mL", [128, 8, S], F32R)
                sg = [scr[0]] * 2
                t_m = [None] * 8
                mt = [scr[1], scr[2]]
                sg_free = [None]
                mt_free = [None, None]
                for m in range(4):
                    prod = {}
                    for which, (nm, xH, xL, ty) in enumerate((("proj_a", yaH, yaL, t_ya), ("proj_b", ybH, ybL, t_yb))):
                        q = slot("mix_w_in")
                        zs = groups(*q, nHk(S), nLk(S), tx, S)
                        ps_ = groups(*slot(nm), lambda i, x=xH: x[:, i, :], lambda i, x=xL: x[:, i, :], ty, S)
                        for i in range(2):
                            f = 2 * m + i
                            b, t = zs[i]
                            g = sg[i]
                            ta = act(g[:, :], banks[b][:, :], ACT.Sigmoid, t, sg_free[0])
                            bank_free[b] = ta
                            b2, t2 = ps_[i]
                            if which == 0:
                                tp = tt(mt[i][:, :], g[:, :], banks[b2][:, :], ALU.mult, ta, t2, mt_free[i])
                                bank_free[b2] = tp
                                sg_free[0] = tp
                                prod[i] = tp
                            else:
                                tp = tt(g[:, :], g[:, :], banks[b2][:, :], ALU.mult, ta, t2)
                                bank_free[b2] = tp
                                tp = tt(mt[i][:, :], mt[i][:, :], g[:, :], ALU.add, tp, prod[i])
                                sg_free[0] = tp
                                t_m[f] = halves(mH[:, f, :], mL[:, f, :], mt[i][:, :], tp)
                                mt_free[i] = t_m[f]
                sink = add_to_h(lambda: mod(1, l, 5))
                for o in range(0, 8, 2):
                    q = slot("w_out")

                    def each(i, b, t):
                        bank_free[b] = sink(False, o + i, b, t)

                    groups(*q, lambda i: mH[:, i, :], lambda i: mL[:, i, :], t_m, S, each)
            ph.close()

        NP, NPT = 5, 3

        def attention1(l, tx, yaH, yaL, fence):
            ph = ExitStack()
            q = sb(ph, "q", [128, 4, S])
            ko = [sb(ph, f"ko{i}", [128, S]) for i in range(2)]
            ks = [sb(ph, f"ks{i}", [128, S]) for i in range(2)]
            Vt = [sb(ph, f"Vt{i}", [128, 4, 128]) for i in range(2)]
            kc = sb(ph, "kc", [128, 2, 32])
            vc = sb(ph, "vc", [32, 128])
            gate = sb(ph, "gate", [128, 4, 24])

            with ExitStack() as sc:
                tab = sb(sc, "tab", [128, 4, S])
                tmp, rot, vx = scr[0], scr[1], scr[2]
                cm = [sb(sc, f"cm{i}", [128, S]) for i in range(2)]
                R = sb(sc, "R", [128, 16, 62])
                RH = sb(sc, "RH", [128, 16, 62], F32R)
                RL = sb(sc, "RL", [128, 16, 62], F32R)
                pe_ = sb(sc, "pe", [128, 2, 16])
                w2 = sb(sc, "w2", [128, 192])
                hc = sb(sc, "hc", [128, 2, 62])
                t_tab = P.dma("sp", "tab", tab[:, :, :], A["rope1"], fence)
                t_pe = P.dma("sp", "pe", pe_[:, :, :], A["pe"][l], fence)
                t_w2 = P.dma("sp", "w2", w2[:, :], A["w2"][l], fence)
                t_vt, t_k, t_ks, t_cm = [None, None], [None, None], [None, None], [None, None]
                ln = {"rope": None, "v": None}

                def kv(i):
                    def each(j, b, t):
                        if i == 0:
                            t_cm[j] = cp("act", cm[j][:, :], banks[b][:, :], t)
                            bank_free[b] = t_cm[j]
                        elif j == 0:
                            t = rope(b, t, S, tab[:, 2, :], tab[:, 3, :], ko[i - 1][:, :], tmp, rot, t_tab, ln["rope"])
                            ln["rope"] = t_k[i - 1] = t
                            for hf in range(2):
                                t_ks[i - 1] = cp("pool", ks[i - 1][64 * hf:64 * hf + 64, :],
                                                 ko[i - 1][64 - 64 * hf:128 - 64 * hf, :], t)
                        else:
                            tv = cp("act", vx[:, :], banks[b][:, :], t, ln["v"])
                            bank_free[b] = tv
                            pend.append((i - 1, tv))
                    groups(*slot("mix_w_in"), nHk(S), nLk(S), tx, S, each)

                pend = []

                def turn_v():
                    i, tv = pend.pop()
                    bt, free = take()
                    for j in range(4):
                        t = tr(banks[bt][:, j * 128:j * 128 + 128], vx[:, j * 128:j * 128 + 128], ident[:, :],
                               free, tv, inc=(j == 3))
                    ln["v"] = t
                    t_vt[i] = cp("act", Vt[i][:, :, :], banks[bt][:, :].rearrange("p (a b) -> p a b", a=4), t)
                    bank_free[bt] = t_vt[i]

                t_q = [None] * 4

                def queries(i):
                    def each(j, b, t):
                        t_q[2 * i + j] = ln["rope"] = rope(b, t, S, tab[:, 0, :], tab[:, 1, :], q[:, 2 * i + j, :], tmp,
                                                           rot, t_tab, ln["rope"])
                    groups(*slot("mix_w_in"), nHk(S), nLk(S), tx, S, each)

                t_R = [None]

                def blocks(j):
                    for hf in range(2):
                        for g in range(2):
                            src = cm[j][64 * g:64 * g + 64, :].rearrange("p (n l) -> p l n", l=16)[:, :, hf:hf + 31]
                            dst = R[64 * hf:64 * hf + 64, :, 31 * g:31 * g + 31]
                            tc_ = cp("dve", dst, src, t_cm[j], t_R[0])
                    pb = pe_[:, j, :].unsqueeze(2).broadcast_to([128, 16, 62])
                    tc_ = tt(R[:, :, :], R[:, :, :], pb, ALU.add, tc_, t_pe)
                    t_R[0] = halves(RH[:, :, :], RL[:, :, :], R[:, :, :], tc_, t_R[0])

                t_hc = [None, None]

                def compress(j):
                    k, hi, lo, tw = slot("cmp_w1")
                    b, free = take()
                    for i in range(16):
                        for n, (w, x) in enumerate(((hi, RH), (hi, RL), (lo, RH))):
                            t = mm(banks[b][:, 0:62], w[:, i, :], x[:, i, :], i == 0 and n == 0, i == 15 and n == 2,
                                   free, tw, t_R[0], inc=(i == 15 and n == 2))
                    done(k, t)
                    t_R[0] = [t, t_R[0]]
                    t_hc[j] = act(hc[:, j, :], banks[b][:, 0:62], ACT.Silu, t)
                    bank_free[b] = t_hc[j]

                kv(0)
                blocks(0)
                kv(1)
                compress(0)
                turn_v()
                blocks(1)
                kv(2)
                compress(1)
                turn_v()
                b, free = take()
                t = mm(banks[b][:, 0:62], w2[:, 0:128], hc[:, 0, :], True, True, free, t_hc[0], t_w2, inc=True)
                for qd in range(4):
                    d0, s0 = 32 * qd, 32 * (qd ^ 1)
                    tr_ = act(rot[d0:d0 + 32, 0:62], banks[b][s0:s0 + 32, 0:62], ACT.Copy, t, ln["rope"])
                v3 = lambda x: x.rearrange("p (g n) -> p g n", g=2)
                cb = ctab[:, 0, 0:31].unsqueeze(1).broadcast_to([128, 2, 31])
                sb_ = ctab[:, 1, 0:31].unsqueeze(1).broadcast_to([128, 2, 31])
                t1 = tt(v3(tmp[:, 0:62]), v3(banks[b][:, 0:62]), cb, ALU.mult, t, t_const, ln["rope"], tr_)
                bank_free[b] = t1
                t2 = tt(v3(rot[:, 0:62]), v3(rot[:, 0:62]), sb_, ALU.mult, tr_, t_const)
                tz = P.op("dve", lambda g: g.memset(kc[:, :, :], 0.0))
                t_kc = tt(kc[:, :, 0:31], v3(tmp[:, 0:62]), v3(rot[:, 0:62]), ALU.add, t1, t2, tz)
                ln["rope"] = t_kc
                queries(0)
                b, free = take()
                for g in range(2):
                    t = mm(banks[b][0:31, 64 * g:64 * g + 64], hc[:, 1, 31 * g:31 * g + 31], w2[:, 128:192],
                           True, True, free, t_hc[1], t_w2, inc=(g == 1))
                tz = P.op("dve", lambda g: g.memset(vc[:, :], 0.0))
                t_vc = cp("dve", vc[0:31, :], banks[b][0:31, 0:128], t, tz)
                bank_free[b] = t_vc
                queries(1)
                k, hi, lo, tw = slot("mix_w_in")
                b, free = take()
                for j in range(4):
                    tok_ = slice(j * 128, j * 128 + 128)
                    for i in range(8):
                        for n, (x, w) in enumerate(((nH, hi), (nL, hi), (nH, lo))):
                            t = mm(banks[b][:, j * 32:j * 32 + 24], x[:, i, tok_], w[:, i, 0:24],
                                   i == 0 and n == 0, i == 7 and n == 2, free, tw, tx[i],
                                   inc=(j == 3 and i == 7 and n == 2))
                done(k, t)
                t_gate = act(gate[:, :, :], banks[b][:, 0:128].rearrange("p (a b) -> p a b", a=4)[:, :, 0:24],
                             ACT.Sigmoid, t)
                bank_free[b] = t_gate

            Pb = [sb(ph, f"P{i}", [128, S]) for i in range(NP)]
            PT = [sb(ph, f"PT{i}", [128, S]) for i in range(NPT)]
            Pc = [sb(ph, f"Pc{i}", [128, 4, 32]) for i in range(2)]
            PcT = [sb(ph, f"PcT{i}", [32, S]) for i in range(2)]
            st_ = sb(ph, "st", [128, 8, 4])
            stc = sb(ph, "stc", [128, 2, 16])
            yo = sb(ph, "yo", [128, 2, S])
            units = []
            for hh in range(8):
                for qt in range(4):
                    units += [(hh, 1, qt), (hh, 2, qt)]
                units.append((hh, 0, 0))
            U = len(units)
            sP, sPT = [None] * U, [None] * U
            p_free, pt_free = {}, {}
            pc_free, pct_free = {}, {}
            o_free = {6: bank_free[6], 7: bank_free[7]}
            t_ya = [None] * 4
            yo_free = [None, None]
            wait_c = [t_const, t_gate, t_kc, t_vc, t_vt[0], t_vt[1], t_k, t_ks, t_q]
            ntok = {"i": 0, "c": 0, "j": 0, "cj": 0}

            def score(u):
                hh, br, qt = units[u]
                hf, g = hh % 2, hh // 4
                ps_ = slice(64 * hf, 64 * hf + 64)
                b, free = take()
                if br == 0:
                    for x in range(4):
                        mm(banks[b][:, 32 * x:32 * x + 32], q[ps_, hh // 2, 128 * x:128 * x + 128], kc[ps_, g, :],
                           x == 0, False, free, wait_c, skip_group_check=True)
                    t = mm(banks[b][:, 0:128], idb[:, :], cneg[:, :], False, True, skip_group_check=True, inc=True)
                    i = ntok["c"] % 2
                    ntok["c"] += 1
                    bk = banks[b][:, 0:128].rearrange("p (a b) -> p a b", a=4)
                    mx, sm, rr = stc[:, i, 0:4], stc[:, i, 4:8], stc[:, i, 8:12]
                    bc = lambda x: x.unsqueeze(2).broadcast_to([128, 4, 32])
                    t = P.op("dve", lambda e: e.tensor_reduce(mx, bk, AX, ALU.max), t, pc_free.get(i))
                    t = tt(Pc[i][:, :, :], bk, bc(mx), ALU.subtract, t)
                    bank_free[b] = t
                    t = act(Pc[i][:, :, :], Pc[i][:, :, :], ACT.Exp, t)
                    t = P.op("dve", lambda e: e.tensor_reduce(sm, Pc[i][:, :, :], AX, ALU.add), t)
                    t = P.op("dve", lambda e: e.reciprocal(rr, sm), t)
                    t = tt(rr, rr, gate[:, :, 3 * hh], ALU.mult, t)
                    t = tt(rr, rr, rowok[:, :], ALU.mult, t, t_const)
                    t = tt(Pc[i][:, :, :], Pc[i][:, :, :], bc(rr), ALU.mult, t)
                    sP[u] = (t, i)
                    return
                nk = 128 * (qt + 1)
                K = (ko if hf == g else ks)[br - 1]
                mm(banks[b][:, 0:nk], q[ps_, hh // 2, 128 * qt:128 * qt + 128], K[ps_, 0:nk], True, False,
                   free, wait_c, skip_group_check=True)
                t = mm(banks[b][:, nk - 128:nk], idb[:, :], negm[:, :], False, True, skip_group_check=True, inc=True)
                i = ntok["i"] % NP
                ntok["i"] += 1
                mx, sm, rr = st_[:, i, 0:1], st_[:, i, 1:2], st_[:, i, 2:3]
                t = P.op("dve", lambda e: e.tensor_reduce(mx, banks[b][:, 0:nk], AX, ALU.max, negate=True),
                         t, p_free.get(i))
                t = act(Pb[i][:, 0:nk], banks[b][:, 0:nk], ACT.Exp, t, bias=mx, accum_out=sm)
                bank_free[b] = t
                t = P.op("dve", lambda e: e.reciprocal(rr, sm), t)
                t = tt(rr, rr, gate[:, qt, 3 * hh + br:3 * hh + br + 1], ALU.mult, t)
                t = ts(Pb[i][:, 0:nk], Pb[i][:, 0:nk], rr, None, ALU.mult, None, t, e="pool")
                sP[u] = (t, i)

            def turn(u):
                hh, br, qt = units[u]
                t, i = sP[u]
                b, free = take()
                if br == 0:
                    for x in range(4):
                        tp = tr(banks[b][0:32, 128 * x:128 * x + 128], Pc[i][:, x, :], ident[:, :], free, t,
                                inc=(x == 3))
                    pc_free[i] = tp
                    j = ntok["cj"] % 2
                    ntok["cj"] += 1
                    t = cp("dve", PcT[j][:, :], banks[b][0:32, :], tp, pct_free.get(j))
                    bank_free[b] = t
                    sPT[u] = (t, j)
                    return
                for x in range(qt + 1):
                    tp = tr(banks[b][:, 128 * x:128 * x + 128], Pb[i][:, 128 * x:128 * x + 128], ident[:, :], free, t,
                            inc=(x == qt))
                p_free[i] = tp
                j = ntok["j"] % NPT
                ntok["j"] += 1
                nk = 128 * (qt + 1)
                t = cp("act" if u % 2 else "dve", PT[j][:, 0:nk], banks[b][:, 0:nk], tp, pt_free.get(j))
                bank_free[b] = t
                sPT[u] = (t, j)

            def value(u):
                hh, br, qt = units[u]
                hf, g, ft = hh % 2, hh // 4, hh // 2
                ob = 6 + ft % 2
                ps_ = slice(64 * hf, 64 * hf + 64)
                t, j = sPT[u]
                last = br == 0
                if last:
                    tp = pct_free[j] = mm(banks[ob][ps_, :], vc[:, 64 * g:64 * g + 64], PcT[j][:, :], False, True,
                                          t, skip_group_check=True, inc=True)
                else:
                    for x in range(qt + 1):
                        tp = mm(banks[ob][ps_, 128 * qt:128 * qt + 128], Vt[br - 1][:, x, 64 * g:64 * g + 64],
                                PT[j][:, 128 * x:128 * x + 128], br == 1 and qt == 0, False, t, o_free[ob],
                                skip_group_check=True, inc=(x == qt))
                    pt_free[j] = tp
                if last and hf == 1:
                    i = ft % 2
                    t = cp("act", yo[:, i, :], banks[ob][:, :], tp, yo_free[i])
                    o_free[ob] = t
                    t_ya[ft] = halves(yaH[:, ft, :], yaL[:, ft, :], yo[:, i, :], t)
                    yo_free[i] = t_ya[ft]

            for u in range(U + 4):
                if u < U:
                    score(u)
                if 3 <= u < U + 3:
                    turn(u - 3)
                if u >= 4:
                    value(u - 4)
            bank_free[6], bank_free[7] = o_free[6], o_free[7]
            ph.close()
            return t_ya

        def gmlp(l, tx, ybH, ybL):
            with ExitStack() as sc:
                uu = sb(sc, "uu", [128, 4, S])
                vf = sb(sc, "vf", [128, 4, S])
                vn = sb(sc, "vn", [128, 4, S])
                wT = sb(sc, "wT", [128, 8, 128])
                bsb = sb(sc, "bsb", [128, 4, 128])
                stt_ = sb(sc, "bst", [128, 4, 16])
                t_w = P.dma("sp", "wT", wT[:, :, :], A["wsT"][l])
                t_bs = P.dma("sp", "bsb", bsb[:, :, :], A["bsb"][l])
                t_ln = [P.dma("sp", f"lnp{i}", scr[2 + i][:, :], A["lnp"][l][:, i, :]) for i in range(2)]
                t_w = tt(wT[:, :, :], wT[:, :, :], msk[:, :].unsqueeze(1).broadcast_to([128, 8, 128]), ALU.mult,
                         t_w, t_const, e="pool")
                t_u = [None] * 4
                t_v = [None] * 4
                def each(i, b, t):
                    f = 2 * m + i
                    d = uu[:, f, :] if f < 4 else vf[:, f - 4, :]
                    t = act(d, banks[b][:, :], ACT.Gelu_apprx_tanh, t)
                    bank_free[b] = t
                    if f < 4:
                        t_u[f] = t
                    else:
                        t_v[f - 4] = t

                for m in range(4):
                    groups(*slot("mix_w_in"), nHk(S), nLk(S), tx, S, each)
                t_n = [None] * 4
                for tt_ in range(4):
                    b, free = take()
                    for f in range(4):
                        t = tr(banks[b][:, f * 128:f * 128 + 128], vf[:, f, tt_ * 128:tt_ * 128 + 128], ident[:, :],
                               free, t_v[f], inc=(f == 3))
                    s = stt_[:, tt_, :]
                    t0 = t
                    t = P.op("dve", lambda g, s=s, b=b: g.bn_stats(s[:, 0:6], banks[b][:, :]), t)
                    t = P.op("dve", lambda g, s=s: g.bn_aggr(s[:, 6:8], s[:, 0:6]), t)
                    t = act(s[:, 8:9], s[:, 7:8], ACT.Sqrt, t, bias=epsc[:, 0:1])
                    t = P.op("dve", lambda g, s=s: g.reciprocal(s[:, 9:10], s[:, 8:9]), t)
                    t = ts(vn[:, tt_, :], banks[b][:, :], s[:, 6:7], s[:, 9:10], ALU.subtract, ALU.mult, t)
                    bank_free[b] = t
                    t = tt(vn[:, tt_, :], vn[:, tt_, :], scr[2][:, :], ALU.mult, t, t_ln)
                    t_n[tt_] = tt(vn[:, tt_, :], vn[:, tt_, :], scr[3][:, :], ALU.add, t, t_ln)
                t_y = [None] * 4
                for f in range(4):
                    b, free = take()
                    for hf in range(2):
                        for tt_ in range(4):
                            g = 2 * f + hf
                            t = mm(banks[b][64 * hf:64 * hf + 64, tt_ * 128:tt_ * 128 + 128],
                                   vn[:, tt_, 64 * g:64 * g + 64], wT[:, g, :], tt_ == 0, tt_ == 3, free, t_w, t_n[tt_],
                                   skip_group_check=True, inc=(hf == 1 and tt_ == 3))
                    v = vf[:, f, :].rearrange("p (a b) -> p a b", a=4)
                    t = tt(v, banks[b][:, :].rearrange("p (a b) -> p a b", a=4),
                           bsb[:, f, :].unsqueeze(1).broadcast_to([128, 4, 128]), ALU.add, t, t_bs)
                    bank_free[b] = t
                    t = tt(vf[:, f, :], vf[:, f, :], uu[:, f, :], ALU.mult, t, t_u[f])
                    t_y[f] = halves(ybH[:, f, :], ybL[:, f, :], vf[:, f, :], t)
                return t_y

        for l in range(2):
            ffn_block1(l, 0)
            mixer(l)
            ffn_block1(l, 1)
        fin = normed(htiles, th, S, V("final_g"), None, None, keep=lambda i: h[:, i, :])
        th[:] = fin

        b2 = ExitStack()
        P.barrier()
        xc = sb(b2, "xc", [128, KT, C])
        t_xc = P.dma("sp", "xc", xc[:, :, :], A["ctxT"], P.everyone())
        tc = [t_xc] * 8
        ctiles = [xc[:, i, :] for i in range(8)]

        def post(tiles, x, tx_, N, g, gt, t_gt):
            i = der_i[0]
            der_i[0] = 1 - i
            Gp = der[:, i, 8:16]
            t_gp = tt(Gp, g, gt, ALU.mult, t_gt, P.last("dve"), P.last("act"), P.last("pool"))
            ts_ = [t for _, t in tiles]
            if True:
                b, t_r = rstd([a for a, _ in tiles], ts_, N, D)
                t_ = [scr[2 + i][:, 0:N] for i in range(2)]
                rd = [None, None]
                for i, (m, tm) in enumerate(tiles):
                    t1 = tt(t_[i % 2][:, :], m, banks[b][:, 0:N], ALU.mult, t_r, tm, rd[i % 2])
                    if i == 7:
                        bank_free[b] = t1
                    tx_[i] = stt(x[i], t_[i % 2][:, :], Gp[:, i:i + 1], x[i], ALU.mult, ALU.add, t1, t_gp, tx_[i])
                    rd[i % 2] = tx_[i]

        def mlp2(l, x, tx_, N, q):
            G, Sh, tg = scaled_gain(V("g_mlp_pre_2", l * 8), 2, l, 3, q)
            tx = normed(x, tx_, N, G, Sh, tg)
            with ExitStack() as sc:
                ma = sb(sc, "ma", [128, KT, N])
                tm = [None] * 8

                def sink(first, o, b, t):
                    if first:
                        tm[o] = cp("dve", ma[:, o, :], banks[b][:, 0:N], t)
                    else:
                        tm[o] = tt(ma[:, o, :], ma[:, o, :], banks[b][:, 0:N], ALU.add, t, tm[o])
                    return tm[o]

                ffn(NF2, "w_mlp_in_2", "w_mlp_out_2", tx, N, False, sink)
                gt, t_gt = mod(2, l, 5, q)
                post([(ma[:, o, :], tm[o]) for o in range(8)], x, tx_, N, V("g_mlp_post_2", l * 8), gt, t_gt)

        def pool_block(x, tx_, N, q, cnt):
            G, Sh, tg = scaled_gain(V("g_mix_pre_2"), 2, 0, 0, q)
            with ExitStack() as sc:
                P.barrier()
                hp = sb(sc, "hp", [128, KT, N + 16])
                t_z = P.op("dve", lambda g: g.memset(hp[:, :, 0:8], 0.0))
                t_z = P.op("dve", lambda g: g.memset(hp[:, :, N + 8:N + 16], 0.0))
                tn = normed(x, tx_, N, G, Sh, tg, keep=lambda i: hp[:, i, 8:N + 8])
                gt, t_gt = mod(2, 0, 2, q)
                P.barrier()
                cn = sb(sc, "cn", [128, 4, N])
                ym = sb(sc, "ym", [128, KT, N])
                t_cn = P.dma("sp", "cn", cn[:, :, :], cnt, P.everyone())
                s_ = [sb(sc, f"s{i}", [128, N + 16]) for i in range(2)]
                tx = [None] * 8
                prev = None
                for f in range(8):
                    g = f // 2
                    src, t, lo, hi = hp[:, f, :], [tn[f], t_z], 0, N + 16
                    for lev in range(g + 1):
                        a = 1 if lev == 0 else 2 ** (lev - 1)
                        b_ = 0 if lev == 0 else 2 ** (lev - 1)
                        lo, hi = lo + a, hi - b_
                        d = s_[lev % 2]
                        t = tt(d[:, lo:hi], src[:, lo - a:hi - a], src[:, lo + b_:hi + b_], ALU.add, t, prev)
                        src = d
                    o = s_[(g + 1) % 2]
                    t = tt(o[:, 8:N + 8], src[:, 8:N + 8], cn[:, g, :], ALU.mult, t, t_cn)
                    t = tt(ym[:, f, :], o[:, 8:N + 8], hp[:, f, 8:N + 8], ALU.subtract, t)
                    prev = t
                    tx[f] = halves(nH[:, f, 0:N], nL[:, f, 0:N], ym[:, f, :], t)
                k, hi, lo, tw = slot("w_pool_2")
                tm = [None] * 8
                for g in range(4):
                    res = groups(k, hi[:, 2 * g:2 * g + 2, :], lo[:, 2 * g:2 * g + 2, :], tw,
                                 lambda i: nH[:, 2 * g + i, 0:N], lambda i: nL[:, 2 * g + i, 0:N], tx[2 * g:2 * g + 2], N)
                    for i, (b, t) in enumerate(res):
                        f = 2 * g + i
                        tm[f] = act(ym[:, f, :], banks[b][:, 0:N], ACT.Copy, t, tx[f],
                                    scale=vec[:, VEC["pool_scale_2"] + f:VEC["pool_scale_2"] + f + 1])
                        bank_free[b] = tm[f]
                post([(ym[:, f, :], tm[f]) for f in range(8)], x, tx_, N, V("g_mix_post_2"), gt, t_gt)

        pool_block(htiles, th, S, 0, A["cnt"])
        mlp2(0, htiles, th, S, 0)
        pool_block(ctiles, tc, C, 1, A["cntc"])
        mlp2(0, ctiles, tc, C, 1)

        T = S + C
        G, Sh, tg = scaled_gain(V("g_mix_pre_2", 8), 2, 1, 0, 1)
        with ExitStack() as ph:
            P.barrier()
            KTt = sb(ph, "KTt", [128, 2, T])
            Vtk = sb(ph, "Vtk", [128, 6, 256])
            ps2 = ExitStack()
            tx = normed(ctiles, tc, C, G, Sh, tg)
            Q = sb(ph, "Q", [128, 8, S])
            tab = sb(ps2, "tab2", [128, 2, S])
            tmp2 = [sb(ps2, f"tmp2{i}", [128, S]) for i in range(2)]
            rot2 = [sb(ps2, f"rot2{i}", [128, S]) for i in range(2)]
            vT = sb(ps2, "vT", [128, S])
            qx2 = [sb(ps2, f"qx{i}", [128, S]) for i in range(2)]
            ssq2 = [sb(ps2, f"ssq{i}", [128, S]) for i in range(2)]
            sdg2 = [sb(ps2, f"sdg{i}", [128, S]) for i in range(2)]
            srs2 = sb(ps2, "srs", [128, 2, 8])
            t_tab = P.dma("sp", "tab2", tab[:, :, :], A["rope2"], P.everyone())
            P.barrier()
            fr = {"vT": None, 0: None, 1: None, "n": 0}

            later = []

            def head_norm(b, t, N, dst, gain, roped, keep):
                nt = N // 128
                u = fr["n"] % 2
                fr["n"] += 1
                qx, ssq, sdg, srs = qx2[u], ssq2[u], sdg2[u], srs2[:, u, :]
                t0 = act(qx[:, 0:N], banks[b][:, 0:N], ACT.Copy, t, fr[u], scale=gain)
                t1 = act(ssq[:, 0:N], banks[b][:, 0:N], ACT.Square, t, fr[u])
                bank_free[b] = [t0, t1]

                def stage1():
                    b1, free = take()
                    for j in range(nt):
                        t = mm(banks[b1][:, j:j + 1], ssq[:, j * 128:j * 128 + 128], ones[:, 0:1], True, True, free, t1,
                               inc=(j == nt - 1))
                    t = act(srs[:, 0:nt], banks[b1][:, 0:nt], ACT.Sqrt, t, bias=epsc[:, 0:1], scale=1.0 / 128)
                    bank_free[b1] = t
                    t = P.op("dve", lambda g: g.reciprocal(srs[:, 4:4 + nt], srs[:, 0:nt]), t)
                    for j in range(nt):
                        td = ts(sdg[:, j * 128:j * 128 + 128], ident[:, :], srs[:, 4 + j:5 + j], None, ALU.mult, None, t)
                    return td

                def stage2(td):
                    b2_, free = take()
                    t = mm(banks[b2_][:, 0:N], ones[:, :], sdg[:, 0:N], True, True, free, td, inc=True)
                    if not roped:
                        t = tt(dst, qx[:, 0:N], banks[b2_][:, 0:N], ALU.mult, t, t0)
                        bank_free[b2_] = t
                    else:
                        t = tt(qx[:, 0:N], qx[:, 0:N], banks[b2_][:, 0:N], ALU.mult, t, t0)
                        bank_free[b2_] = t
                        for q in range(4):
                            d0, s0 = 32 * q, 32 * (q ^ 1)
                            tr_ = cp("act", rot2[u][d0:d0 + 32, 0:N], qx[s0:s0 + 32, 0:N], t)
                        ta = tt(tmp2[u][:, 0:N], qx[:, 0:N], tab[:, 0, 0:N], ALU.mult, t, t_tab)
                        tb = tt(rot2[u][:, 0:N], rot2[u][:, 0:N], tab[:, 1, 0:N], ALU.mult, tr_, t_tab)
                        t = tt(dst, tmp2[u][:, 0:N], rot2[u][:, 0:N], ALU.add, ta, tb)
                    fr[u] = t
                    keep(t)

                later.append([stage1, stage2])

            def flush():
                tds = [a() for a, _ in later]
                for (_, z), td in zip(later, tds):
                    z(td)
                later.clear()

            t_K, t_V = [], []

            def values(b, t, N, hd, base):
                tv = cp("act", vT[:, 0:N], banks[b][:, 0:N], t, fr["vT"])
                bank_free[b] = tv
                bt, free = take()
                for j in range(N // 128):
                    t = tr(banks[bt][:, j * 128:j * 128 + 128], vT[:, j * 128:j * 128 + 128], ident[:, :], free, tv,
                           inc=(j == N // 128 - 1))
                fr["vT"] = t
                t = cp("dve", Vtk[:, base:base + N // 128, hd * 128:hd * 128 + 128],
                       banks[bt][:, 0:N].rearrange("p (a b) -> p a b", b=128), t)
                bank_free[bt] = t
                t_V.append(t)

            gq, gk = V("g_q_2", 0, 1), V("g_k_2", 0, 1)
            t_Q = [None] * 8

            def heads(N, dst, gain, roped, keep):
                def each(i, b, t):
                    if i == 0:
                        first.append((b, t))
                        return
                    flush()
                    for i_, (b_, t_) in enumerate((first[0], (b, t))):
                        head_norm(b_, t_, N, dst(i_), gain, roped, lambda t, i_=i_: keep(i_, t))
                first = []
                groups(*slot("w_qkv_2"), nHk(N), nLk(N), tx, N, each)

            heads(C, lambda i: KTt[:, i, 0:C], gk, False, lambda i, t: t_K.append(t))
            groups(*slot("w_qkv_2"), nHk(C), nLk(C), tx, C, lambda i, b, t: values(b, t, C, i, 0))
            flush()
            G, Sh, tg = scaled_gain(V("g_mix_pre_2", 8), 2, 1, 0, 0)
            tx = normed(htiles, th, S, G, Sh, tg)
            heads(S, lambda i: KTt[:, i, C:T], gk, True, lambda i, t: t_K.append(t))
            for m in range(4):
                heads(S, lambda i: Q[:, 2 * m + i, :], gq, True, lambda i, t, m=m: t_Q.__setitem__(2 * m + i, t))
            groups(*slot("w_qkv_2"), nHk(S), nLk(S), tx, S, lambda i, b, t: values(b, t, S, i, 2))
            flush()
            ps2.close()
            P.barrier()
            Pb = [sb(ph, f"Pb{i}", [128, T]) for i in range(4)]
            PT = sb(ph, "PTb", [128, 3, T])
            yo = sb(ph, "yo2", [128, 2, S])
            st2 = sb(ph, "st2", [128, 4, 8])
            SC = 128 ** -0.5
            units = [(hh, qt) for hh in range(8) for qt in range(4)]
            sP, sT = {}, {}
            p_free, pt_free = {}, {}
            o_free = {6: bank_free[6], 7: bank_free[7]}
            t_o = [None] * 8
            yo_free = [None, None]

            def score2(u):
                hh, qt = units[u]
                kv = hh // 4
                i = u % 4
                m1, m2, mm_, s1, s2, rr = (st2[:, i, x:x + 1] for x in range(6))
                bk, tk = [], []
                for part, (c0, n) in enumerate(((0, 384), (384, 384))):
                    b, free = take()
                    t = mm(banks[b][:, 0:n], Q[:, hh, 128 * qt:128 * qt + 128], KTt[:, kv, c0:c0 + n], True, True,
                           free, t_K, t_Q[hh], inc=True)
                    bk.append(b)
                    tk.append(P.op("dve", lambda g, o=(m1, m2)[part], b=b, n=n: g.tensor_reduce(
                        o, banks[b][:, 0:n], AX, ALU.max), t, p_free.get(i)))
                t = tt(mm_, m1, m2, ALU.max, tk)
                t = ts(mm_, mm_, -SC, None, ALU.mult, None, t)
                ta = act(Pb[i][:, 0:384], banks[bk[0]][:, 0:384], ACT.Exp, t, bias=mm_, scale=SC, accum_out=s1)
                bank_free[bk[0]] = ta
                tb = act(Pb[i][:, 384:768], banks[bk[1]][:, 0:384], ACT.Exp, t, bias=mm_, scale=SC, accum_out=s2)
                bank_free[bk[1]] = tb
                t = tt(rr, s1, s2, ALU.add, ta, tb)
                t = P.op("dve", lambda g: g.reciprocal(rr, rr), t)
                t = ts(Pb[i][:, :], Pb[i][:, :], rr, None, ALU.mult, None, t, e="pool")
                sP[u] = t

            def turn2(u):
                i, j = u % 4, u % 3
                t = []
                for part in range(2):
                    b, free = take()
                    for x in range(3):
                        c = 3 * part + x
                        tp = tr(banks[b][:, 128 * x:128 * x + 128], Pb[i][:, 128 * c:128 * c + 128], ident[:, :],
                                free, sP[u], inc=(x == 2))
                    e = "act" if part else "dve"
                    tq = cp(e, PT[:, j, 384 * part:384 * part + 384], banks[b][:, 0:384], tp, pt_free.get(j))
                    bank_free[b] = tq
                    t.append(tq)
                p_free[i] = tp
                sT[u] = t

            def value2(u):
                hh, qt = units[u]
                kv, j, ob = hh // 4, u % 3, 6 + hh % 2
                for x in range(6):
                    tp = mm(banks[ob][:, 128 * qt:128 * qt + 128], Vtk[:, x, 128 * kv:128 * kv + 128],
                            PT[:, j, 128 * x:128 * x + 128], qt == 0 and x == 0, qt == 3 and x == 5, sT[u], t_V,
                            o_free[ob] if qt == 0 else None, skip_group_check=True, inc=(x == 5))
                pt_free[j] = tp
                if qt == 3:
                    i = hh % 2
                    t = cp("act", yo[:, i, :], banks[ob][:, :], tp, yo_free[i])
                    o_free[ob] = t
                    t_o[hh] = halves(nH[:, hh, :], nL[:, hh, :], yo[:, i, :], t)
                    yo_free[i] = t_o[hh]

            U = len(units)
            for u in range(U + 3):
                if u < U:
                    score2(u)
                if 2 <= u < U + 2:
                    turn2(u - 2)
                if u >= 3:
                    value2(u - 3)
            bank_free[6], bank_free[7] = o_free[6], o_free[7]
        gt, t_gt = mod(2, 1, 2)
        with ExitStack() as sc:
            P.barrier()
            ym = sb(sc, "ym1", [128, KT, S])
            tm = [None] * 8
            for m in range(4):
                def each(i, b, t):
                    tm[2 * m + i] = cp("act", ym[:, 2 * m + i, :], banks[b][:, :], t)
                    bank_free[b] = tm[2 * m + i]

                groups(*slot("w_o_2"), nHk(S), nLk(S), t_o, S, each)
            post([(ym[:, f, :], tm[f]) for f in range(8)], htiles, th, S, V("g_mix_post_2", 8), gt, t_gt)
        mlp2(1, htiles, th, S, 0)
        b2.close()
        t_end = [P.dma("sp", f"out{i}", out[:, i, :], h[:, i, :], th[i]) for i in range(8)]
        P.wait("sp", t_end)
        assert st["used"] == len(slots), (st, len(slots))

        block = ctx.enter_context(nc.Block())
        P.emit(block)


def tables():
    f = np.float32
    c = {}
    c["ident"] = np.eye(128, dtype=f)
    inv = (1.0 / (f(10000.0) ** (np.arange(0, 64, 2, dtype=f) / f(64)))).astype(f)
    p = np.arange(128)
    sign = np.where((p % 64) < 32, -1.0, 1.0).astype(f)[:, None]

    def rope(pos):
        ang = (pos.astype(f)[None, :] * inv[p % 32][:, None]).astype(f)
        return np.cos(ang).astype(f), (np.sin(ang).astype(f) * sign).astype(f)

    co, si = rope(np.arange(S))
    c["rope1"] = np.stack([co * f(0.125), si * f(0.125), co, si], 1).reshape(128, 4, S).astype(f)
    ce = np.arange(31) * 16 + 31
    cc, cs_ = rope(np.concatenate([ce, ce[-1:]]))
    c["crope"] = np.stack([cc, cs_], 1).astype(f)
    inv2 = np.power(f(10000.0), -np.arange(0, 64, 2, dtype=f) / f(64)).astype(f)
    t = np.arange(S)
    pos = np.where(p[:, None] < 64, (t // 64)[None, :], (t % 64)[None, :]).astype(f)
    ang = (pos * inv2[p % 32][:, None]).astype(f)
    c["rope2"] = np.stack([np.cos(ang).astype(f), np.sin(ang).astype(f) * sign], 1).astype(f)
    q, k = np.arange(128)[:, None], np.arange(128)[None, :]
    c["negm"] = np.where(k <= q, 0.0, -1e30).astype(f)
    c["msk"] = (k >= q).astype(f)
    n = np.arange(32)
    cn = np.full((128, 4, 32), -1e30, f)
    for qt in range(4):
        ok = (n[None, :] < 31) & (16 * n[None, :] + 31 <= np.arange(128)[:, None] + 128 * qt)
        cn[:, qt][ok] = 0.0
    c["cneg"] = cn.reshape(128, 128)
    row = np.ones((128, 4), f)
    row[:31, 0] = 0.0
    c["rowok"] = row
    for name, L in (("cnt", S), ("cntc", C)):
        t = np.arange(L)
        o = np.zeros((4, L), f)
        for g, w in enumerate((2, 4, 8, 16)):
            o[g] = f(1.0) / (np.clip(t + w - w // 2, 0, L) - np.clip(t - w // 2, 0, L)).astype(f)
        c[name] = np.ascontiguousarray(np.broadcast_to(o[None], (128, 4, L)))
    return c


_IN = {"ident": (128, 128), "rope1": (128, 4, S), "crope": (128, 2, 32), "rope2": (128, 2, S), "msk": (128, 128),
       "rowok": (128, 4), "cnt": (128, 4, S), "cntc": (128, 4, C)}


def kernel(**inputs):
    import ml_dtypes as _ml
    import concourse.bacc as _bacc
    from concourse import mybir as _mybir
    from concourse.bass_utils import run_bass_kernel_spmd as _run

    I = {k: np.asarray(v) for k, v in inputs.items()}
    arrays = {}
    cst = tables()
    for n in _IN:
        arrays[n] = cst[n]
    for n in ("negm", "cneg"):
        arrays[n] = cst[n].astype(_ml.bfloat16)
    arrays["idb"] = np.eye(128).astype(_ml.bfloat16)

    def fm(a):
        r, n = a.shape
        return np.ascontiguousarray(a.T.reshape(n // 128, 128, r).transpose(1, 0, 2))

    arrays["xT"] = fm(I["x"][0])
    arrays["ctxT"] = fm(I["ctx_2"][0])
    parts = []
    for a, idx, r0, nk, c0, n in plan():
        w = I[a][idx]
        if a == "cmp_w1":
            b = w.reshape(2, 16, 64, 128).transpose(0, 2, 1, 3)
        elif a == "w_pool_2":
            b = w.reshape(8, 128, 256).transpose(1, 0, 2)
        else:
            b = w[r0:r0 + nk * 128, c0:c0 + n].reshape(nk, 128, n).transpose(1, 0, 2)
        parts.append(b.reshape(-1))
    arrays["wst"] = np.concatenate(parts)
    parts = []
    for b_, l, m, _, _ in ada_plan():
        w = I["ada_w" if b_ == 1 else "w_ada_2"][l][:, m * 1024:(m + 1) * 1024]
        parts.append(w.reshape(8, 128, 1024))
    arrays["ast"] = np.concatenate(parts)
    lay, nv = vec_layout()
    arrays["vec"] = np.ascontiguousarray(np.concatenate([I[n].reshape(-1) for n in lay]).reshape(nv, 128).T)
    arrays["pe"] = np.ascontiguousarray(I["cmp_pe"].reshape(2, 2, 2, 16, 64).transpose(0, 2, 4, 1, 3).reshape(2, 128, 2, 16))
    w2 = I["cmp_w2"]
    arrays["w2"] = np.ascontiguousarray(np.concatenate([w2[:, 0], w2[:, 0], w2[:, 1]], axis=2))
    arrays["wsT"] = np.ascontiguousarray(I["gm_ws"].transpose(0, 3, 1, 2))
    bs = I["gm_bs"].reshape(2, 4, 2, 1, 128)
    arrays["bsb"] = np.ascontiguousarray(np.broadcast_to(bs, (2, 4, 2, 64, 128)).reshape(2, 4, 128, 128).transpose(0, 2, 1, 3))
    ln = np.stack([I["gm_ln_g"], I["gm_ln_b"]], 1)[:, None]
    arrays["lnp"] = np.ascontiguousarray(np.broadcast_to(ln, (2, 128, 2, 512)))

    nc = _bacc.Bacc("TRN2", target_bir_lowering=False, num_devices=1, dynamic_dma_scratch_size=1024)
    A = {}
    for n, a in arrays.items():
        A[n] = nc.dram_tensor(f"in_{n}", a.shape, _mybir.dt.from_np(a.dtype), kind="ExternalInput").ap()
    out = nc.dram_tensor("out_0", (128, 8, S), F32, kind="ExternalOutput").ap()
    build(nc, A, out)
    r = _run(nc, [{f"in_{n}": a for n, a in arrays.items()}], core_ids=[0])
    got = r.results[0]["out_0"]
    return np.ascontiguousarray(got.transpose(2, 1, 0).reshape(1, S, D))
```

```python
from contextlib import ExitStack

import numpy as np
import concourse.bass as bass
from concourse import mybir

F32 = mybir.dt.float32
F32R = mybir.dt.float32r
BF16 = mybir.dt.bfloat16
ALU = mybir.AluOpType
ACT = mybir.ActivationFunctionType
AX = mybir.AxisListType.X

D = 1024
KT = 8
S = 512
C = 256
NF = 22
NF2 = 32
EPS = 1e-6
ENGINES = ("pe", "act", "dve", "pool", "sp")


ALONE = (34, 7, 20)
AFTER_POST = (78, 7, 20)
POOL_CONTEXT = (11, 15, 18, 22)
POOL_LATENTS = (15, 19, 23, 26)


def ffn_chunks(nf):
    out, at = [], 0
    while at < nf:
        out.append((at, min(4, nf - at)))
        at += 4
    return out


def plan():
    out = []

    def cols(a, idx, r0, nk, c0, n, w):
        for c in range(c0, c0 + n, w):
            out.append((a, idx, r0, nk, c, min(w, c0 + n - c)))

    def ffn1(l, j):
        cs = ffn_chunks(NF)
        for i, (f0, nf) in enumerate(cs):
            for p in range(0, nf, 2):
                out.append(("ffn_w_in", (l, j), 0, KT, (f0 + p) * 128, 256))
                out.append(("ffn_w_in", (l, j), 0, KT, (NF + f0 + p) * 128, 256))
            for g0, ng in ([cs[i - 1]] if i else []) + ([(f0, nf)] if i == len(cs) - 1 else []):
                cols("ffn_w_out", (l, j), g0 * 128, ng, 0, D, 2048 // ng)

    def ffn2(l):
        cs = ffn_chunks(NF2)
        for i, (f0, nf) in enumerate(cs):
            cols("w_mlp_in_2", (l,), 0, KT, f0 * 128, nf * 128, 256)
            for g0, ng in ([cs[i - 1]] if i else []) + ([(f0, nf)] if i == len(cs) - 1 else []):
                cols("w_mlp_out_2", (l,), g0 * 128, ng, 0, D, 2048 // ng)

    for l in range(2):
        ffn1(l, 0)
        cols("mix_w_in", (l,), 0, KT, 512, 512, 256)
        cols("mix_w_in", (l,), 0, KT, 1024, 256, 256)
        cols("mix_w_in", (l,), 0, KT, 0, 512, 256)
        out.append(("mix_w_in", (l,), 0, KT, 1280, 128))
        cols("mix_w_in", (l,), 0, KT, 1304, 1024, 256)
        for m in range(4):
            out.append(("mix_w_in", (l,), 0, KT, 2328 + 256 * m, 256))
            out.append(("proj_a", (l,), 0, 4, 256 * m, 256))
            out.append(("mix_w_in", (l,), 0, KT, 3352 + 256 * m, 256))
            out.append(("proj_b", (l,), 0, 4, 256 * m, 256))
        cols("w_out", (l,), 0, KT, 0, D, 256)
        ffn_start = len(out)
        ffn1(l, 1)

    def among(start, places):
        for g in (3, 2, 1, 0):
            out.insert(start + places[g], ("w_pool_2", (0,), 256 * g, 2, 0, 256))

    among(ffn_start, POOL_CONTEXT)
    ffn_start = len(out)
    ffn2(0)
    among(ffn_start, POOL_LATENTS)
    ffn2(0)
    cols("w_qkv_2", (0,), 0, KT, 1024, 512, 256)
    cols("w_qkv_2", (0,), 0, KT, 1024, 256, 256)
    cols("w_qkv_2", (0,), 0, KT, 0, 1024, 256)
    cols("w_qkv_2", (0,), 0, KT, 1280, 256, 256)
    cols("w_o_2", (0,), 0, KT, 0, D, 256)
    ffn2(1)
    return out


def ada_plan():
    out = [(1, l, m, True, False) for l in range(2) for m in range(9)]
    out += [(2, 0, m, True, True) for m in range(6)]
    out += [(2, 1, m, True, m < 2) for m in range(6)]
    return out


VEC = {}


def vec_layout():
    at, out = 0, {}
    for name, n in (("norm_g", 48), ("ada_b", 144), ("final_g", 8), ("b_ada_2", 96), ("g_mix_pre_2", 16),
                    ("g_mix_post_2", 16), ("g_mlp_pre_2", 16), ("g_mlp_post_2", 16), ("pool_scale_2", 8),
                    ("g_q_2", 1), ("g_k_2", 1)):
        out[name] = at
        at += n
    return out, at


class Program:

    def __init__(self, nc, ctx):
        self.nc, self.ctx = nc, ctx
        self.queue = {e: [] for e in ENGINES}
        self.count = {e: 0 for e in ENGINES}
        self.sem = {e: ctx.enter_context(nc.semaphore("s_" + e)) for e in ENGINES}
        self.seen = {e: {} for e in ENGINES}
        self.dma_sems = {}
        self.n = 0

    def wait(self, e, *tokens):
        for t in tokens:
            if t is None:
                continue
            if isinstance(t, list):
                self.wait(e, *t)
                continue
            key, sem, val = t
            if self.seen[e].get(key, 0) < val:
                self.seen[e][key] = val
                self.queue[e].append(lambda g, sem=sem, val=val: g.wait_ge(sem, val))

    def op(self, e, fn, *tokens):
        self.wait(e, *tokens)
        self.count[e] += 1
        self.queue[e].append(lambda g, fn=fn, s=self.sem[e]: fn(g).then_inc(s, 1))
        return (e, self.sem[e], self.count[e])

    def quiet(self, e, fn, *tokens):
        self.wait(e, *tokens)
        self.queue[e].append(fn)

    def last(self, e):
        return (e, self.sem[e], self.count[e]) if self.count[e] else None

    def dma(self, e, name, out, in_, *tokens):
        self.wait(e, *tokens)
        if name not in self.dma_sems:
            self.dma_sems[name] = [self.ctx.enter_context(self.nc.semaphore("d_" + name)), 0]
        d = self.dma_sems[name]
        d[1] += 16
        self.queue[e].append(lambda g, s=d[0]: g.dma_start(out, in_).then_inc(s, 16))
        return ("d_" + name, d[0], d[1])

    def everyone(self):
        return [self.last(e) for e in ("pe", "act", "dve", "pool")]

    def barrier(self):
        now = self.everyone()
        for e in ("act", "dve", "pool"):
            self.wait(e, now)

    def emit(self, block):
        def run(e):
            def body(g):
                for f in self.queue[e]:
                    f(g)
            return body
        block.tensor(run("pe"))
        block.scalar(run("act"))
        block.vector(run("dve"))
        block.gpsimd(run("pool"))
        block.sync(run("sp"))


def build(nc, A, out):
    ctx = ExitStack()
    P = Program(nc, ctx)
    slots = plan()
    adas = ada_plan()
    VEC, NV = vec_layout()
    names = [0]

    def sb(scope, name, shape, dt=F32, side="left"):
        names[0] += 1
        return scope.enter_context(nc.sbuf_tensor(f"{name}_{names[0]}", shape, dt, side=side))

    with ctx:
        h = sb(ctx, "h", [128, KT, S])
        nn = ExitStack()
        nH = sb(nn, "nH", [128, KT, S], F32R, side="right")
        nL = sb(nn, "nL", [128, KT, S], F32R, side="right")
        NR, NW, NA = 2, 4, 2
        raw = [sb(ctx, f"raw{i}", [128, 2048]) for i in range(NR)]
        WH = [sb(ctx, f"WH{i}", [128, 2048], F32R) for i in range(NW)]
        WL = [sb(ctx, f"WL{i}", [128, 2048], F32R) for i in range(NW)]
        araw = [sb(ctx, f"araw{i}", [128, 1024]) for i in range(NA)]
        half = sb(ctx, "half", [128, 2])
        cB = [sb(ctx, f"cB{i}", [128, 1024]) for i in range(2)]
        vec = sb(ctx, "vec", [128, NV])
        mods = sb(ctx, "mods", [128, 38 * 8])
        der = sb(ctx, "der", [128, 4, 32])
        ident = sb(ctx, "ident", [128, 128])
        ones = sb(ctx, "ones", [128, 128])
        epsc = sb(ctx, "epsc", [128, 1])
        scr = [sb(ctx, f"scr{i}", [128, S]) for i in range(4)]
        dummy = sb(ctx, "dummy", [128, 1])
        negm = sb(ctx, "negm", [128, 128], BF16)
        idb = sb(ctx, "idb", [128, 128], BF16)
        cneg = sb(ctx, "cneg", [128, 128], BF16)
        rowok = sb(ctx, "rowok", [128, 4])
        ctab = sb(ctx, "ctab", [128, 2, 32])
        edge = sb(ctx, "edge", [128, 4, 16])
        msk = sb(ctx, "msk", [128, 128])
        banks = [ctx.enter_context(nc.psum_tensor(f"ps{i}", [128, 512], F32)) for i in range(8)]

        class Banks(dict):

            def __init__(self):
                super().__init__({b: None for b in range(8)})
                self.order = list(range(6))

            def __setitem__(self, b, token):
                super().__setitem__(b, token)
                if b < 6:
                    if b in self.order:
                        self.order.remove(b)
                    self.order.append(b)

        bank_free = Banks()

        def take():
            b = bank_free.order.pop(0)
            return b, bank_free[b]

        def mm(out_, lhsT, rhs, start, stop, *tokens, inc=False, **kw):
            f = lambda g: g.matmul(out_, lhsT, rhs, start=start, stop=stop, **kw)
            if inc:
                return P.op("pe", f, *tokens)
            P.quiet("pe", f, *tokens)

        def tr(out_, in_, idn, *tokens, inc=False):
            f = lambda g: g.transpose(out_, in_, idn)
            if inc:
                return P.op("pe", f, *tokens)
            P.quiet("pe", f, *tokens)

        def act(out_, in_, func, *tokens, **kw):
            return P.op("act", lambda g: g.activation(out_, in_, func, **kw), *tokens)

        def tt(out_, a, b, op, *tokens, e="dve"):
            return P.op(e, lambda g: g.tensor_tensor(out_, a, b, op), *tokens)

        def ts(out_, a, s1, s2, op0, op1, *tokens, e="dve"):
            if s2 is None:
                return P.op(e, lambda g: g.tensor_scalar(out_, a, s1, None, op0), *tokens)
            return P.op(e, lambda g: g.tensor_scalar(out_, a, s1, s2, op0, op1), *tokens)

        def stt(out_, a, s, b, op0, op1, *tokens):
            return P.op("dve", lambda g: g.scalar_tensor_tensor(out=out_, in0=a, scalar=s, in1=b, op0=op0, op1=op1),
                        *tokens)

        def cp(e, out_, in_, *tokens):
            if e == "act":
                return act(out_, in_, ACT.Copy, *tokens)
            return P.op(e, lambda g: g.tensor_copy(out_, in_), *tokens)

        t_vec = P.dma("sp", "vec", vec[:, :], A["vec"])
        t_id = P.dma("sp", "ident", ident[:, :], A["ident"])
        t_h = P.dma("sp", "h", h[:, :, :], A["xT"])
        t_ones = P.op("dve", lambda g: g.memset(ones[:, :], 1.0))
        t_eps = P.op("dve", lambda g: g.memset(epsc[:, :], EPS))
        t_cb = [None, None]

        def condition(i, name, *tokens):
            t_cb[i] = P.dma("sp", f"cB{i}", cB[i][:, :], A[name], *tokens)

        def condition_silu(i):
            t_cb[i] = act(cB[i][:, :], cB[i][:, :], ACT.Silu, t_cb[i])

        condition(0, "cb")
        condition_silu(0)
        for e in ("pe", "act", "dve", "pool"):
            P.wait(e, t_vec, t_id, t_ones, t_eps)
        def V(name, i=0, n=8):
            return vec[:, VEC[name] + i:VEC[name] + i + n]

        offs, at = [], 0
        for s in slots:
            offs.append(at)
            at += 128 * s[3] * s[5]
        W = A["wst"]
        st = dict(loaded=0, split=0, used=0)
        t_raw = [None] * len(slots)
        t_hi = [None] * len(slots)
        t_lo = [None] * len(slots)
        t_use = [None] * len(slots)

        share = [False]

        def load(k):
            n = slots[k][3] * slots[k][5]
            src = W[offs[k]:offs[k] + 128 * n].rearrange("(p n) -> p n", p=128)
            free = [t_hi[k - NR], t_lo[k - NR]] if k >= NR else None
            t_raw[k] = P.dma("sp", f"raw{k % NR}", raw[k % NR][:, 0:n], src, free)

        def split(k):
            n = slots[k][3] * slots[k][5]
            free = t_use[k - NW] if k >= NW else None
            r, a, b = raw[k % NR], WH[k % NW], WL[k % NW]
            t_hi[k] = act(a[:, 0:n], r[:, 0:n], ACT.Copy, t_raw[k], free)
            t_lo[k] = tt(b[:, 0:n], r[:, 0:n], a[:, 0:n].bitcast(F32), ALU.subtract, t_raw[k], free, t_hi[k],
                         e="pool" if share[0] and k % 2 else "dve")

        def advance(ahead=NW):
            done_ = next((i for i in range(st["used"] + 1) if i == st["used"] or t_use[i] is None))
            while st["split"] < min(done_ + ahead, len(slots)):
                while st["loaded"] < min(st["split"] + NR, len(slots)):
                    if st["loaded"] >= NR and t_lo[st["loaded"] - NR] is None:
                        break
                    load(st["loaded"])
                    st["loaded"] += 1
                split(st["split"])
                st["split"] += 1
            while st["loaded"] < min(st["split"] + NR, len(slots)):
                load(st["loaded"])
                st["loaded"] += 1

        def slot(want):
            k = st["used"]
            assert slots[k][0] == want, (slots[k], want)
            advance()
            st["used"] += 1
            if not share[0]:
                ada_step()
            _, _, _, nk, _, nc_ = slots[k]
            hi = WH[k % NW][:, 0:nk * nc_].rearrange("p (k c) -> p k c", k=nk)
            lo = WL[k % NW][:, 0:nk * nc_].rearrange("p (k c) -> p k c", k=nk)
            return k, hi, lo, [t_hi[k], t_lo[k]]

        def done(k, tok):
            t_use[k] = tok

        mod_col, c_ = {}, 0
        for b_, l_, m_, a1, a2 in adas:
            mod_col[(b_, l_, m_, 0)] = c_
            c_ += 8
            if a2:
                mod_col[(b_, l_, m_, 1)] = c_
                c_ += 8
        assert c_ <= 38 * 8
        ad = dict(step=0, loaded=0)
        t_araw, t_aread, t_mod = {}, {}, {}

        early = ExitStack()
        NE = 16
        rows = [sb(early, f"row{j}", [128, 1024], side="right") for j in range(NE)]

        def ada_place(j):
            if j < NE:
                return f"row{j}", rows[j], None
            return f"araw{j % NA}", araw[j % NA], t_aread[j - NA] if j >= NE + NA else None

        def ada_load(j):
            name, w, free = ada_place(j)
            t_araw[j] = P.dma("sp", name, w[:, :], A["ast"][j], free)

        def rowsum(out_, a, b, total, *tokens):
            return P.op("dve", lambda g: g.scalar_tensor_tensor(
                out=out_, in0=a, scalar=1.0, in1=b, op0=ALU.mult, op1=ALU.mult, accum_out=total), *tokens)

        t_half = [None]

        def ada_step():
            j = ad["step"]
            if j >= 8 * len(adas):
                return
            while ad["loaded"] < (NE if j < 14 else min(8 * len(adas), j + NA)):
                ada_load(ad["loaded"])
                ad["loaded"] += 1
            if j == 24:
                condition(1, "cbc")
            if j == 26:
                condition_silu(1)
            if j == 8 * 18:
                condition_silu(0)
            b_, l_, m_, a1, a2 = adas[j // 8]
            f = j % 8
            w = ada_place(j)[1]
            kinds = [0, 1] if a2 else [0]
            reads = []
            for q in kinds:
                m = mod_col[(b_, l_, m_, q)]
                if q == kinds[-1]:
                    t = rowsum(w[:, :], w[:, :], cB[q][:, :], mods[:, m + f:m + f + 1], t_araw[j], t_cb[q], *reads)
                else:
                    for x in range(2):
                        b, free = 6 + x, bank_free[6 + x]
                        cut = slice(512 * x, 512 * x + 512)
                        t = rowsum(banks[b][:, :], w[:, cut], cB[q][:, cut], half[:, x:x + 1], t_araw[j], t_cb[q], free,
                                   t_half[0])
                        bank_free[b] = t
                    reads = [t]
                    t_half[0] = t = tt(mods[:, m + f:m + f + 1], half[:, 0:1], half[:, 1:2], ALU.add, t)
                if f == 7:
                    bias = V("ada_b", l_ * 72 + m_ * 8) if b_ == 1 else V("b_ada_2", l_ * 48 + m_ * 8)
                    t_mod[m] = t = tt(mods[:, m:m + 8], mods[:, m:m + 8], bias, ALU.add, t)
            t_aread[j] = t
            ad["step"] += 1
            if j == 8 * 18 - 1:
                condition(0, "cb2", t)

        while ad["loaded"] < NE:
            ada_load(ad["loaded"])
            ad["loaded"] += 1
        for k in range(NR):
            load(k)
            st["loaded"] += 1
        t_const = [P.dma("sp", nm, tl, A[nm]) for nm, tl in (
            ("negm", negm[:, :]), ("idb", idb[:, :]), ("cneg", cneg[:, :]), ("rowok", rowok[:, :]),
            ("crope", ctab[:, :, :]), ("msk", msk[:, :]), ("edge", edge[:, :, :]))]

        def mod(b_, l_, m_, q=0):
            m = mod_col[(b_, l_, m_, q)]
            while m not in t_mod:
                ada_step()
            return mods[:, m:m + 8], t_mod[m]

        class Path:

            def __init__(self, nH, nL, scr, rs, at):
                self.nH, self.nL, self.scr, self.rs, self.at, self.turn = nH, nL, scr, rs, at, 0
                self.busy = None

            def gains(self):
                self.turn = 1 - self.turn
                return self.at + self.turn

        rs = sb(ctx, "rs", [128, 8])
        lat = Path(nH, nL, scr, rs, 0)

        def drain(g):
            while True:
                try:
                    next(g)
                except StopIteration as e:
                    return e.value

        def weave(main, side, steps):
            out, n = [None, None], 0
            live = [True, True]
            while live[0] or live[1]:
                for which, (g, c) in enumerate(((main, 1), (side, steps(n) if live[0] else 1))):
                    for _ in range(c):
                        if live[which]:
                            try:
                                next(g)
                            except StopIteration as e:
                                live[which], out[which] = False, e.value
                n += 1
            return out

        def scaled_gain(p, g, b_, l_, m_, q=0):
            sh, t1 = mod(b_, l_, m_, q)
            sc, t2 = mod(b_, l_, m_ + 1, q)
            G = der[:, p.gains(), 0:8]
            t = stt(G, sc, 1.0, g, ALU.add, ALU.mult, t1, t2, P.last("act"), P.last("dve"), P.last("pool"))
            return G, sh, [t, t1]

        def busy_clock(n):
            if n:
                b, free = take()
                for i in range(n):
                    t = mm(banks[b][:, 0:128], ones[:, :], ones[:, :], True, True, free, inc=(i == n - 1))
                bank_free[b] = t

        def rstd(p, tiles, toks, N, dim, waits=(0, 0, 0)):
            scr = p.scr
            sq, ssum, dg = [scr[0][:, 0:N], scr[1][:, 0:N]], scr[2][:, 0:N], scr[3][:, 0:N]
            act(dummy[:, :], epsc[:, :], ACT.Sqrt, P.last("act"))
            before = P.last("dve")
            t_add = [None] * len(tiles)
            busy = p.busy
            for i, (x, tk) in enumerate(zip(tiles, toks)):
                t = act(sq[i % 2], x, ACT.Square, tk, t_add[i - 2] if i >= 2 else busy)
                if i == 0:
                    t_first = t
                    t_add[0] = t
                elif i == 1:
                    t_add[0] = t_add[1] = tt(ssum, sq[0], sq[1], ALU.add, t_first, t, before)
                else:
                    t_add[i] = tt(ssum, ssum, sq[i % 2], ALU.add, t, t_add[i - 1])
                if i in (3, 5):
                    yield
            yield
            t_sum = t_add[-1]
            nt = N // 128
            busy_clock(waits[0])
            b, free = take()
            for j in range(nt):
                t = mm(banks[b][:, j:j + 1], ssum[:, j * 128:j * 128 + 128], ones[:, 0:1], True, True,
                       free, t_sum, inc=(j == nt - 1))
            s = p.rs
            t = act(s[:, 0:nt], banks[b][:, 0:nt], ACT.Sqrt, t, bias=epsc[:, 0:1], scale=1.0 / dim)
            bank_free[b] = t
            t = P.op("dve", lambda g: g.reciprocal(s[:, 4:4 + nt], s[:, 0:nt]), t)
            for j in range(nt):
                td = ts(dg[:, j * 128:j * 128 + 128], ident[:, :], s[:, 4 + j:5 + j], None, ALU.mult, None, t)
            busy_clock(waits[1])
            yield
            b, free = take()
            t = mm(banks[b][:, 0:N], ones[:, :], dg[:, :], True, True, free, td, inc=True)
            busy_clock(waits[2])
            return b, t

        def halves(dH, dL, y, tok, free=None):
            t1 = act(dH, y, ACT.Copy, tok, free)
            t2 = tt(dL, y, dH.bitcast(F32), ALU.subtract, tok, t1, free)
            return [t1, t2]

        def normed(p, tiles, toks, N, G, Sh, t_gs, keep=None, clear=None, waits=(0, 0, 0)):
            outs = []
            nH, nL, scr = p.nH, p.nL, p.scr
            if True:
                b, t_r = yield from rstd(p, tiles, toks, N, D, waits)
                if callable(G):
                    G, Sh, t_gs = G()
                t_ = [scr[i][:, 0:N] for i in range(2)]
                y_ = [scr[2 + i][:, 0:N] for i in range(2)]
                ty = [None] * len(tiles)
                tl = [None] * len(tiles)
                th = [None] * len(tiles)
                for i, x in enumerate(tiles):
                    t, y = t_[i % 2], y_[i % 2]
                    fr = [ty[i - 2], th[i - 2]] if i >= 2 else None
                    t1 = tt(t[:, :], x, banks[b][:, 0:N], ALU.mult, t_r, toks[i], fr)
                    if i == len(tiles) - 1:
                        bank_free[b] = t1
                    sh = Sh[:, i:i + 1] if Sh is not None else None
                    if keep is not None:
                        if sh is None:
                            ty[i] = th[i] = ts(keep(i), t[:, :], G[:, i:i + 1], None, ALU.mult, None, t1, t_gs)
                        else:
                            ty[i] = th[i] = act(keep(i), t[:, :], ACT.Identity, t1, t_gs, clear, scale=G[:, i:i + 1],
                                                bias=sh)
                        outs.append(ty[i])
                        if i % 2:
                            yield
                        continue
                    th[i] = act(nH[:, i, 0:N], t[:, :], ACT.Identity, t1, t_gs, scale=G[:, i:i + 1], bias=sh)
                    ty[i] = ts(y[:, :], t[:, :], G[:, i:i + 1], sh, ALU.mult, ALU.add, t1, t_gs,
                               tl[i - 2] if i >= 2 else None, e="pool")
                    tl[i] = tt(nL[:, i, 0:N], y[:, :], nH[:, i, 0:N].bitcast(F32), ALU.subtract, ty[i], th[i])
                    outs.append([th[i], tl[i]])
                    if i % 2:
                        yield
            p.busy = ty[-2:] + th[-2:] + tl[-2:]
            return outs

        def groups(k, hi, lo, tw, xH, xL, tx, N, each=None):
            nk = hi.shape[1]
            res = []
            for c in range(hi.shape[2] // 128):
                b, free = take()
                cc = slice(c * 128, c * 128 + 128)
                for i in range(nk):
                    for n, (w, x) in enumerate(((hi, xH), (hi, xL), (lo, xH))):
                        t = mm(banks[b][:, 0:N], w[:, i, cc], x(i), i == 0 and n == 0, i == nk - 1 and n == 2,
                               free, tw, tx[i], inc=(i == nk - 1 and n == 2))
                res.append((b, t))
                if c == hi.shape[2] // 128 - 1:
                    done(k, t)
                if each:
                    each(c, b, t)
            return res

        def wide(sl, xH, xL, tx, N):
            cols, res = [], []
            for (k, hi, lo, tw) in sl:
                for c in range(hi.shape[2] // 128):
                    b, free = take()
                    cols.append((b, free, k, hi, lo, tw, slice(c * 128, c * 128 + 128)))
            nk = sl[0][1].shape[1]
            toks = {}
            for i in range(nk):
                for b, free, k, hi, lo, tw, cc in cols:
                    for n, (w, x) in enumerate(((hi, xH), (hi, xL), (lo, xH))):
                        t = mm(banks[b][:, 0:N], w[:, i, cc], x(i), i == 0 and n == 0, i == nk - 1 and n == 2,
                               free, tw, tx[i], inc=(i == nk - 1 and n == 2), skip_group_check=True)
                    toks[b] = t
            for b, free, k, *_ in cols:
                res.append((b, toks[b]))
                done(k, toks[b])
            return res

        nHk = lambda N, p=lat: (lambda i: p.nH[:, i, 0:N])
        nLk = lambda N, p=lat: (lambda i: p.nL[:, i, 0:N])

        def ffn(p_, nf, w_in, w_out, tx, N, gated, sink):
            with ExitStack() as sc:
                side = "right" if gated else "left"
                hH = sb(sc, "hH", [128, 2, 4, N], F32R, side=side)
                hL = sb(sc, "hL", [128, 2, 4, N], F32R, side=side)
                scr = p_.scr
                a_ = [scr[i][:, 0:N] for i in range(2)]
                y_ = [scr[2 + i][:, 0:N] for i in range(2)]
                chunks = ffn_chunks(nf)
                t_hid = {}
                t_out = {}
                rd = [None, None]
                ra = [None, None]
                n_ = [0]

                def hidden(ci):
                    f0, cn = chunks[ci]
                    free_h = t_out.get(ci - 2)
                    for p in range(0, cn, 2):
                        ta, us = {}, {}

                        def first(i, b, t):
                            u = us[i] = n_[0] % 2
                            n_[0] += 1
                            ta[i] = act(a_[u][:, :], banks[b][:, 0:N], ACT.Silu if gated else ACT.Relu, t, ra[u])
                            bank_free[b] = ta[i]
                            if not gated:
                                finish(i, tt(y_[u][:, :], a_[u][:, :], a_[u][:, :], ALU.mult, ta[i], rd[u]))

                        def second(i, b, t):
                            u = us[i]
                            ty = tt(y_[u][:, :], a_[u][:, :], banks[b][:, 0:N], ALU.mult, ta[i], t, rd[u])
                            bank_free[b] = ty
                            finish(i, ty)

                        def finish(i, ty):
                            u = us[i]
                            ra[u] = ty
                            rd[u] = halves(hH[:, ci % 2, p + i, :], hL[:, ci % 2, p + i, :], y_[u][:, :], ty, free_h)
                            t_hid[(ci, p + i)] = rd[u]

                        if ci == 0 and p == 0:
                            res = wide([slot(w_in) for _ in range(2 if gated else 1)], nHk(N, p_), nLk(N, p_), tx, N)
                            for i in range(2):
                                first(i, *res[i])
                            for i in range(2 if gated else 0):
                                second(i, *res[2 + i])
                        else:
                            groups(*slot(w_in), nHk(N, p_), nLk(N, p_), tx, N, first)
                            if gated:
                                yield
                                groups(*slot(w_in), nHk(N, p_), nLk(N, p_), tx, N, second)
                        yield

                def outp(ci):
                    f0, cn = chunks[ci]
                    tx_ = [t_hid[(ci, f)] for f in range(cn)]
                    o = 0
                    while o < 8:
                        q = slot(w_out)

                        def each(c, b, t):
                            bank_free[b] = sink(ci == 0, o + c, b, t)

                        res = groups(*q, lambda i: hH[:, ci % 2, i, :], lambda i: hL[:, ci % 2, i, :], tx_, N, each)
                        o += len(res)
                        yield
                    t_out[ci] = res[-1][1]

                for ci in range(len(chunks)):
                    yield from hidden(ci)
                    if ci:
                        yield from outp(ci - 1)
                yield from outp(len(chunks) - 1)

        th = [t_h] * 8
        htiles = [h[:, i, :] for i in range(8)]

        def add_to_h(gate_of):
            got = []

            def sink(first, o, b, t):
                if not got:
                    got.extend(gate_of())
                gate, t_g = got
                th[o] = stt(h[:, o, :], banks[b][:, :], gate[:, o:o + 1], h[:, o, :], ALU.mult, ALU.add, t, t_g, th[o])
                return th[o]
            return sink

        def ffn_block1(l, j):
            def gain():
                got = scaled_gain(lat, V("norm_g", (l * 3 + 2 * j) * 8), 1, l, 6 * j)
                advance(2 if l == j == 0 else NW)
                return got

            tx = yield from normed(lat, htiles, th, S, gain, None, None, waits=ALONE if l or j else (0, 0, 60))
            if l == j == 0:
                early.close()

            def half_gate():
                g, t_g = mod(1, l, 6 * j + 2)
                gh = der[:, j, 16:24]
                return gh, ts(gh, g, 0.5, None, ALU.mult, None, t_g, P.last("dve"))

            yield from ffn(lat, NF, "ffn_w_in", "ffn_w_out", tx, S, True, add_to_h(half_gate))

        def rope(b, t, N, cosT, sinT, dst, tmp, rot, t_tab, frees):
            for q in range(4):
                d0, s0 = 32 * q, 32 * (q ^ 1)
                tr_ = act(rot[d0:d0 + 32, 0:N], banks[b][s0:s0 + 32, 0:N], ACT.Copy, t, frees)
            t1 = tt(tmp[:, 0:N], banks[b][:, 0:N], cosT, ALU.mult, t, t_tab, frees, tr_)
            bank_free[b] = t1
            t2 = tt(rot[:, 0:N], rot[:, 0:N], sinT, ALU.mult, tr_, t_tab)
            return tt(dst, tmp[:, 0:N], rot[:, 0:N], ALU.add, t1, t2)

        def mixer(l):
            G, Sh, tg = scaled_gain(lat, V("norm_g", (l * 3 + 1) * 8), 1, l, 3)
            fence = P.everyone()
            tx = drain(normed(lat, htiles, th, S, G, Sh, tg, waits=ALONE))
            ph = ExitStack()
            yaH = sb(ph, "yaH", [128, 4, S], F32R)
            yaL = sb(ph, "yaL", [128, 4, S], F32R)
            t_ya = attention1(l, tx, yaH, yaL, fence)
            P.barrier()
            ybH = sb(ph, "ybH", [128, 4, S], F32R)
            ybL = sb(ph, "ybL", [128, 4, S], F32R)
            ready = []

            def merge_products(nm, xH, xL, ty):
                zs = groups(*slot("mix_w_in"), nHk(S), nLk(S), tx, S)
                return zs, groups(*slot(nm), lambda i: xH[:, i, :], lambda i: xL[:, i, :], ty, S)

            t_yb = gmlp(l, tx, ybH, ybL, lambda: ready.append(merge_products("proj_a", yaH, yaL, t_ya)))
            with ExitStack() as sc:
                P.barrier()
                mH = sb(sc, "mH", [128, 8, S], F32R)
                mL = sb(sc, "mL", [128, 8, S], F32R)
                sg = [scr[0]] * 2
                t_m = [None] * 8
                mt = [scr[1], scr[2]]
                sg_free = [None]
                mt_free = [None, None]
                for m in range(4):
                    prod = {}
                    for which, (nm, xH, xL, ty) in enumerate((("proj_a", yaH, yaL, t_ya), ("proj_b", ybH, ybL, t_yb))):
                        zs, ps_ = ready.pop() if ready else merge_products(nm, xH, xL, ty)
                        for i in range(2):
                            f = 2 * m + i
                            b, t = zs[i]
                            g = sg[i]
                            ta = act(g[:, :], banks[b][:, :], ACT.Sigmoid, t, sg_free[0])
                            bank_free[b] = ta
                            b2, t2 = ps_[i]
                            if which == 0:
                                tp = tt(mt[i][:, :], g[:, :], banks[b2][:, :], ALU.mult, ta, t2, mt_free[i])
                                bank_free[b2] = tp
                                sg_free[0] = tp
                                prod[i] = tp
                            else:
                                tp = tt(g[:, :], g[:, :], banks[b2][:, :], ALU.mult, ta, t2)
                                bank_free[b2] = tp
                                tp = tt(mt[i][:, :], mt[i][:, :], g[:, :], ALU.add, tp, prod[i])
                                sg_free[0] = tp
                                t_m[f] = halves(mH[:, f, :], mL[:, f, :], mt[i][:, :], tp)
                                mt_free[i] = t_m[f]
                sink = add_to_h(lambda: mod(1, l, 5))
                for o in range(0, 8, 2):
                    q = slot("w_out")

                    def each(i, b, t):
                        bank_free[b] = sink(False, o + i, b, t)

                    groups(*q, lambda i: mH[:, i, :], lambda i: mL[:, i, :], t_m, S, each)
            ph.close()

        NP = 5

        def attention1(l, tx, yaH, yaL, fence):
            ph = ExitStack()
            q = sb(ph, "q", [128, 4, S])
            ko = [sb(ph, f"ko{i}", [128, S]) for i in range(2)]
            ks = [sb(ph, f"ks{i}", [128, S]) for i in range(2)]
            Vt = [sb(ph, f"Vt{i}", [128, 4, 128]) for i in range(2)]
            kc = sb(ph, "kc", [128, 2, 32])
            vc = sb(ph, "vc", [32, 128])
            gate = sb(ph, "gate", [128, 4, 24])

            with ExitStack() as sc:
                tab = sb(sc, "tab", [128, 4, S])
                tmp, rot, vx = scr[0], scr[1], scr[2]
                cm = [sb(sc, f"cm{i}", [128, S]) for i in range(2)]
                R = sb(sc, "R", [128, 16, 62])
                cw = sb(sc, "cw", [128, 16, 128])
                pe_ = sb(sc, "pe", [128, 2, 16])
                w2 = sb(sc, "w2", [128, 192])
                hc = sb(sc, "hc", [128, 2, 62])
                t_tab = P.dma("pool", "tab", tab[:, :, :], A["rope1"], fence)
                t_cw = [P.dma("pool", "cw", cw[:, :, :], A["cw"][l, 0], fence)]
                t_pe = P.dma("pool", "pe", pe_[:, :, :], A["pe"][l], fence)
                t_w2 = P.dma("pool", "w2", w2[:, :], A["w2"][l], fence)
                t_vt, t_k, t_ks, t_cm = [None, None], [None, None], [None, None], [None, None]
                ln = {"rope": None, "v": None}

                def kv(i):
                    def each(j, b, t):
                        if i == 0:
                            t_cm[j] = cp("act", cm[j][:, :], banks[b][:, :], t)
                            bank_free[b] = t_cm[j]
                        elif j == 0:
                            t = rope(b, t, S, tab[:, 2, :], tab[:, 3, :], ko[i - 1][:, :], tmp, rot, t_tab, ln["rope"])
                            ln["rope"] = t_k[i - 1] = t
                            for hf in range(2):
                                t_ks[i - 1] = cp("pool", ks[i - 1][64 * hf:64 * hf + 64, :],
                                                 ko[i - 1][64 - 64 * hf:128 - 64 * hf, :], t)
                        else:
                            tv = cp("act", vx[:, :], banks[b][:, :], t, ln["v"])
                            bank_free[b] = tv
                            pend.append((i - 1, tv))
                    groups(*slot("mix_w_in"), nHk(S), nLk(S), tx, S, each)

                pend = []

                def turn_v():
                    i, tv = pend.pop()
                    bt, free = take()
                    for j in range(4):
                        t = tr(banks[bt][:, j * 128:j * 128 + 128], vx[:, j * 128:j * 128 + 128], ident[:, :],
                               free, tv, inc=(j == 3))
                    ln["v"] = t
                    t_vt[i] = cp("act", Vt[i][:, :, :], banks[bt][:, :].rearrange("p (a b) -> p a b", a=4), t)
                    bank_free[bt] = t_vt[i]

                t_q = [None] * 4

                def queries(i):
                    def each(j, b, t):
                        t_q[2 * i + j] = ln["rope"] = rope(b, t, S, tab[:, 0, :], tab[:, 1, :], q[:, 2 * i + j, :], tmp,
                                                           rot, t_tab, ln["rope"])
                    groups(*slot("mix_w_in"), nHk(S), nLk(S), tx, S, each)

                t_R = [None]

                def blocks(j):
                    for hf in range(2):
                        for g in range(2):
                            src = cm[j][64 * g:64 * g + 64, :].rearrange("p (n l) -> p l n", l=16)[:, :, hf:hf + 31]
                            dst = R[64 * hf:64 * hf + 64, :, 31 * g:31 * g + 31]
                            tc_ = cp("dve", dst, src, t_cm[j], t_R[0])
                    pb = pe_[:, j, :].unsqueeze(2).broadcast_to([128, 16, 62])
                    tc_ = tt(R[:, :, :], R[:, :, :], pb, ALU.add, tc_, t_pe)
                    t_R[0] = tc_

                t_hc = [None, None]

                def compress(j):
                    b, free = take()
                    for i in range(16):
                        t = mm(banks[b][:, 0:62], cw[:, i, :], R[:, i, :], i == 0, i == 15, free, t_cw[0], t_R[0],
                               inc=(i == 15))
                    t_R[0] = t
                    if j == 0:
                        t_cw[0] = P.dma("pool", "cw", cw[:, :, :], A["cw"][l, 1], t)
                    t_hc[j] = act(hc[:, j, :], banks[b][:, 0:62], ACT.Silu, t)
                    bank_free[b] = t_hc[j]

                kv(0)
                blocks(0)
                kv(1)
                compress(0)
                turn_v()
                blocks(1)
                kv(2)
                compress(1)
                turn_v()
                b, free = take()
                t = mm(banks[b][:, 0:62], w2[:, 0:128], hc[:, 0, :], True, True, free, t_hc[0], t_w2, inc=True)
                for qd in range(4):
                    d0, s0 = 32 * qd, 32 * (qd ^ 1)
                    tr_ = act(rot[d0:d0 + 32, 0:62], banks[b][s0:s0 + 32, 0:62], ACT.Copy, t, ln["rope"])
                v3 = lambda x: x.rearrange("p (g n) -> p g n", g=2)
                cb = ctab[:, 0, 0:31].unsqueeze(1).broadcast_to([128, 2, 31])
                sb_ = ctab[:, 1, 0:31].unsqueeze(1).broadcast_to([128, 2, 31])
                t1 = tt(v3(tmp[:, 0:62]), v3(banks[b][:, 0:62]), cb, ALU.mult, t, t_const, ln["rope"], tr_)
                bank_free[b] = t1
                t2 = tt(v3(rot[:, 0:62]), v3(rot[:, 0:62]), sb_, ALU.mult, tr_, t_const)
                tz = P.op("dve", lambda g: g.memset(kc[:, :, :], 0.0))
                t_kc = tt(kc[:, :, 0:31], v3(tmp[:, 0:62]), v3(rot[:, 0:62]), ALU.add, t1, t2, tz)
                ln["rope"] = t_kc
                queries(0)
                b, free = take()
                for g in range(2):
                    t = mm(banks[b][0:31, 64 * g:64 * g + 64], hc[:, 1, 31 * g:31 * g + 31], w2[:, 128:192],
                           True, True, free, t_hc[1], t_w2, inc=(g == 1))
                tz = P.op("dve", lambda g: g.memset(vc[:, :], 0.0))
                t_vc = cp("dve", vc[0:31, :], banks[b][0:31, 0:128], t, tz)
                bank_free[b] = t_vc
                queries(1)
                t_g24 = [None]

                def each(i, b, t):
                    t_g24[0] = bank_free[b] = act(vx[0:24, :], banks[b][0:24, :], ACT.Sigmoid, t, ln["v"])

                groups(*slot("mix_w_in"), nHk(S), nLk(S), tx, S, each)
                b, free = take()
                for j in range(4):
                    t = tr(banks[b][:, j * 32:j * 32 + 24], vx[0:24, j * 128:j * 128 + 128], ident[0:24, 0:24],
                           free, t_g24[0], inc=(j == 3))
                t_gate = cp("act", gate[:, :, :], banks[b][:, 0:128].rearrange("p (a b) -> p a b", a=4)[:, :, 0:24], t)
                bank_free[b] = t_gate

            Pb = [sb(ph, f"P{i}", [128, S]) for i in range(NP)]
            PT = [sb(ph, f"PT{i}", [128, 4, S]) for i in range(2)]
            Pc = [sb(ph, f"Pc{i}", [128, 4, 32]) for i in range(2)]
            PcT = [scr[i][0:32, :] for i in range(2)]
            st_ = sb(ph, "st", [128, 8, 4])
            stc = sb(ph, "stc", [128, 2, 16])
            yo = [scr[2], scr[3]]
            units = []
            for hh in range(8):
                units += [(hh, br, qt) for br in (1, 2) for qt in range(4)] + [(hh, 0, 0)]
            U = len(units)
            sP, sPT = [None] * U, {}
            p_free, pt_free = {}, {}
            pc_free, pct_free = {}, {}
            o_free = {6: bank_free[6], 7: bank_free[7]}
            t_ya = [None] * 4
            yo_free = [None, None]
            wait_c = [t_const, t_gate, t_kc, t_vc, t_vt[0], t_vt[1], t_k, t_ks, t_q]
            ntok = {"i": 0, "c": 0, "j": 0, "cj": 0}

            def score(u):
                hh, br, qt = units[u]
                hf, g = hh % 2, hh // 4
                ps_ = slice(64 * hf, 64 * hf + 64)
                b, free = take()
                if br == 0:
                    for x in range(4):
                        mm(banks[b][:, 32 * x:32 * x + 32], q[ps_, hh // 2, 128 * x:128 * x + 128], kc[ps_, g, :],
                           x == 0, False, free, wait_c, skip_group_check=True)
                    t = mm(banks[b][:, 0:128], idb[:, :], cneg[:, :], False, True, skip_group_check=True, inc=True)
                    i = ntok["c"] % 2
                    ntok["c"] += 1
                    bk = banks[b][:, 0:128].rearrange("p (a b) -> p a b", a=4)
                    mx, sm, rr = stc[:, i, 0:4], stc[:, i, 4:8], stc[:, i, 8:12]
                    bc = lambda x: x.unsqueeze(2).broadcast_to([128, 4, 32])
                    t = P.op("dve", lambda e: e.tensor_reduce(mx, bk, AX, ALU.max), t, pc_free.get(i))
                    t = tt(Pc[i][:, :, :], bk, bc(mx), ALU.subtract, t)
                    bank_free[b] = t
                    t = act(Pc[i][:, :, :], Pc[i][:, :, :], ACT.Exp, t)
                    t = P.op("dve", lambda e: e.tensor_reduce(sm, Pc[i][:, :, :], AX, ALU.add), t)
                    t = P.op("dve", lambda e: e.reciprocal(rr, sm), t)
                    t = tt(rr, rr, gate[:, :, 3 * hh], ALU.mult, t)
                    t = tt(rr, rr, rowok[:, :], ALU.mult, t, t_const)
                    t = tt(Pc[i][:, :, :], Pc[i][:, :, :], bc(rr), ALU.mult, t)
                    sP[u] = (t, i)
                    return
                nk = 128 * (qt + 1)
                K = (ko if hf == g else ks)[br - 1]
                mm(banks[b][:, 0:nk], q[ps_, hh // 2, 128 * qt:128 * qt + 128], K[ps_, 0:nk], True, False,
                   free, wait_c, skip_group_check=True)
                t = mm(banks[b][:, nk - 128:nk], idb[:, :], negm[:, :], False, True, skip_group_check=True, inc=True)
                i = ntok["i"] % NP
                ntok["i"] += 1
                mx, sm, rr = st_[:, i, 0:1], st_[:, i, 1:2], st_[:, i, 2:3]
                t = P.op("dve", lambda e: e.tensor_reduce(mx, banks[b][:, 0:nk], AX, ALU.max, negate=True),
                         t, p_free.get(i))
                t = act(Pb[i][:, 0:nk], banks[b][:, 0:nk], ACT.Exp, t, bias=mx, accum_out=sm)
                bank_free[b] = t
                t = P.op("dve", lambda e: e.reciprocal(rr, sm), t)
                t = tt(rr, rr, gate[:, qt, 3 * hh + br:3 * hh + br + 1], ALU.mult, t)
                t = ts(Pb[i][:, 0:nk], Pb[i][:, 0:nk], rr, None, ALU.mult, None, t, e="pool")
                sP[u] = (t, i)

            def turn(u):
                hh, br, qt = units[u]
                t, i = sP[u]
                b, free = take()
                if br == 0:
                    for x in range(4):
                        tp = tr(banks[b][0:32, 128 * x:128 * x + 128], Pc[i][:, x, :], ident[:, :], free, t,
                                inc=(x == 3))
                    pc_free[i] = tp
                    j = ntok["cj"] % 2
                    ntok["cj"] += 1
                    t = cp("dve", PcT[j], banks[b][0:32, :], tp, pct_free.get(j))
                    bank_free[b] = t
                    sPT[u] = (t, j)
                    return
                for x in range(qt + 1):
                    tp = tr(banks[b][:, 128 * x:128 * x + 128], Pb[i][:, 128 * x:128 * x + 128], ident[:, :], free, t,
                            inc=(x == qt))
                p_free[i] = tp
                j = (2 * hh + br - 1) % 2
                nk = 128 * (qt + 1)
                t = cp("act" if qt % 2 else "dve", PT[j][:, 0:qt + 1, 128 * qt:128 * qt + 128],
                       banks[b][:, 0:nk].rearrange("p (a b) -> p a b", b=128), tp, pt_free.get(j))
                bank_free[b] = t
                sPT.setdefault((hh, br), []).append(t)

            def value(u):
                hh, br, qt = units[u]
                hf, g, ft = hh % 2, hh // 4, hh // 2
                ob = 6 + ft % 2
                ps_ = slice(64 * hf, 64 * hf + 64)
                last = br == 0
                if last:
                    t, j = sPT[u]
                else:
                    if qt < 3:
                        return
                    t, j = sPT[(hh, br)], br - 1
                if last:
                    tp = pct_free[j] = mm(banks[ob][ps_, :], vc[:, 64 * g:64 * g + 64], PcT[j], False, True,
                                          t, skip_group_check=True, inc=True)
                else:
                    for x in range(4):
                        tp = mm(banks[ob][ps_, 128 * x:512], Vt[br - 1][:, x, 64 * g:64 * g + 64],
                                PT[j][:, x, 128 * x:512], br == 1 and x == 0, False, t, o_free[ob],
                                skip_group_check=True, inc=(x == 3))
                    pt_free[j] = tp
                if last and hf == 1:
                    i = ft % 2
                    t = cp("act", yo[i][:, :], banks[ob][:, :], tp, yo_free[i])
                    o_free[ob] = t
                    t_ya[ft] = halves(yaH[:, ft, :], yaL[:, ft, :], yo[i][:, :], t)
                    yo_free[i] = t_ya[ft]

            for u in range(U + 4):
                if u < U:
                    score(u)
                if 3 <= u < U + 3:
                    turn(u - 3)
                if u >= 4:
                    value(u - 4)
            bank_free[6], bank_free[7] = o_free[6], o_free[7]
            ph.close()
            return t_ya

        def gmlp(l, tx, ybH, ybL, meanwhile):
            with ExitStack() as sc:
                uu = sb(sc, "uu", [128, 4, S])
                vf = sb(sc, "vf", [128, 4, S])
                vn = sb(sc, "vn", [128, 4, S])
                wT = sb(sc, "wT", [128, 8, 128])
                bsb = sb(sc, "bsb", [128, 4, 128])
                stt_ = sb(sc, "bst", [128, 4, 16])
                t_w = P.dma("pool", "wT", wT[:, :, :], A["wsT"][l])
                t_bs = P.dma("pool", "bsb", bsb[:, :, :], A["bsb"][l])
                t_ln = [P.dma("pool", f"lnp{i}", scr[2 + i][:, :], A["lnp"][l][:, i, :]) for i in range(2)]
                t_w = tt(wT[:, :, :], wT[:, :, :], msk[:, :].unsqueeze(1).broadcast_to([128, 8, 128]), ALU.mult,
                         t_w, t_const, e="pool")
                t_u = [None] * 4
                t_v = [None] * 4
                def each(i, b, t):
                    f = 2 * m + i
                    d = uu[:, f, :] if f < 4 else vf[:, f - 4, :]
                    t = act(d, banks[b][:, :], ACT.Gelu_apprx_tanh, t)
                    bank_free[b] = t
                    if f < 4:
                        t_u[f] = t
                    else:
                        t_v[f - 4] = t

                for m in range(4):
                    groups(*slot("mix_w_in"), nHk(S), nLk(S), tx, S, each)
                t_n = [None] * 4
                for tt_ in range(4):
                    b, free = take()
                    for f in range(4):
                        t = tr(banks[b][:, f * 128:f * 128 + 128], vf[:, f, tt_ * 128:tt_ * 128 + 128], ident[:, :],
                               free, t_v[f], inc=(f == 3))
                    s = stt_[:, tt_, :]
                    t0 = t
                    t = P.op("dve", lambda g, s=s, b=b: g.bn_stats(s[:, 0:6], banks[b][:, :]), t)
                    t = P.op("dve", lambda g, s=s: g.bn_aggr(s[:, 6:8], s[:, 0:6]), t)
                    t = act(s[:, 8:9], s[:, 7:8], ACT.Sqrt, t, bias=epsc[:, 0:1])
                    t = P.op("dve", lambda g, s=s: g.reciprocal(s[:, 9:10], s[:, 8:9]), t)
                    t = ts(vn[:, tt_, :], banks[b][:, :], s[:, 6:7], s[:, 9:10], ALU.subtract, ALU.mult, t)
                    bank_free[b] = t
                    t = tt(vn[:, tt_, :], vn[:, tt_, :], scr[2][:, :], ALU.mult, t, t_ln)
                    t_n[tt_] = tt(vn[:, tt_, :], vn[:, tt_, :], scr[3][:, :], ALU.add, t, t_ln)
                meanwhile()
                t_y = [None] * 4
                for f in range(4):
                    b, free = take()
                    for hf in range(2):
                        for tt_ in range(4):
                            g = 2 * f + hf
                            t = mm(banks[b][64 * hf:64 * hf + 64, tt_ * 128:tt_ * 128 + 128],
                                   vn[:, tt_, 64 * g:64 * g + 64], wT[:, g, :], tt_ == 0, tt_ == 3, free, t_w, t_n[tt_],
                                   skip_group_check=True, inc=(hf == 1 and tt_ == 3))
                    v = vf[:, f, :].rearrange("p (a b) -> p a b", a=4)
                    t = tt(v, banks[b][:, :].rearrange("p (a b) -> p a b", a=4),
                           bsb[:, f, :].unsqueeze(1).broadcast_to([128, 4, 128]), ALU.add, t, t_bs)
                    bank_free[b] = t
                    t = tt(vf[:, f, :], vf[:, f, :], uu[:, f, :], ALU.mult, t, t_u[f])
                    t_y[f] = halves(ybH[:, f, :], ybL[:, f, :], vf[:, f, :], t)
                return t_y

        for l in range(2):
            run_ = ffn_block1(l, 0)
            if l == 0:
                for n in (0, 2, 4, 4):
                    next(run_)
                    for _ in range(n):
                        ada_step()
            drain(run_)
            mixer(l)
            if l == 0:
                drain(ffn_block1(l, 1))

        b2 = ExitStack()
        xc = sb(b2, "xc", [128, KT, C])
        t_xc = P.dma("pool", "xc", xc[:, :, :], A["ctxT"], P.everyone())
        tc = [t_xc] * 8
        ctiles = [xc[:, i, :] for i in range(8)]
        bc = ExitStack()
        con = Path(sb(bc, "nHc", [128, KT, C], F32R), None,
                   [sb(bc, f"scrc{i}", [128, C + 16]) for i in range(4)], sb(bc, "rsc", [128, 8]), 2)
        bp = ExitStack()
        hpc = sb(bp, "hpc", [128, KT, C + 16])

        def post(p, tiles, x, tx_, N, g, gt, t_gt, waits=(0, 0, 0)):
            Gp = der[:, p.gains(), 8:16]
            t_gp = tt(Gp, g, gt, ALU.mult, t_gt, P.last("dve"), P.last("act"), P.last("pool"))
            ts_ = [t for _, t in tiles]
            scr = p.scr
            if True:
                b, t_r = yield from rstd(p, [a for a, _ in tiles], ts_, N, D, waits)
                t_ = [scr[2 + i][:, 0:N] for i in range(2)]
                rd = [None, None]
                for i, (m, tm) in enumerate(tiles):
                    t1 = tt(t_[i % 2][:, :], m, banks[b][:, 0:N], ALU.mult, t_r, tm, rd[i % 2])
                    if i == 7:
                        bank_free[b] = t1
                    tx_[i] = stt(x[i], t_[i % 2][:, :], Gp[:, i:i + 1], x[i], ALU.mult, ALU.add, t1, t_gp, tx_[i])
                    rd[i % 2] = tx_[i]
                    if i % 2:
                        yield
                p.busy = rd

        def mlp2_in(p, l, x, tx_, N, q, waits=(0, 0, 0)):
            G, Sh, tg = scaled_gain(p, V("g_mlp_pre_2", l * 8), 2, l, 3, q)
            return (yield from normed(p, x, tx_, N, G, Sh, tg, waits=waits))

        def mlp2(p, l, x, tx_, N, q, tx):
            with ExitStack() as sc:
                ma = sb(sc, "ma", [128, KT, N])
                tm = [None] * 8

                def sink(first, o, b, t):
                    if first:
                        tm[o] = cp("dve", ma[:, o, :], banks[b][:, 0:N], t)
                    else:
                        tm[o] = tt(ma[:, o, :], ma[:, o, :], banks[b][:, 0:N], ALU.add, t, tm[o])
                    return tm[o]

                yield from ffn(p, NF2, "w_mlp_in_2", "w_mlp_out_2", tx, N, False, sink)
                gt, t_gt = mod(2, l, 5, q)
                yield from post(p, [(ma[:, o, :], tm[o]) for o in range(8)], x, tx_, N, V("g_mlp_post_2", l * 8), gt, t_gt)

        def pool_block(p, x, tx_, N, q, hp, gH, gL, s_):
            W_ = N + 16
            G, Sh, tg = scaled_gain(p, V("g_mix_pre_2"), 2, 0, 0, q)
            clear = P.everyone()
            P.op("dve", lambda g: g.memset(hp[:, :, 0:8], 0.0), clear)
            t_z = P.op("dve", lambda g: g.memset(hp[:, :, N + 8:N + 16], 0.0))
            tn = yield from normed(p, x, tx_, N, G, Sh, tg, keep=lambda i: hp[:, i, 8:N + 8], clear=clear)
            gt, t_gt = mod(2, 0, 2, q)
            rd = [clear, clear]
            t_y, t_pe, tm = [clear, clear], None, [None] * 8
            last = 0
            ends = lambda a: a.rearrange("p (a b) -> p a b", b=8)[:, ::N // 8 - 1, :]
            for f in range(8):
                g = f // 2
                src, t, lo, hi = hp[:, f, :], [tn[f], t_z], 0, W_
                for lev in range(g + 1):
                    a = 1 if lev == 0 else 2 ** (lev - 1)
                    b_ = 0 if lev == 0 else 2 ** (lev - 1)
                    lo, hi = lo + a, hi - b_
                    last = 1 - last
                    d = s_[last]
                    t = tt(d[:, lo:hi], src[:, lo - a:hi - a], src[:, lo + b_:hi + b_], ALU.add, t, rd[last],
                           P.last("pool"), e="pool")
                    rd[last] = t
                    src = d
                    if lev == 1:
                        yield
                yield
                y = p.scr[f % 2][:, 0:N]
                x_ = hp[:, f, 8:N + 8]
                t = stt(y, src[:, 8:N + 8], 2.0 ** -(g + 1), x_, ALU.mult, ALU.subtract, t, t_y[f % 2])
                ec = edge[:, g, :].rearrange("p (a b) -> p a b", b=8)
                t = tt(ends(y), ends(src[:, 8:N + 8]), ec, ALU.mult, t)
                t = rd[last] = tt(ends(y), ends(y), ends(x_), ALU.subtract, t)
                t_y[f % 2] = halves(gH[:, f % 2, :], gL[:, f % 2, :], y, t, [t_pe, clear])
                if f % 2 == 0:
                    continue
                yield
                res = groups(*slot("w_pool_2"), lambda i: gH[:, i, :], lambda i: gL[:, i, :], t_y, N)
                t_pe = res[-1][1]
                for i, (b, t) in enumerate(res):
                    o = f - 1 + i
                    tm[o] = act(hp[:, o, 8:N + 8], banks[b][:, 0:N], ACT.Copy, t, t_y, rd[last],
                                scale=vec[:, VEC["pool_scale_2"] + o:VEC["pool_scale_2"] + o + 1])
                    bank_free[b] = tm[o]
            p.busy = t_y
            yield
            yield from post(p, [(hp[:, f, 8:N + 8], tm[f]) for f in range(8)], x, tx_, N, V("g_mix_post_2"), gt, t_gt)

        def context():
            P.barrier()
            yield from pool_block(con, ctiles, tc, C, 1, hpc, con.nH[:, 0:2, :], con.nH[:, 2:4, :], con.scr[2:4])
            bp.close()
            con.nL = sb(bc, "nLc", [128, KT, C], F32R)
            return (yield from mlp2_in(con, 0, ctiles, tc, C, 1))

        def latents():
            fin = yield from normed(lat, htiles, th, S, V("final_g"), None, None, keep=lambda i: h[:, i, :])
            th[:] = fin
            with ExitStack() as sc:
                hp = sb(sc, "hp", [128, KT, S + 16], side="right")
                gH, gL = (sb(sc, n, [128, 2, S], F32R, side="right") for n in ("gH", "gL"))
                s_ = [sb(sc, f"s{i}", [128, S + 16], side="right") for i in range(2)]
                yield from pool_block(lat, htiles, th, S, 0, hp, gH, gL, s_)
            lat.nH = sb(nn, "nH", [128, KT, S], F32R, side="right")
            lat.nL = sb(nn, "nL", [128, KT, S], F32R, side="right")
            return (yield from mlp2_in(lat, 0, htiles, th, S, 0))

        _, tx = weave(ffn_block1(1, 1), context(), lambda n: 0 if n < 9 else 1 + (n % 3 == 0))
        nn.close()
        P.barrier()
        share[0] = True
        _, tx = weave(mlp2(con, 0, ctiles, tc, C, 1, tx), latents(), lambda n: 1 + (n % 3 == 1))
        T = S + C
        fr = {"vT": None, 0: None, 1: None, "n": 0}

        later = []

        def head_norm(b, t, N, dst, gain, roped, keep):
            nt = N // 128
            u = fr["n"] % 2
            fr["n"] += 1
            qx, ssq, sdg, srs = qx2[u], ssq2[u], sdg2[u], srs2[:, u, :]
            t0 = act(qx[:, 0:N], banks[b][:, 0:N], ACT.Copy, t, fr[u], scale=gain)
            t1 = act(ssq[:, 0:N], banks[b][:, 0:N], ACT.Square, t, fr[u])
            bank_free[b] = [t0, t1]

            def stage1():
                b1, free = take()
                for j in range(nt):
                    t = mm(banks[b1][:, j:j + 1], ssq[:, j * 128:j * 128 + 128], ones[:, 0:1], True, True, free, t1,
                           inc=(j == nt - 1))
                t = act(srs[:, 0:nt], banks[b1][:, 0:nt], ACT.Sqrt, t, bias=epsc[:, 0:1], scale=1.0 / 128)
                bank_free[b1] = t
                t = P.op("dve", lambda g: g.reciprocal(srs[:, 4:4 + nt], srs[:, 0:nt]), t)
                for j in range(nt):
                    td = ts(sdg[:, j * 128:j * 128 + 128], ident[:, :], srs[:, 4 + j:5 + j], None, ALU.mult, None, t)
                return td

            def stage2(td):
                b2_, free = take()
                t = mm(banks[b2_][:, 0:N], ones[:, :], sdg[:, 0:N], True, True, free, td, inc=True)
                if not roped:
                    t = tt(dst, qx[:, 0:N], banks[b2_][:, 0:N], ALU.mult, t, t0)
                    bank_free[b2_] = t
                else:
                    t = tt(qx[:, 0:N], qx[:, 0:N], banks[b2_][:, 0:N], ALU.mult, t, t0)
                    bank_free[b2_] = t
                    for q in range(4):
                        d0, s0 = 32 * q, 32 * (q ^ 1)
                        tr_ = cp("act", rot2[u][d0:d0 + 32, 0:N], qx[s0:s0 + 32, 0:N], t)
                    ta = tt(tmp2[u][:, 0:N], qx[:, 0:N], tab[:, 0, 0:N], ALU.mult, t, t_tab)
                    tb = tt(rot2[u][:, 0:N], rot2[u][:, 0:N], tab[:, 1, 0:N], ALU.mult, tr_, t_tab)
                    t = tt(dst, tmp2[u][:, 0:N], rot2[u][:, 0:N], ALU.add, ta, tb)
                fr[u] = t
                keep(t)

            later.append([stage1, stage2])

        def flush():
            tds = [a() for a, _ in later]
            for (_, z), td in zip(later, tds):
                z(td)
            later.clear()

        t_K, t_V = [], []

        def values(b, t, N, hd, base):
            tv = cp("act", vT[:, 0:N], banks[b][:, 0:N], t, fr["vT"])
            bank_free[b] = tv
            bt, free = take()
            for j in range(N // 128):
                t = tr(banks[bt][:, j * 128:j * 128 + 128], vT[:, j * 128:j * 128 + 128], ident[:, :], free, tv,
                       inc=(j == N // 128 - 1))
            fr["vT"] = t
            t = cp("dve", Vtk[:, base:base + N // 128, hd * 128:hd * 128 + 128],
                   banks[bt][:, 0:N].rearrange("p (a b) -> p a b", b=128), t)
            bank_free[bt] = t
            t_V.append(t)

        gq, gk = V("g_q_2", 0, 1), V("g_k_2", 0, 1)
        t_Q = [None] * 8

        def heads(p, tx, N, dst, gain, roped, keep):
            def each(i, b, t):
                if i == 0:
                    first.append((b, t))
                    return
                flush()
                for i_, (b_, t_) in enumerate((first[0], (b, t))):
                    head_norm(b_, t_, N, dst(i_), gain, roped, lambda t, i_=i_: keep(i_, t))
            first = []
            groups(*slot("w_qkv_2"), nHk(N, p), nLk(N, p), tx, N, each)

        KTt = Vtk = Q = tab = t_tab = tmp2 = rot2 = vT = qx2 = ssq2 = sdg2 = srs2 = None
        kvs = ExitStack()

        def work(scope, N, side):
            nonlocal vT, qx2, ssq2, sdg2, srs2
            vT = sb(scope, "vT", [128, N], side=side)
            qx2, ssq2, sdg2 = ([sb(scope, f"{n}{i}", [128, N], side=side) for i in range(2)]
                               for n in ("qx", "ssq", "sdg"))
            srs2 = sb(scope, "srs", [128, 2, 8], side=side)
            for k_ in ("vT", 0, 1):
                fr[k_] = None

        def context_keys():
            nonlocal KTt, Vtk
            P.barrier()
            KTt = sb(kvs, "KTt", [128, 2, T], side="right")
            Vtk = sb(kvs, "Vtk", [128, 6, 256], side="right")
            with ExitStack() as sc:
                con = Path(sb(sc, "nHk", [128, KT, C], F32R, side="right"), sb(sc, "nLk", [128, KT, C], F32R, side="right"),
                           [sb(sc, f"scrk{i}", [128, C], side="right") for i in range(4)],
                           sb(sc, "rsk", [128, 8], side="right"), 2)
                work(sc, C, "right")
                G, Sh, tg = scaled_gain(con, V("g_mix_pre_2", 8), 2, 1, 0, 1)
                tx = yield from normed(con, ctiles, tc, C, G, Sh, tg)
                heads(con, tx, C, lambda i: KTt[:, i, 0:C], gk, False, lambda i, t: t_K.append(t))
                yield
                groups(*slot("w_qkv_2"), nHk(C, con), nLk(C, con), tx, C, lambda i, b, t: values(b, t, C, i, 0))
                yield
                flush()

        share[0] = False
        nH, nL = lat.nH, lat.nL
        bc.close()
        P.barrier()

        def latents_on(tx):
            yield from mlp2(lat, 0, htiles, th, S, 0, tx)
            G, Sh, tg = scaled_gain(lat, V("g_mix_pre_2", 8), 2, 1, 0, 0)
            return (yield from normed(lat, htiles, th, S, G, Sh, tg))

        tx, _ = weave(latents_on(tx), context_keys(), lambda n: 0 if n < 32 else 1)

        with ExitStack() as ph:
            P.barrier()
            ps2 = ExitStack()
            Q = sb(ph, "Q", [128, 8, S])
            tab = sb(ps2, "tab2", [128, 2, S])
            tmp2 = [sb(ps2, f"tmp2{i}", [128, S]) for i in range(2)]
            rot2 = [sb(ps2, f"rot2{i}", [128, S]) for i in range(2)]
            work(ps2, S, "left")
            t_tab = P.dma("pool", "tab2", tab[:, :, :], A["rope2"])
            heads(lat, tx, S, lambda i: KTt[:, i, C:T], gk, True, lambda i, t: t_K.append(t))
            for m in range(4):
                heads(lat, tx, S, lambda i: Q[:, 2 * m + i, :], gq, True, lambda i, t, m=m: t_Q.__setitem__(2 * m + i, t))
            groups(*slot("w_qkv_2"), nHk(S), nLk(S), tx, S, lambda i, b, t: values(b, t, S, i, 2))
            flush()
            ps2.close()
            P.barrier()
            Pb = [sb(ph, f"Pb{i}", [128, T]) for i in range(3)]
            PT = sb(ph, "PTb", [128, 3, 3, S])
            st2 = sb(ph, "st2", [128, 4, 8])
            SC = 128 ** -0.5
            units = [(hh, qt) for hh in range(8) for qt in range(4)]
            sP, sT = {}, {}
            p_free, pt_free = {}, {}
            o_free = {6: bank_free[6], 7: bank_free[7]}
            t_o = [None] * 8
            yo_free = [None, None]

            def score2(u):
                hh, qt = units[u]
                kv = hh // 4
                i = u % 3
                m1, m2, mm_, s1, s2, rr = (st2[:, i, x:x + 1] for x in range(6))
                bk, tk = [], []
                for part, (c0, n) in enumerate(((0, 384), (384, 384))):
                    b, free = take()
                    t = mm(banks[b][:, 0:n], Q[:, hh, 128 * qt:128 * qt + 128], KTt[:, kv, c0:c0 + n], True, True,
                           free, t_K, t_Q[hh], inc=True)
                    bk.append(b)
                    tk.append(P.op("dve", lambda g, o=(m1, m2)[part], b=b, n=n: g.tensor_reduce(
                        o, banks[b][:, 0:n], AX, ALU.max), t, p_free.get(i)))
                t = tt(mm_, m1, m2, ALU.max, tk)
                t = ts(mm_, mm_, -SC, None, ALU.mult, None, t)
                ta = act(Pb[i][:, 0:384], banks[bk[0]][:, 0:384], ACT.Exp, t, bias=mm_, scale=SC, accum_out=s1)
                bank_free[bk[0]] = ta
                tb = act(Pb[i][:, 384:768], banks[bk[1]][:, 0:384], ACT.Exp, t, bias=mm_, scale=SC, accum_out=s2)
                bank_free[bk[1]] = tb
                t = tt(rr, s1, s2, ALU.add, ta, tb)
                t = P.op("dve", lambda g: g.reciprocal(rr, rr), t)
                t = ts(Pb[i][:, :], Pb[i][:, :], rr, None, ALU.mult, None, t, e="pool")
                sP[u] = t

            def turn2(u):
                i = u % 3
                hh, qt = units[u]
                t = []
                for part in range(2):
                    b, free = take()
                    for x in range(3):
                        c = 3 * part + x
                        tp = tr(banks[b][:, 128 * x:128 * x + 128], Pb[i][:, 128 * c:128 * c + 128], ident[:, :],
                                free, sP[u], inc=(x == 2))
                    e = "act" if part else "dve"
                    j = (2 * hh + part) % 3
                    tq = cp(e, PT[:, j, :, 128 * qt:128 * qt + 128],
                            banks[b][:, 0:384].rearrange("p (a b) -> p a b", b=128), tp, pt_free.get(j))
                    bank_free[b] = tq
                    t.append(tq)
                p_free[i] = tp
                sT.setdefault(units[u][0], []).extend(t)

            def value2(u):
                hh, qt = units[u]
                kv, ob = hh // 4, 6 + hh % 2
                if qt < 3:
                    return
                for x in range(6):
                    j = (2 * hh + x // 3) % 3
                    tp = mm(banks[ob][:, :], Vtk[:, x, 128 * kv:128 * kv + 128], PT[:, j, x % 3, :], x == 0, x == 5,
                            sT[hh], t_V, o_free[ob], inc=(x % 3 == 2))
                    pt_free[j] = tp
                i = hh % 2
                t = cp("act", scr[i][:, :], banks[ob][:, :], tp, yo_free[i])
                o_free[ob] = t
                t_o[hh] = halves(nH[:, hh, :], nL[:, hh, :], scr[i][:, :], t)
                yo_free[i] = t_o[hh]

            U = len(units)
            for u in range(U + 3):
                if u < U:
                    score2(u)
                if u >= 3:
                    value2(u - 3)
                if 2 <= u < U + 2:
                    turn2(u - 2)
            bank_free[6], bank_free[7] = o_free[6], o_free[7]
        kvs.close()
        gt, t_gt = mod(2, 1, 2)
        with ExitStack() as sc:
            P.barrier()
            ym = sb(sc, "ym1", [128, KT, S])
            tm = [None] * 8
            for m in range(4):
                def each(i, b, t):
                    tm[2 * m + i] = cp("act", ym[:, 2 * m + i, :], banks[b][:, :], t)
                    bank_free[b] = tm[2 * m + i]

                groups(*slot("w_o_2"), nHk(S), nLk(S), t_o, S, each)
            drain(post(lat, [(ym[:, f, :], tm[f]) for f in range(8)], htiles, th, S, V("g_mix_post_2", 8), gt, t_gt,
                       waits=ALONE[0:2] + (0,)))
        tx = drain(mlp2_in(lat, 1, htiles, th, S, 0, waits=AFTER_POST))
        drain(mlp2(lat, 1, htiles, th, S, 0, tx))
        b2.close()
        nn.close()
        t_end = [P.dma("sp", f"out{i}", out[:, i, :], h[:, i, :], th[i]) for i in range(8)]
        P.wait("sp", t_end)
        assert st["used"] == len(slots), (st, len(slots))

        block = ctx.enter_context(nc.Block())
        P.emit(block)


def tables():
    f = np.float32
    c = {}
    c["ident"] = np.eye(128, dtype=f)
    inv = (1.0 / (f(10000.0) ** (np.arange(0, 64, 2, dtype=f) / f(64)))).astype(f)
    p = np.arange(128)
    sign = np.where((p % 64) < 32, -1.0, 1.0).astype(f)[:, None]

    def rope(pos):
        ang = (pos.astype(f)[None, :] * inv[p % 32][:, None]).astype(f)
        return np.cos(ang).astype(f), (np.sin(ang).astype(f) * sign).astype(f)

    co, si = rope(np.arange(S))
    c["rope1"] = np.stack([co * f(0.125), si * f(0.125), co, si], 1).reshape(128, 4, S).astype(f)
    ce = np.arange(31) * 16 + 31
    cc, cs_ = rope(np.concatenate([ce, ce[-1:]]))
    c["crope"] = np.stack([cc, cs_], 1).astype(f)
    inv2 = np.power(f(10000.0), -np.arange(0, 64, 2, dtype=f) / f(64)).astype(f)
    t = np.arange(S)
    pos = np.where(p[:, None] < 64, (t // 64)[None, :], (t % 64)[None, :]).astype(f)
    ang = (pos * inv2[p % 32][:, None]).astype(f)
    c["rope2"] = np.stack([np.cos(ang).astype(f), np.sin(ang).astype(f) * sign], 1).astype(f)
    q, k = np.arange(128)[:, None], np.arange(128)[None, :]
    c["negm"] = np.where(k <= q, 0.0, -1e30).astype(f)
    c["msk"] = (k >= q).astype(f)
    n = np.arange(32)
    cn = np.full((128, 4, 32), -1e30, f)
    for qt in range(4):
        ok = (n[None, :] < 31) & (16 * n[None, :] + 31 <= np.arange(128)[:, None] + 128 * qt)
        cn[:, qt][ok] = 0.0
    c["cneg"] = cn.reshape(128, 128)
    row = np.ones((128, 4), f)
    row[:31, 0] = 0.0
    c["rowok"] = row
    t = np.arange(S)
    o = np.zeros((4, S), f)
    for g, w in enumerate((2, 4, 8, 16)):
        o[g] = f(1.0) / (np.clip(t + w - w // 2, 0, S) - np.clip(t - w // 2, 0, S)).astype(f)
    o = np.concatenate([o[:, 0:8], o[:, S - 8:S]], axis=1)
    c["edge"] = np.ascontiguousarray(np.broadcast_to(o[None], (128, 4, 16)))
    return c


_IN = {"ident": (128, 128), "rope1": (128, 4, S), "crope": (128, 2, 32), "rope2": (128, 2, S), "msk": (128, 128),
       "rowok": (128, 4), "edge": (128, 4, 16)}


def kernel(**inputs):
    import ml_dtypes as _ml
    import concourse.bacc as _bacc
    from concourse import mybir as _mybir
    from concourse.bass_utils import run_bass_kernel_spmd as _run

    I = {k: np.asarray(v) for k, v in inputs.items()}
    arrays = {}
    cst = tables()
    for n in _IN:
        arrays[n] = cst[n]
    for n in ("negm", "cneg"):
        arrays[n] = cst[n].astype(_ml.bfloat16)
    arrays["idb"] = np.eye(128).astype(_ml.bfloat16)

    def fm(a):
        r, n = a.shape
        return np.ascontiguousarray(a.T.reshape(n // 128, 128, r).transpose(1, 0, 2))

    arrays["xT"] = fm(I["x"][0])
    arrays["ctxT"] = fm(I["ctx_2"][0])
    parts = []
    for a, idx, r0, nk, c0, n in plan():
        w = I[a][idx]
        if a == "w_pool_2":
            w = w.reshape(1024, 256)
        b = w[r0:r0 + nk * 128, c0:c0 + n].reshape(nk, 128, n).transpose(1, 0, 2)
        parts.append(b.reshape(-1))
    arrays["wst"] = np.concatenate(parts)
    parts = []
    for b_, l, m, _, _ in ada_plan():
        w = I["ada_w" if b_ == 1 else "w_ada_2"][l][:, m * 1024:(m + 1) * 1024]
        parts.append(w.T.reshape(8, 128, 1024))
    arrays["ast"] = np.concatenate(parts)
    lay, nv = vec_layout()
    arrays["vec"] = np.ascontiguousarray(np.concatenate([I[n].reshape(-1) for n in lay]).reshape(nv, 128).T)
    for n, a in (("cb", I["c"]), ("cb2", I["c_2"]), ("cbc", I["c_ctx_2"])):
        arrays[n] = np.ascontiguousarray(np.broadcast_to(a.reshape(1, D), (128, D)))
    arrays["cw"] = np.ascontiguousarray(I["cmp_w1"].reshape(2, 2, 2, 16, 64, 128).transpose(0, 1, 2, 4, 3, 5).reshape(
        2, 2, 128, 2048))
    arrays["pe"] = np.ascontiguousarray(I["cmp_pe"].reshape(2, 2, 2, 16, 64).transpose(0, 2, 4, 1, 3).reshape(2, 128, 2, 16))
    w2 = I["cmp_w2"]
    arrays["w2"] = np.ascontiguousarray(np.concatenate([w2[:, 0], w2[:, 0], w2[:, 1]], axis=2))
    arrays["wsT"] = np.ascontiguousarray(I["gm_ws"].transpose(0, 3, 1, 2))
    bs = I["gm_bs"].reshape(2, 4, 2, 1, 128)
    arrays["bsb"] = np.ascontiguousarray(np.broadcast_to(bs, (2, 4, 2, 64, 128)).reshape(2, 4, 128, 128).transpose(0, 2, 1, 3))
    ln = np.stack([I["gm_ln_g"], I["gm_ln_b"]], 1)[:, None]
    arrays["lnp"] = np.ascontiguousarray(np.broadcast_to(ln, (2, 128, 2, 512)))

    nc = _bacc.Bacc("TRN2", target_bir_lowering=False, num_devices=1, dynamic_dma_scratch_size=1024)
    A = {}
    for n, a in arrays.items():
        A[n] = nc.dram_tensor(f"in_{n}", a.shape, _mybir.dt.from_np(a.dtype), kind="ExternalInput").ap()
    out = nc.dram_tensor("out_0", (128, 8, S), F32, kind="ExternalOutput").ap()
    build(nc, A, out)
    r = _run(nc, [{f"in_{n}": a for n, a in arrays.items()}], core_ids=[0])
    got = r.results[0]["out_0"]
    return np.ascontiguousarray(got.transpose(2, 1, 0).reshape(1, S, D))
```
